# Optimizing a Trainium2 kernel written in Bass

```python
import math
import jax, jax.numpy as jnp
from jax import lax
import numpy as np

D_MODEL = 1024
BATCH = 1
SEQ = 1024
DEPTH = 1
DEC_BATCH = 8
DEC_SEQ = 1
PAST_LEN = 8192
PAGE_SIZE = 128

GDN_HEAD_DIM = 128
GDN_WIDTH = D_MODEL // 2
GDN_HEADS = GDN_WIDTH // GDN_HEAD_DIM
GDN_CHUNK = 64
CONV_WIDTH = 4
S5_CH_PER_GROUP = 16
S5_WIDTH = D_MODEL - GDN_WIDTH
S5_GROUPS = S5_WIDTH // S5_CH_PER_GROUP
S5_STATE = 64
MIX_WIDTH = GDN_WIDTH + S5_WIDTH
QKV_WIDTH = 3 * GDN_WIDTH
IN_COLS = QKV_WIDTH + GDN_WIDTH + 2 * GDN_HEADS + S5_WIDTH
N_EXPERTS = 16
N_EXPERT_GROUPS = 4
EXPERTS_PER_GROUP = N_EXPERTS // N_EXPERT_GROUPS
TOP_K = 2
D_EXPERT = 256
NORM_EPS = 1e-6

kernel_name = 'hymba_gdn_s5_grouped_moe_step'

def rms_norm(x, g):
    xf = x.astype(jnp.float32)
    y = xf * lax.rsqrt(jnp.mean(xf * xf, axis=-1, keepdims=True) + NORM_EPS)
    return (y * g.astype(jnp.float32)).astype(x.dtype)

def l2_normalize(x):
    return x * lax.rsqrt(jnp.sum(x * x, axis=-1, keepdims=True) + NORM_EPS)

def causal_short_conv(x, buf, w):
    L = x.shape[1]
    xp = jnp.concatenate([buf.astype(x.dtype), x], axis=1)
    y = xp[:, 0:L] * w[0]
    for i in range(1, CONV_WIDTH):
        y = y + xp[:, i:i + L] * w[i]
    return jax.nn.silu(y), xp[:, -(CONV_WIDTH - 1):]

def gdn_chunked(q, k, v, g, beta, s0):
    Bn, L, H, DK = q.shape
    C = min(GDN_CHUNK, L)
    pad = (-L) % C
    if pad:
        pw = ((0, 0), (0, pad), (0, 0), (0, 0))
        q, k, v = jnp.pad(q, pw), jnp.pad(k, pw), jnp.pad(v, pw)
        g, beta = jnp.pad(g, pw[:3]), jnp.pad(beta, pw[:3])
    N = (L + pad) // C

    def blocks(t):
        return jnp.moveaxis(t.reshape((Bn, N, C) + t.shape[2:]), 3, 2)

    q, k, v, g, beta = blocks(q), blocks(k), blocks(v), blocks(g), blocks(beta)
    G = jnp.cumsum(g, axis=-1)
    pos = jnp.arange(C)
    incl = pos[:, None] >= pos[None, :]
    strict = pos[:, None] > pos[None, :]
    decay = jnp.exp(jnp.where(incl, G[..., :, None] - G[..., None, :], -jnp.inf))
    kk = jnp.einsum('bnhid,bnhjd->bnhij', k, k)
    lmat = jnp.where(strict, beta[..., :, None] * kk * decay, 0.0)
    eG = jnp.exp(G)
    rhs = jnp.concatenate([(beta * eG)[..., None] * k, beta[..., None] * v], axis=-1)
    sol = lax.linalg.triangular_solve(lmat + jnp.eye(C, dtype=lmat.dtype), rhs,
                                      left_side=True, lower=True, unit_diagonal=True)
    w_blk, u0_blk = sol[..., :DK], sol[..., DK:]
    attn = jnp.einsum('bnhid,bnhjd->bnhij', q, k) * decay
    qg = q * eG[..., None]
    kd = k * jnp.exp(G[..., -1:] - G)[..., None]
    g_last = eG[..., -1]

    def step(s, xs):
        w_c, u0_c, qg_c, attn_c, kd_c, gl_c = xs
        u = u0_c - jnp.einsum('bhcd,bhde->bhce', w_c, s)
        o = jnp.einsum('bhcd,bhde->bhce', qg_c, s) + jnp.einsum('bhij,bhje->bhie', attn_c, u)
        s = gl_c[..., None, None] * s + jnp.einsum('bhcd,bhce->bhde', kd_c, u)
        return s, o

    xs = (w_blk, u0_blk, qg, attn, kd, g_last)
    xs = tuple(jnp.moveaxis(t, 1, 0) for t in xs)
    s_final, o = lax.scan(step, s0, xs)
    o = jnp.moveaxis(jnp.moveaxis(o, 0, 1), 2, 3).reshape(Bn, N * C, H, -1)[:, :L]
    return o, s_final

def s5_scan(u, x0, lam_re, lam_im, log_dt, b_re, b_im, c_re, c_im, d):
    f32 = jnp.float32
    Bn, L, _ = u.shape
    uf = u.astype(f32).reshape(Bn, L, S5_GROUPS, S5_CH_PER_GROUP)
    lam = lax.complex(lam_re.astype(f32), lam_im.astype(f32))
    dt = jnp.exp(log_dt.astype(f32))[:, None]
    lam_bar = jnp.exp(lam * dt)
    b = lax.complex(b_re.astype(f32), b_im.astype(f32))
    b_bar = ((lam_bar - 1) / lam)[..., None] * b
    bu = jnp.einsum('blgc,gpc->blgp', uf.astype(jnp.complex64), b_bar)
    bu = bu.at[:, 0].add(lam_bar * x0)
    a = jnp.broadcast_to(lam_bar, bu.shape)

    def combine(e1, e2):
        a1, b1 = e1
        a2, b2 = e2
        return a2 * a1, a2 * b1 + b2

    _, xs = lax.associative_scan(combine, (a, bu), axis=1)
    c = lax.complex(c_re.astype(f32), c_im.astype(f32))
    y = jnp.real(jnp.einsum('blgp,gcp->blgc', xs, c))
    y = y + d.astype(f32).reshape(S5_GROUPS, S5_CH_PER_GROUP) * uf
    return y.reshape(Bn, L, S5_WIDTH), xs[:, -1]

def hybrid_mixer(h, conv_buf, s_gdn, x0_s5, w_in, conv_w, a_log, dt_bias, gdn_norm_g,
                 lam_re, lam_im, log_dt, b_re, b_im, c_re, c_im, s5_d, glu_w, glu_b,
                 s5_norm_g, w_out):
    f32 = jnp.float32
    Bn, L, _ = h.shape
    proj = h @ w_in
    cuts = [QKV_WIDTH, QKV_WIDTH + GDN_WIDTH, QKV_WIDTH + GDN_WIDTH + GDN_HEADS,
            QKV_WIDTH + GDN_WIDTH + 2 * GDN_HEADS]
    qkv, z, beta_raw, alpha_raw, u = jnp.split(proj, cuts, axis=-1)
    qkv, new_buf = causal_short_conv(qkv, conv_buf, conv_w)
    q, k, v = jnp.split(qkv.astype(f32), 3, axis=-1)
    hs = (Bn, L, GDN_HEADS, GDN_HEAD_DIM)
    q = l2_normalize(q.reshape(hs)) * (GDN_HEAD_DIM ** -0.5)
    k = l2_normalize(k.reshape(hs))
    v = v.reshape(hs)
    beta = jax.nn.sigmoid(beta_raw.astype(f32))
    g = -jnp.exp(a_log.astype(f32)) * jax.nn.softplus(alpha_raw.astype(f32) + dt_bias.astype(f32))
    o, s_new = gdn_chunked(q, k, v, g, beta, s_gdn.astype(f32))
    o = rms_norm(o, gdn_norm_g) * jax.nn.silu(z.astype(f32).reshape(hs))
    o_a = o.reshape(Bn, L, GDN_WIDTH).astype(h.dtype)
    y, x_new = s5_scan(u, x0_s5, lam_re, lam_im, log_dt, b_re, b_im, c_re, c_im, s5_d)
    y = jax.nn.gelu(y).astype(h.dtype)
    y = y * jax.nn.sigmoid(y @ glu_w + glu_b)
    o_b = rms_norm(y, s5_norm_g)
    out = jnp.concatenate([o_a, o_b], axis=-1) @ w_out
    return out, new_buf, s_new, x_new

def grouped_moe(h, w_router, b_router, w_gate, w_up, w_down):
    Bn, L, D = h.shape
    t = h.reshape(-1, D)
    T = t.shape[0]
    scores = jax.nn.sigmoid((t @ w_router).astype(jnp.float32))
    sel = scores + b_router.astype(jnp.float32)
    grp_top = lax.top_k(sel.reshape(T, N_EXPERT_GROUPS, EXPERTS_PER_GROUP), TOP_K)[0]
    best_group = jnp.argmax(jnp.sum(grp_top, axis=-1), axis=-1)
    in_group = (jnp.arange(N_EXPERTS) // EXPERTS_PER_GROUP)[None, :] == best_group[:, None]
    _, idx = lax.top_k(jnp.where(in_group, sel, -jnp.inf), TOP_K)
    wts = jnp.take_along_axis(scores, idx, axis=-1)
    wts = wts / jnp.sum(wts, axis=-1, keepdims=True)
    combine = jnp.sum(jax.nn.one_hot(idx, N_EXPERTS, dtype=jnp.float32) * wts[..., None], axis=1)
    hg = jnp.einsum('td,edf->tef', t, w_gate)
    hu = jnp.einsum('td,edf->tef', t, w_up)
    act = jax.nn.silu(hg) * hu * combine[..., None].astype(t.dtype)
    out = jnp.einsum('tef,efd->td', act, w_down)
    return out.reshape(Bn, L, D)

def trunk(x, c, st_conv, st_gdn, st_re, st_im, norm1_g, norm2_g, w_ada, b_ada, w_in, conv_w,
          a_log, dt_bias, gdn_norm_g, s5_lambda_re, s5_lambda_im, s5_log_dt, s5_b_re, s5_b_im,
          s5_c_re, s5_c_im, s5_d, s5_glu_w, s5_glu_b, s5_norm_g, w_out, w_router, b_router,
          w_gate, w_up, w_down, final_g):
    f32 = jnp.float32
    bufs, gdns, res, ims = [], [], [], []
    for l in range(DEPTH):
        mod = (jax.nn.silu(c) @ w_ada[l] + b_ada[l])[:, None, :]
        sh1, sc1, gt1, sh2, sc2, gt2 = jnp.split(mod, 6, axis=-1)
        hn = rms_norm(x, norm1_g[l]) * (1 + sc1) + sh1
        x0 = lax.complex(st_re[l].astype(f32), st_im[l].astype(f32))
        mix, nb, ns, nx = hybrid_mixer(
            hn, st_conv[l], st_gdn[l], x0, w_in[l], conv_w[l], a_log[l], dt_bias[l],
            gdn_norm_g[l], s5_lambda_re[l], s5_lambda_im[l], s5_log_dt[l], s5_b_re[l],
            s5_b_im[l], s5_c_re[l], s5_c_im[l], s5_d[l], s5_glu_w[l], s5_glu_b[l],
            s5_norm_g[l], w_out[l])
        x = x + gt1 * mix
        hn = rms_norm(x, norm2_g[l]) * (1 + sc2) + sh2
        x = x + gt2 * grouped_moe(hn, w_router, b_router, w_gate[l], w_up[l], w_down[l])
        bufs.append(nb)
        gdns.append(ns)
        res.append(jnp.real(nx))
        ims.append(jnp.imag(nx))
    y = rms_norm(x, final_g)
    return y, jnp.stack(bufs), jnp.stack(gdns), jnp.stack(res), jnp.stack(ims)

def setup_inputs(seed: int = 0) -> dict:
    key = jax.random.key(seed)
    ks = iter(jax.random.split(key, 48))
    f32 = jnp.float32

    def nrm(shape, scale):
        return scale * jax.random.normal(next(ks), shape, f32)

    def unif(shape, lo, hi):
        return jax.random.uniform(next(ks), shape, f32, lo, hi)

    x_prompt = nrm((BATCH, SEQ, D_MODEL), 1.0)
    x_sample = nrm((DEC_BATCH, DEC_SEQ, D_MODEL), 1.0)
    c_prompt = nrm((BATCH, D_MODEL), 1.0)
    c_sample = nrm((DEC_BATCH, D_MODEL), 1.0)
    state_conv = nrm((DEPTH, DEC_BATCH, CONV_WIDTH - 1, QKV_WIDTH), 1.0)
    state_gdn = nrm((DEPTH, DEC_BATCH, GDN_HEADS, GDN_HEAD_DIM, GDN_HEAD_DIM), 0.3)
    state_s5_re = nrm((DEPTH, DEC_BATCH, S5_GROUPS, S5_STATE), 0.1)
    state_s5_im = nrm((DEPTH, DEC_BATCH, S5_GROUPS, S5_STATE), 0.1)
    norm1_g = 1.0 + nrm((DEPTH, D_MODEL), 0.02)
    norm2_g = 1.0 + nrm((DEPTH, D_MODEL), 0.02)
    w_ada = nrm((DEPTH, D_MODEL, 6 * D_MODEL), 0.2 * D_MODEL ** -0.5)
    b_ada = nrm((DEPTH, 6 * D_MODEL), 0.02)
    w_in = nrm((DEPTH, D_MODEL, IN_COLS), D_MODEL ** -0.5)
    conv_w = nrm((DEPTH, CONV_WIDTH, QKV_WIDTH), CONV_WIDTH ** -0.5)
    a_log = jnp.log(unif((DEPTH, GDN_HEADS), 1.0, 16.0))
    dt = jnp.exp(unif((DEPTH, GDN_HEADS), math.log(1e-3), math.log(1e-1)))
    dt_bias = dt + jnp.log(-jnp.expm1(-dt))
    gdn_norm_g = 1.0 + nrm((DEPTH, GDN_HEAD_DIM), 0.02)
    n = jnp.arange(S5_STATE, dtype=f32)
    s5_lambda_re = -0.5 + nrm((DEPTH, S5_GROUPS, S5_STATE), 0.01)
    s5_lambda_im = math.pi * n + nrm((DEPTH, S5_GROUPS, S5_STATE), 0.01)
    s5_log_dt = unif((DEPTH, S5_GROUPS), math.log(1e-3), math.log(1e-1))
    b_scale = (2 * S5_CH_PER_GROUP) ** -0.5
    s5_b_re = nrm((DEPTH, S5_GROUPS, S5_STATE, S5_CH_PER_GROUP), b_scale)
    s5_b_im = nrm((DEPTH, S5_GROUPS, S5_STATE, S5_CH_PER_GROUP), b_scale)
    c_scale = (2 * S5_STATE) ** -0.5
    s5_c_re = nrm((DEPTH, S5_GROUPS, S5_CH_PER_GROUP, S5_STATE), c_scale)
    s5_c_im = nrm((DEPTH, S5_GROUPS, S5_CH_PER_GROUP, S5_STATE), c_scale)
    s5_d = nrm((DEPTH, S5_WIDTH), 1.0)
    s5_glu_w = nrm((DEPTH, S5_WIDTH, S5_WIDTH), S5_WIDTH ** -0.5)
    s5_glu_b = nrm((DEPTH, S5_WIDTH), 0.02)
    s5_norm_g = 1.0 + nrm((DEPTH, S5_WIDTH), 0.02)
    w_out = nrm((DEPTH, MIX_WIDTH, D_MODEL), MIX_WIDTH ** -0.5)
    w_router = nrm((D_MODEL, N_EXPERTS), D_MODEL ** -0.5)
    b_router = nrm((N_EXPERTS,), 0.01)
    w_gate = nrm((DEPTH, N_EXPERTS, D_MODEL, D_EXPERT), D_MODEL ** -0.5)
    w_up = nrm((DEPTH, N_EXPERTS, D_MODEL, D_EXPERT), D_MODEL ** -0.5)
    w_down = nrm((DEPTH, N_EXPERTS, D_EXPERT, D_MODEL), D_EXPERT ** -0.5)
    final_g = 1.0 + nrm((D_MODEL,), 0.02)
    return {
        'x_prompt': x_prompt, 'x_sample': x_sample, 'c_prompt': c_prompt, 'c_sample': c_sample,
        'state_conv': state_conv, 'state_gdn': state_gdn,
        'state_s5_re': state_s5_re, 'state_s5_im': state_s5_im,
        'norm1_g': norm1_g, 'norm2_g': norm2_g, 'w_ada': w_ada, 'b_ada': b_ada,
        'w_in': w_in, 'conv_w': conv_w, 'a_log': a_log, 'dt_bias': dt_bias,
        'gdn_norm_g': gdn_norm_g, 's5_lambda_re': s5_lambda_re, 's5_lambda_im': s5_lambda_im,
        's5_log_dt': s5_log_dt, 's5_b_re': s5_b_re, 's5_b_im': s5_b_im,
        's5_c_re': s5_c_re, 's5_c_im': s5_c_im, 's5_d': s5_d,
        's5_glu_w': s5_glu_w, 's5_glu_b': s5_glu_b, 's5_norm_g': s5_norm_g,
        'w_out': w_out, 'w_router': w_router, 'b_router': b_router,
        'w_gate': w_gate, 'w_up': w_up, 'w_down': w_down, 'final_g': final_g,
    }

def reference(x_prompt, x_sample, c_prompt, c_sample, state_conv, state_gdn, state_s5_re,
              state_s5_im, norm1_g, norm2_g, w_ada, b_ada, w_in, conv_w, a_log, dt_bias,
              gdn_norm_g, s5_lambda_re, s5_lambda_im, s5_log_dt, s5_b_re, s5_b_im, s5_c_re,
              s5_c_im, s5_d, s5_glu_w, s5_glu_b, s5_norm_g, w_out, w_router, b_router,
              w_gate, w_up, w_down, final_g):
    weights = (norm1_g, norm2_g, w_ada, b_ada, w_in, conv_w, a_log, dt_bias, gdn_norm_g,
               s5_lambda_re, s5_lambda_im, s5_log_dt, s5_b_re, s5_b_im, s5_c_re, s5_c_im,
               s5_d, s5_glu_w, s5_glu_b, s5_norm_g, w_out, w_router, b_router,
               w_gate, w_up, w_down, final_g)
    bp = x_prompt.shape[0]
    zero_conv = jnp.zeros((DEPTH, bp, CONV_WIDTH - 1, QKV_WIDTH), x_prompt.dtype)
    zero_gdn = jnp.zeros((DEPTH, bp, GDN_HEADS, GDN_HEAD_DIM, GDN_HEAD_DIM), jnp.float32)
    zero_s5 = jnp.zeros((DEPTH, bp, S5_GROUPS, S5_STATE), jnp.float32)
    y_prompt, conv_p, gdn_p, s5re_p, s5im_p = trunk(
        x_prompt, c_prompt, zero_conv, zero_gdn, zero_s5, zero_s5, *weights)
    y_sample, conv_s, gdn_s, s5re_s, s5im_s = trunk(
        x_sample, c_sample, state_conv, state_gdn, state_s5_re, state_s5_im, *weights)
    return (y_prompt, y_sample, conv_p, gdn_p, s5re_p, s5im_p, conv_s, gdn_s, s5re_s, s5im_s)


_drawn_inputs = setup_inputs


def setup_inputs(seed=0):
    import zlib

    import numpy as np

    out = dict(_drawn_inputs(seed))
    spreads = {}
    factors = {'norm2_g': 6.088,
     'gdn_norm_g': 8.0,
     's5_lambda_re': 3.785,
     's5_c_re': 8.0,
     's5_c_im': 8.0,
     's5_glu_b': 8.0,
     's5_norm_g': 8.0,
     'b_router': 4.26,
     'final_g': 2.849}
    for name, (base, spread) in spreads.items():
        noise = np.random.default_rng([zlib.crc32(name.encode()), seed]).standard_normal(out[name].shape)
        drawn = base * np.exp(spread * noise) if base else spread * noise
        out[name] = __import__('jax').numpy.asarray(drawn.astype(out[name].dtype))
    for name, factor in factors.items():
        out[name] = (out[name] * factor).astype(out[name].dtype)
    return out
```

```python
from contextlib import ExitStack

import concourse.bass as bass
from concourse import mybir

ALU = mybir.AluOpType
ACT = mybir.ActivationFunctionType
AX = mybir.AxisListType
F32 = mybir.dt.float32
I32 = mybir.dt.int32
U32 = mybir.dt.uint32

P = 128
D = 1024
KD = D // P
SEQ = 1024
NT = SEQ // P
DEC = 8
T = SEQ + DEC
HEADS = 4
GW = 512
QKV = 3 * GW
MQ = QKV // P
CW = 4
GROUPS = 32
CH = 16
ST = 64
LAGS = 8
NCH = SEQ // LAGS
EXPERTS = 16
FE = 256
EPS = 1e-6
SEG = T // 3
PI2 = 6.283185307179586


class Steps:

    def __init__(self, sem, at):
        self.sem, self.at, self.n = sem, at, 0

    def did(self, ins, name=None):
        ins.then_inc(self.sem, 1)
        self.n += 1
        if name is not None:
            self.at[name] = self.n

    def wait(self, eng, name):
        eng.wait_ge(self.sem, self.at.get(name, 1))

    def drain(self, eng):
        if self.n:
            eng.wait_ge(self.sem, self.n)


def emit(nc, A, O, marks, stages=99, dbg=None):
    ctx = ExitStack()

    def sem(name):
        return ctx.enter_context(nc.semaphore(name))

    def steps(name):
        return Steps(sem(name), marks.setdefault(name, {}))

    def dram(name, shape, dt=F32):
        return nc.dram_tensor(name, shape, dt, kind="Internal").ap()

    with ctx:
        sb = lambda name, shape, dt=F32: ctx.enter_context(nc.sbuf_tensor(name, shape, dt))
        ps = [ctx.enter_context(nc.psum_tensor(f"bank{i}", [P, 512], F32)) for i in range(8)]

        ident = sb("ident", [P, P])
        vecT = sb("vecT", [P, 117])
        modT = sb("modT", [P, 48, 9])
        hT = sb("hT", [P, KD, T])
        tail = sb("tail", [P, MQ, 3 + DEC])
        small = sb("small", [P, 64])
        cT = sb("cT", [P, KD, 9])
        B_ADA, N1G, N2G, CONVW, GNG, SNG = 0, 48, 56, 64, 112, 113

        front = ctx.enter_context(ExitStack())
        fsb = lambda name, shape, dt=F32: front.enter_context(nc.sbuf_tensor(name, shape, dt))

        loads1, x_land = sem("loads1"), sem("x_land")
        ada_land = [sem(f"ada_land{q}") for q in range(4)]
        pe, act, dve, pool = steps("s1_pe"), steps("s1_act"), steps("s1_dve"), steps("s1_pool")
        ada_in = fsb("ada_in", [P, 4, KD, 512])
        X = fsb("X", [P, 9, D])
        crow = fsb("crow", [9, D])
        vrow = fsb("vrow", [117, P])
        sq = fsb("sq", [P, D])
        A1 = fsb("A1", [P, KD, 9])
        w_ada = A["w_ada"][0].rearrange("(k p) n -> p k n", p=P)
        rows = [(A["b_ada"][0], 48), (A["norm1_g"][0], 8), (A["norm2_g"][0], 8),
                (A["conv_w"][0].rearrange("i n -> (i n)"), 48), (A["gdn_norm_g"][0], 1),
                (A["s5_norm_g"][0], 4)]
        with nc.Block() as block:
            @block.sync
            def _(sp):
                sp.dma_start(crow[0:1, :], A["c_prompt"]).then_inc(loads1, 16)
                sp.dma_start(crow[1:9, :], A["c_sample"]).then_inc(loads1, 16)
                at = 0
                for v, n in rows:
                    sp.dma_start(vrow[at:at + n, :], v.rearrange("(m p) -> m p", p=P)).then_inc(loads1, 16)
                    at += n
                for q in (0, 2):
                    sp.dma_start(ada_in[:, q], w_ada[:, :, q * 512:(q + 1) * 512]).then_inc(ada_land[q], 16)
                sp.dma_start(X[:, 0:NT, :], A["x_prompt"][0].rearrange("(i p) d -> p i d", p=P)).then_inc(x_land, 16)
                sp.dma_start(X[0:DEC, NT, :], A["x_sample"].rearrange("b o d -> (b o) d")).then_inc(x_land, 16)
                for q in (1, 3):
                    sp.dma_start(ada_in[:, q], w_ada[:, :, q * 512:(q + 1) * 512]).then_inc(ada_land[q], 16)

            @block.gpsimd
            def _(g):
                pool.did(g.memset(ident[:, :], 0.0))
                pool.drain(g)
                pool.did(g.affine_select(out=ident[:, :], in_=ident[:, :], compare_op=ALU.not_equal, fill=1.0,
                                         base=0, pattern=[[-1, P]], channel_multiplier=1), "ident")

            @block.scalar
            def _(a):
                a.wait_ge(loads1, 16 * 8)
                act.did(a.activation(crow[:, :], crow[:, :], ACT.Silu), "silu_c")
                a.wait_ge(x_land, 32)
                dve.wait(a, "clear_ss")
                for i in range(9):
                    n = P if i < NT else DEC
                    act.drain(a)
                    act.did(a.activation(sq[0:n, :], X[0:n, i, :], ACT.Square, accum_out=small[0:n, i:i + 1]), "ss")
                dve.wait(a, "ms")
                act.did(a.activation(small[:, 10:19], small[:, 10:19], ACT.Sqrt), "rms")
                dve.wait(a, "A1_0")
                for i in range(NT):
                    pe.wait(a, f"xT0_{i}")
                    for k in range(4):
                        act.did(a.activation(hT[:, k, i * P:(i + 1) * P], ps[i % 3][:, k * P:(k + 1) * P],
                                             ACT.Identity, scale=A1[:, k, 0:1], bias=modT[:, k, 0:1]), f"hT{i}")

            @block.tensor
            def _(t):
                pool.wait(t, "ident")
                t.wait_ge(loads1, 16 * 8)
                act.wait(t, "silu_c")
                for k in range(KD):
                    mm = t.transpose(ps[7][:, k * 9:k * 9 + 9], crow[:, k * P:(k + 1) * P], ident[0:9, 0:9])
                mm = t.transpose(ps[7][:, 128:128 + 117], vrow[:, :], ident[0:117, 0:117])
                pe.did(mm, "vec")
                dve.wait(t, "cT")
                def ada(q):
                    t.wait_ge(ada_land[q], 16)
                    for m in range(4):
                        for k in range(KD):
                            mm = t.matmul(ps[6 + q // 2][:, 256 + (q % 2) * 36 + m * 9:256 + (q % 2) * 36 + m * 9 + 9],
                                          ada_in[:, q, k, m * P:(m + 1) * P], cT[:, k, :],
                                          start=(k == 0), stop=(k == KD - 1))
                    pe.did(mm, f"ada{q}")

                def x_transpose(half_, i):
                    n, b = P if i < NT else DEC, i % 3 + 3 * half_
                    dve.wait(t, f"xs{i}")
                    if i >= 3:
                        (dve if half_ else act).wait(t, f"hT{i - 3}")
                    for k in range(4):
                        mm = t.transpose(ps[b][:, k * P:k * P + n], X[0:n, i, (4 * half_ + k) * P:(4 * half_ + k + 1) * P], ident[0:n, 0:n])
                    pe.did(mm, f"xT{half_}_{i}")

                dve.wait(t, "vecT")
                ada(0)
                ada(2)
                for i in range(9):
                    x_transpose(0, i)
                dve.wait(t, "A1_0")
                ada(1)
                ada(3)
                for i in range(9):
                    x_transpose(1, i)

            @block.vector
            def _(v):
                dve.did(v.memset(small[:, :], 1.0), "clear_ss")
                pe.wait(v, "vec")
                dve.did(v.tensor_copy(cT[:, :, :].rearrange("p k n -> p (k n)"), ps[7][:, 0:72]), "cT")
                dve.did(v.tensor_copy(vecT[:, :], ps[7][:, 128:128 + 117]), "vecT")
                act.wait(v, "ss")
                dve.did(v.tensor_scalar(small[:, 10:19], small[:, 0:9], 1.0 / D, EPS, ALU.mult, ALU.add), "ms")
                act.wait(v, "rms")
                dve.did(v.reciprocal(small[:, 20:29], small[:, 10:19]))
                dve.drain(v)

                for i in range(9):
                    n = P if i < NT else DEC
                    dve.did(v.tensor_scalar(X[0:n, i, :], X[0:n, i, :], small[0:n, 20 + i:21 + i], None, ALU.mult), f"xs{i}")
                for half_ in range(2):
                    ks = slice(4 * half_, 4 * half_ + 4)
                    pe.wait(v, f"ada{2 + half_}")
                    for n in range(2):
                        dve.did(v.tensor_tensor(modT[:, 8 * n + 4 * half_:8 * n + 4 * half_ + 4, :],
                                                ps[6 + n][:, 256 + 36 * half_:292 + 36 * half_].rearrange("p (m n) -> p m n", m=4),
                                                vecT[:, B_ADA + 8 * n + 4 * half_:B_ADA + 8 * n + 4 * half_ + 4].unsqueeze(2).to_broadcast([P, 4, 9]), ALU.add))
                    dve.drain(v)
                    dve.did(v.tensor_scalar(A1[:, ks, :], modT[:, 8 + 4 * half_:12 + 4 * half_, :], 1.0, None, ALU.add))
                    dve.drain(v)
                    dve.did(v.tensor_tensor(A1[:, ks, :], A1[:, ks, :],
                                            vecT[:, N1G + 4 * half_:N1G + 4 * half_ + 4].unsqueeze(2).to_broadcast([P, 4, 9]), ALU.mult), f"A1_{half_}")
                    dve.drain(v)
                    for i in range(9):
                        if i < NT and half_ == 0:
                            continue
                        pe.wait(v, f"xT{half_}_{i}")
                        if i < NT:
                            for k in range(4, KD):
                                dve.did(v.tensor_scalar(hT[:, k, i * P:(i + 1) * P], ps[i % 3 + 3][:, (k - 4) * P:(k - 3) * P],
                                                        A1[:, k, 0:1], modT[:, k, 0:1], ALU.mult, ALU.add), f"hT{i}")
                        else:
                            src = ps[i % 3 + 3 * half_][:, :].rearrange("p (k n) -> p k n", k=4)[:, :, 0:DEC]
                            dve.did(v.tensor_tensor(hT[:, ks, SEQ:T], src, A1[:, ks, 1:9], ALU.mult))
                            dve.drain(v)
                            dve.did(v.tensor_tensor(hT[:, ks, SEQ:T], hT[:, ks, SEQ:T], modT[:, ks, 1:9], ALU.add))
        front.close()
        if stages == 1:
            return finish_debug(nc, sem, dbg, locals())

        mid = ctx.enter_context(ExitStack())
        msb = lambda name, shape, dt=F32: mid.enter_context(nc.sbuf_tensor(name, shape, dt))
        V = msb("V", [P, GROUPS, LAGS, CH])
        Vd = msb("Vd", [DEC, GW])
        mid2 = ctx.enter_context(ExitStack())
        msb = lambda name, shape, dt=F32: mid2.enter_context(nc.sbuf_tensor(name, shape, dt))
        Z = msb("Z", [P, 9, GW])
        gates = msb("gates", [P, 9, 8])
        Og = msb("Og", [P, 9, GW])
        qkvT = msb("qkvT", [P, MQ, T])
        s2 = ctx.enter_context(ExitStack())
        w_ring = s2.enter_context(nc.sbuf_tensor("w_ring", [P, 2, KD, 512], F32))
        w_gates = s2.enter_context(nc.sbuf_tensor("w_gates", [P, KD, 8], F32))
        pre = s2.enter_context(nc.sbuf_tensor("pre", [P, 2, 3 + T], F32))
        convd = s2.enter_context(nc.sbuf_tensor("convd", [P, MQ, 3, DEC], F32))
        crows = s2.enter_context(nc.sbuf_tensor("crows", [3 * DEC, QKV], F32))
        newrows = crows[0:11, :]
        w_in_v = A["w_in"][0].rearrange("(k p) n -> p k n", p=P)
        w_cols = [0, 512, 1024, QKV, QKV + GW + 8]
        w_land = [sem("w_in_a"), sem("w_in_b")]
        gate_land, conv_land, conv_out = sem("gate_land"), sem("conv_land"), sem("conv_out")
        pe, act, dve, pool = steps("s2_pe"), steps("s2_act"), steps("s2_dve"), steps("s2_pool")
        with nc.Block() as block:
            @block.sync
            def _(sp):
                with nc.allow_non_contiguous_dma(reason="eight gate columns"):
                    sp.dma_start(w_gates[:, :, :], w_in_v[:, :, QKV + GW:QKV + GW + 8]).then_inc(gate_land, 16)
                sp.dma_start(crows[:, :], A["state_conv"][0].rearrange("b i n -> (b i) n")).then_inc(conv_land, 16)
                for q in range(5):
                    if q >= 2:
                        pe.wait(sp, f"chunk{q - 2}")
                    sp.dma_start(w_ring[:, q % 2], w_in_v[:, :, w_cols[q]:w_cols[q] + 512]).then_inc(w_land[q % 2], 16)
                dve.wait(sp, "newrows")
                sp.dma_start(O["conv_p"][0, 0], newrows[0:3, :]).then_inc(conv_out, 16)
                sp.dma_start(O["conv_s"][0, :, 2, :], newrows[3:11, :]).then_inc(conv_out, 16)
                sp.dma_start(O["conv_s"][0, :, 0:2, :], A["state_conv"][0, :, 1:3, :]).then_inc(conv_out, 16)
                sp.wait_ge(conv_out, 48)

            @block.tensor
            def _(t):
                t.wait_ge(conv_land, 16)
                for m in range(MQ):
                    mm = t.transpose(ps[7][:, m * 24:m * 24 + 24], crows[:, m * P:(m + 1) * P], ident[0:24, 0:24])
                pe.did(mm, "conv_state")
                for m in range(MQ):
                    q = m // 4
                    if m % 4 == 0:
                        t.wait_ge(w_land[q % 2], 16 * (q // 2 + 1))
                    if m >= 2:
                        act.wait(t, f"pre{m - 2}")
                    for s in range(3):
                        for k in range(KD):
                            mm = t.matmul(ps[3 * (m % 2) + s][:, 0:SEG], w_ring[:, q % 2, k, (m % 4) * P:(m % 4 + 1) * P],
                                          hT[:, k, s * SEG:(s + 1) * SEG], start=(k == 0), stop=(k == KD - 1))
                    pe.did(mm, f"qkv{m}")
                    if m % 4 == 3:
                        pe.at[f"chunk{q}"] = pe.n
                t.wait_ge(gate_land, 16)
                for i in range(9):
                    n = P if i < NT else DEC
                    for k in range(KD):
                        mm = t.matmul(ps[6][0:n, i * 8:i * 8 + 8], hT[:, k, i * P:i * P + n], w_gates[:, k, :],
                                      start=(k == 0), stop=(k == KD - 1))
                pe.did(mm, "gates")
                act.wait(t, f"pre{MQ - 1}")
                dve.wait(t, "conv_state")
                for step in range(2):
                    q = 3 + step
                    t.wait_ge(w_land[q % 2], 16 * (q // 2 + 1))
                    for i in range(9):
                        n = P if i < NT else DEC
                        b = 9 * step + i
                        if b >= 4:
                            act.wait(t, f"zu{b - 4}")
                        for k in range(KD):
                            if i == NT:
                                tok = hT[:, k, SEQ:T]
                            elif step == 0:
                                tok = hT[:, k, i * P:(i + 1) * P]
                            else:
                                tok = hT[:, k, i:SEQ:LAGS]
                            mm = t.matmul(ps[b % 4][0:n, :], tok, w_ring[:, q % 2, k, :],
                                          start=(k == 0), stop=(k == KD - 1))
                        pe.did(mm, f"zu{b}")
                dve.wait(t, "gates")
                for m in range(MQ):
                    dst = ps[4 + m // 4]
                    mm = t.transpose(dst[0:11, (m % 4) * P:(m % 4 + 1) * P], tail[:, m, :], ident[:, :])
                pe.did(mm, "newrows")

            @block.scalar
            def _(a):
                for m in range(MQ):
                    pe.wait(a, f"qkv{m}")
                    if m >= 2:
                        dve.wait(a, f"conv{m - 2}")
                    else:
                        pool.wait(a, "pad")
                    for s in range(3):
                        act.did(a.activation(pre[:, m % 2, 3 + s * SEG:3 + (s + 1) * SEG],
                                             ps[3 * (m % 2) + s][:, 0:SEG], ACT.Copy), f"pre{m}")
                    if m >= 1:
                        dve.wait(a, f"conv{m - 1}")
                        act.did(a.activation(qkvT[:, m - 1, :], qkvT[:, m - 1, :], ACT.Silu))
                dve.wait(a, f"conv{MQ - 1}")
                act.did(a.activation(qkvT[:, MQ - 1, :], qkvT[:, MQ - 1, :], ACT.Silu))
                for b in range(18):
                    i, n = b % 9, P if b % 9 < NT else DEC
                    pe.wait(a, f"zu{b}")
                    if b < 9:
                        act.did(a.activation(Z[0:n, i, :], ps[b % 4][0:n, :], ACT.Silu), f"zu{b}")
                    elif i < NT:
                        act.did(a.activation(V[:, :, i, :], ps[b % 4][:, :].rearrange("p (g c) -> p g c", c=CH), ACT.Copy), f"zu{b}")
                    else:
                        act.did(a.activation(Vd[:, :], ps[b % 4][0:n, :], ACT.Copy), f"zu{b}")

            @block.gpsimd
            def _(g):
                pool.did(g.memset(Z[:, NT, :], 0.0))
                pool.did(g.memset(gates[:, NT, :], 0.0))
                pool.did(g.memset(pre[:, :, 0:3], 0.0), "pad")

            @block.vector
            def _(v):
                pe.wait(v, "conv_state")
                dve.did(v.tensor_copy(convd[:, :, :, :].rearrange("p m i b -> p m b i"),
                                      ps[7][:, 0:24 * MQ].rearrange("p (m b i) -> p m b i", m=MQ, i=3)), "conv_state")
                dve.drain(v)
                for m in range(MQ):
                    act.wait(v, f"pre{m}")
                    w = [vecT[:, CONVW + i * MQ + m:CONVW + i * MQ + m + 1] for i in range(CW)]
                    y, yd = qkvT[:, m, 0:SEQ], qkvT[:, m, SEQ:T]
                    dve.did(v.tensor_copy(tail[:, m, :], pre[:, m % 2, SEQ:3 + T]))
                    dve.did(v.tensor_scalar(yd, convd[:, m, 0, :], w[0], None, ALU.mult))
                    dve.did(v.tensor_scalar(y, pre[:, m % 2, 0:SEQ], w[0], None, ALU.mult))
                    for i in range(1, CW):
                        dve.drain(v)
                        old = convd[:, m, i, :] if i < 3 else pre[:, m % 2, 3 + SEQ:3 + T]
                        dve.did(v.scalar_tensor_tensor(out=yd, in0=old, scalar=w[i], in1=yd, op0=ALU.mult, op1=ALU.add))
                        dve.did(v.scalar_tensor_tensor(out=y, in0=pre[:, m % 2, i:i + SEQ], scalar=w[i], in1=y,
                                                       op0=ALU.mult, op1=ALU.add), f"conv{m}")
                pe.wait(v, "gates")
                pool.wait(v, "pad")
                dve.did(v.tensor_copy(gates[:, 0:8, :].rearrange("p i n -> p (i n)"), ps[6][:, 0:64]))
                dve.did(v.tensor_copy(gates[0:DEC, 8, :], ps[6][0:DEC, 64:72]), "gates")
                pe.wait(v, "newrows")
                for b in range(3):
                    dve.did(v.tensor_copy(newrows[:, b * 512:(b + 1) * 512], ps[4 + b][0:11, :]), "newrows")
        s2.close()
        if stages == 2:
            return finish_debug(nc, sem, dbg, locals())


        s3 = ctx.enter_context(ExitStack())
        t3 = lambda name, shape: s3.enter_context(nc.sbuf_tensor(name, shape, F32))
        upper = t3("upper", [P, P])
        neg_lo = t3("neg_lo", [P, P])
        big_up = t3("big_up", [P, P])
        bd = t3("bd", [P, 4, P])
        ones = t3("ones", [P, 1])
        beta = t3("beta", [P, 9, HEADS])
        gg = t3("gg", [P, 9, HEADS])
        sp_t = t3("sp_t", [P, 2, 9, HEADS])
        hp = t3("hp", [P, 2, HEADS])
        Gc = t3("Gc", [P, NT, HEADS])
        nbe = t3("nbe", [P, NT, HEADS])
        rn = t3("rn", [P, 9, 2 * HEADS])
        sqT = t3("sqT", [P, T])
        half = [P, 2, 2, P]
        kn = t3("kn", half)
        R = t3("R", half)
        D0, D1 = t3("D0", half), t3("D1", half)
        L, N = t3("L", half), t3("N", half)
        NL1 = t3("NL1", [P, 2, 2, 2, P])
        NL2, NL4 = t3("NL2", [P, 2, 2, 2, P]), t3("NL4", [P, 2, 2, 2, P])
        L8, Xi, Zi, Lk = t3("L8", half), t3("Xi", half), t3("Zi", half), t3("Lk", half)
        egb = t3("egb", half)
        Y, vb, kTn, at, qg, kd = (hT[:, :, :].rearrange("p k t -> p (k t)")[:, n * 1024:(n + 1) * 1024]
                                  .rearrange("p (b l h n) -> p b l h n", b=2, l=2, h=2) for n in range(6))
        egl = t3("egl", [P, 2, HEADS])
        r, u = t3("r", half), t3("u", half)
        S = t3("S", [P, HEADS, P])
        BIG = 1e30
        zland = sem("zland")
        SLOTS = 2 * T // P + EXPERTS
        xs_d = dram("xs_d", ((SLOTS + 4) * P, D))
        ys_d = xs_d
        hp_land, s_out = sem("hp_land"), sem("gdn_out")
        pe, act, dve, pool = steps("s3_pe"), steps("s3_act"), steps("s3_dve"), steps("s3_pool")

        def bc(ap, shape, axis=2):
            return ap.unsqueeze(axis).to_broadcast(shape)

        def chunk(m, c):
            return qkvT[:, m, c * P:(c + 1) * P]

        with nc.Block() as block:
            @block.sync
            def _(sp):
                sp.dma_start(hp[:, 0, :], A["dt_bias"][0:1, :].to_broadcast([P, HEADS])).then_inc(hp_land, 16)
                sp.dma_start(hp[:, 1, :], A["a_log"][0:1, :].to_broadcast([P, HEADS])).then_inc(hp_land, 16)
                pool.wait(sp, "masks")
                for n in range(SLOTS // 2 + 2):
                    sp.dma_start(xs_d[n * 2 * P:(n + 1) * 2 * P, :].rearrange("(a p) d -> p a d", p=P),
                                 Og[:, 4:8, :].rearrange("p i n -> p (i n)").rearrange("p (a d) -> p a d", a=2)).then_inc(zland, 16)
                dve.wait(sp, "S7_1")
                sp.dma_start(O["gdn_p"][0, 0].rearrange("h k v -> k h v"), S[:, :, :]).then_inc(s_out, 16)
                sp.wait_ge(s_out, 16)

            @block.gpsimd
            def _(g):
                pool.did(g.memset(ones[:, :], 1.0))
                pool.did(g.memset(Og[:, 4:9, :], 0.0))
                pool.did(g.memset(upper[:, :], 1.0))
                pool.did(g.memset(neg_lo[:, :], 0.0))
                pool.did(g.memset(big_up[:, :], BIG))
                pool.did(g.memset(bd[:, :, :], 1.0))
                pool.did(g.memset(S[:, :, :], 0.0))
                pool.drain(g)
                pool.did(g.affine_select(out=upper[:, :], in_=upper[:, :], compare_op=ALU.is_ge, fill=0.0,
                                         base=0, pattern=[[1, P]], channel_multiplier=-1))
                pool.did(g.affine_select(out=neg_lo[:, :], in_=neg_lo[:, :], compare_op=ALU.is_ge, fill=-BIG,
                                         base=0, pattern=[[1, P]], channel_multiplier=-1))
                pool.did(g.affine_select(out=big_up[:, :], in_=big_up[:, :], compare_op=ALU.is_ge, fill=0.0,
                                         base=0, pattern=[[1, P]], channel_multiplier=-1))
                for j, b in enumerate((16, 32, 64)):
                    blocks = bd[:, j, :].rearrange("p (n b) -> p n b", b=b)
                    pool.drain(g)
                    pool.did(g.affine_select(out=blocks, in_=blocks, compare_op=ALU.is_ge, fill=0.0,
                                             base=0, pattern=[[-b, P // b], [0, b]], channel_multiplier=1))
                    pool.drain(g)
                    pool.did(g.affine_select(out=blocks, in_=blocks, compare_op=ALU.is_ge, fill=0.0,
                                             base=b - 1, pattern=[[b, P // b], [0, b]], channel_multiplier=-1))
                for j in (3, 2, 1):
                    pool.drain(g)
                    pool.did(g.tensor_tensor(bd[:, j, :], bd[:, j, :], bd[:, j - 1, :], ALU.subtract))
                pool.drain(g)
                pool.did(g.memset(sp_t[:, 1, :, :], 0.0), "masks")
                for c in range(NT):
                    b = c % 2
                    for l in range(2):
                        act.wait(g, f"egb{c}_{l}")
                        if c >= 2:
                            pe.wait(g, f"o{c - 2}_{l}")
                        for hh in range(2):
                            pool.did(g.tensor_tensor(qg[:, b, l, hh, :], chunk(2 * l + hh, c), egb[:, l, hh, :], ALU.mult))
                        pool.did(g.tensor_copy(egl[:, b, 2 * l:2 * l + 2], egb[:, l, :, P - 1]), f"qg{c}_{l}")
                        dve.wait(g, f"kn{c}_{l}")
                        act.wait(g, f"D{c}_{l}")
                        pool.did(g.tensor_tensor(kd[:, b, l], kn[:, l], D1[:, l, :, P - 1:P].to_broadcast([P, 2, P]), ALU.mult), f"kd{c}_{l}")
                    for l in range(2):
                        dve.wait(g, f"L{c}_{l}")
                        pool.did(g.tensor_tensor(NL1[:, l, 1], L[:, l], bc(bd[:, 0, :], [P, 2, P], 1), ALU.mult), f"Ld{c}_{l}")
                    for k in range(1, 4):
                        for l in range(2):
                            if k > 1:
                                pe.wait(g, f"Z{k - 1}_{c}_{l}")
                            elif c > 0:
                                pe.wait(g, f"Z3_{c - 1}_{l}")
                            pool.did(g.tensor_tensor(Lk[:, l], L[:, l], bc(bd[:, k, :], [P, 2, P], 1), ALU.mult), f"Lk{k}_{c}_{l}")

            @block.tensor
            def _(t):
                pool.wait(t, "masks")
                for m in range(2 * HEADS):
                    act.wait(t, f"sq{m}")
                    for i in range(9):
                        n = P if i < NT else DEC
                        mm = t.matmul(ps[0][0:n, i * 8 + m:i * 8 + m + 1], sqT[:, i * P:i * P + n], ones[:, :], start=True, stop=True)
                    pe.did(mm, f"ss{m}")
                dve.wait(t, "gg")
                pe.did(t.matmul(ps[1][:, 0:NT * HEADS], upper[:, :], gg[:, 0:NT, :], start=True, stop=True), "G")
                dve.wait(t, "rn")
                dve.wait(t, "Gc")

                def scan_step(c, l, step):
                    b = c % 2
                    bank = ps[6 + l]
                    for hh in range(2):
                        h = 2 * l + hh
                        lo, hi = bank[:, hh * P:(hh + 1) * P], bank[:, 256 + hh * P:256 + (hh + 1) * P]
                        if step == 0:
                            if hh == 0:
                                if c > 0:
                                    dve.wait(t, f"S{c - 1}_{l}")
                            mm = t.matmul(lo, kTn[:, b, l, hh, :], S[:, h, :], start=True, stop=True)
                        elif step == 1:
                            if hh == 0:
                                dve.wait(t, f"r{c}_{l}")
                            mm = t.matmul(hi, Y[:, b, l, hh, :], r[:, l, hh, :], start=True, stop=True)
                        else:
                            if hh == 0:
                                act.wait(t, f"u{c}_{l}")
                                pool.wait(t, f"kd{c}_{l}")
                            t.matmul(lo, kd[:, b, l, hh, :], u[:, l, hh, :], start=True, stop=True)
                            t.matmul(hi, qg[:, b, l, hh, :], S[:, h, :], start=True, stop=False)
                            mm = t.matmul(hi, at[:, b, l, hh, :], u[:, l, hh, :], start=False, stop=True)
                    pe.did(mm, f"{('ks', 'u', 'o')[step]}{c}_{l}")

                def scan(c, step):
                    if c >= 0:
                        for l in range(2):
                            scan_step(c, l, step)

                for c in range(NT):
                    b = c % 2
                    for l in range(2):
                        if c > 0:
                            dve.wait(t, f"Y3_{c - 1}_{l}")
                        for hh in range(2):
                            t.transpose(ps[3 * l][:, hh * P:(hh + 1) * P], chunk(HEADS + 2 * l + hh, c), ident[:, :])
                            mm = t.transpose(ps[3 * l][:, 256 + hh * P:256 + (hh + 1) * P], chunk(2 * HEADS + 2 * l + hh, c), ident[:, :])
                        pe.did(mm, f"kv{c}_{l}")
                        for hh in range(2):
                            h = 2 * l + hh
                            mm = t.matmul(ps[3 * l + 1][:, hh * P:(hh + 1) * P], gg[:, c, h:h + 1].to_broadcast([P, P]), upper[:, :], start=True, stop=True)
                        pe.did(mm, f"Gb{c}_{l}")
                    for l in range(2):
                        dve.wait(t, f"kn{c}_{l}")
                        for hh in range(2):
                            mm = t.transpose(ps[3 * l + 2][:, hh * P:(hh + 1) * P], kn[:, l, hh, :], ident[:, :])
                        pe.did(mm, f"kTn{c}_{l}")
                    scan(c - 1, 0)
                    for l in range(2):
                        act.wait(t, f"kTn{c}_{l}")
                        dve.wait(t, f"vb{c}_{l}")
                        for hh in range(2):
                            t.matmul(ps[3 * l][:, hh * P:(hh + 1) * P], kTn[:, b, l, hh, :], kTn[:, b, l, hh, :], start=True, stop=True)
                            mm = t.matmul(ps[3 * l][:, 256 + hh * P:256 + (hh + 1) * P], kTn[:, b, l, hh, :], chunk(2 * l + hh, c), start=True, stop=True)
                        pe.did(mm, f"kk{c}_{l}")
                    scan(c - 1, 1)
                    for l in range(2):
                        dve.wait(t, f"L{c}_{l}")
                        for hh in range(2):
                            mm = t.transpose(ps[3 * l + 2][:, hh * P:(hh + 1) * P], L[:, l, hh, :], ident[:, :])
                        pe.did(mm, f"N{c}_{l}")
                    scan(c - 1, 2)
                    for l in range(2):
                        dve.wait(t, f"Y0_{c}_{l}")
                        pool.wait(t, f"Ld{c}_{l}")
                        for hh in range(2):
                            t.matmul(ps[3 * l][:, hh * P:(hh + 1) * P], NL1[:, l, 1, hh, :], NL1[:, l, 0, hh, :], start=True, stop=True)
                            mm = t.matmul(ps[3 * l][:, 256 + hh * P:256 + (hh + 1) * P], NL1[:, l, 0, hh, :], NL1[:, l, 1, hh, :], start=True, stop=True)
                        pe.did(mm, f"NL2_{c}_{l}")
                    for l in range(2):
                        act.wait(t, f"NL2_{c}_{l}")
                        for hh in range(2):
                            t.matmul(ps[3 * l][:, hh * P:(hh + 1) * P], NL2[:, l, 1, hh, :], NL2[:, l, 0, hh, :], start=True, stop=True)
                            mm = t.matmul(ps[3 * l][:, 256 + hh * P:256 + (hh + 1) * P], NL2[:, l, 0, hh, :], NL2[:, l, 1, hh, :], start=True, stop=True)
                        pe.did(mm, f"NL4_{c}_{l}")
                        for hh in range(2):
                            mm = t.matmul(ps[3 * l + 1][:, hh * P:(hh + 1) * P], NL2[:, l, 1, hh, :], Y[:, b, l, hh, :], start=True, stop=True)
                        pe.did(mm, f"dYa{c}_{l}")
                    for l in range(2):
                        act.wait(t, f"NL4_{c}_{l}")
                        for hh in range(2):
                            mm = t.matmul(ps[3 * l][:, hh * P:(hh + 1) * P], NL4[:, l, 0, hh, :], NL4[:, l, 1, hh, :], start=True, stop=True)
                        pe.did(mm, f"L8_{c}_{l}")
                        dve.wait(t, f"Ya{c}_{l}")
                        for hh in range(2):
                            mm = t.matmul(ps[3 * l + 1][:, hh * P:(hh + 1) * P], NL4[:, l, 1, hh, :], Y[:, b, l, hh, :], start=True, stop=True)
                        pe.did(mm, f"dYb{c}_{l}")
                    for l in range(2):
                        act.wait(t, f"L8_{c}_{l}")
                        dve.wait(t, f"Yb{c}_{l}")
                        for hh in range(2):
                            mm = t.matmul(ps[3 * l + 2][:, hh * P:(hh + 1) * P], L8[:, l, hh, :], Y[:, b, l, hh, :], start=True, stop=True)
                        pe.did(mm, f"dYc{c}_{l}")
                    for l in range(2):
                        dve.wait(t, f"Yc{c}_{l}")
                        for hh in range(2):
                            mm = t.transpose(ps[3 * l + 1][:, hh * P:(hh + 1) * P], Y[:, b, l, hh, :], ident[:, :])
                        pe.did(mm, f"X{c}_{l}")
                    for k in range(1, 4):
                        for l in range(2):
                            pool.wait(t, f"Lk{k}_{c}_{l}")
                            if k > 1:
                                dve.wait(t, f"Y{k - 1}_{c}_{l}")
                            for hh in range(2):
                                mm = t.matmul(ps[3 * l][:, hh * P:(hh + 1) * P], Lk[:, l, hh, :], Y[:, b, l, hh, :], start=True, stop=True)
                            pe.did(mm, f"Z{k}_{c}_{l}")
                        for l in range(2):
                            act.wait(t, f"Z{k}_{c}_{l}")
                            if k == 1:
                                act.wait(t, f"X{c}_{l}")
                            for hh in range(2):
                                mm = t.matmul(ps[3 * l + 2][:, hh * P:(hh + 1) * P], Xi[:, l, hh, :], Zi[:, l, hh, :], start=True, stop=True)
                            if k < 3:
                                for hh in range(2):
                                    mm = t.matmul(ps[3 * l + 2][:, 256 + hh * P:256 + (hh + 1) * P], Zi[:, l, hh, :], Xi[:, l, hh, :], start=True, stop=True)
                            pe.did(mm, f"dY{k}_{c}_{l}")
                for step in range(3):
                    if step == 0:
                        for l in range(2):
                            dve.wait(t, f"Y3_{NT - 1}_{l}")
                    scan(NT - 1, step)

            @block.scalar
            def _(a):
                for m in range(2 * HEADS):
                    if m > 0:
                        pe.wait(a, f"ss{m - 1}")
                    act.did(a.activation(sqT[:, :], qkvT[:, m, :], ACT.Square), f"sq{m}")
                act.did(a.activation(beta[:, :, :], gates[:, :, 0:HEADS], ACT.Sigmoid), "beta")
                dve.wait(a, "rs")
                act.did(a.activation(rn[:, 0:NT], rn[:, 0:NT], ACT.Sqrt))
                act.did(a.activation(rn[0:DEC, NT], rn[0:DEC, NT], ACT.Sqrt), "rs")
                dve.wait(a, "absx")
                a.wait_ge(hp_land, 32)
                act.did(a.activation(hp[:, 1, :], hp[:, 1, :], ACT.Exp))
                pool.wait(a, "masks")
                act.did(a.activation(sp_t[:, 1], sp_t[:, 0], ACT.Abs))
                act.drain(a)
                act.did(a.activation(sp_t[:, 1], sp_t[:, 1], ACT.Exp, scale=-1.0))
                act.drain(a)
                act.did(a.activation(sp_t[:, 1], sp_t[:, 1], ACT.Ln, bias=1.0), "ln")
                dve.wait(a, "Gc")
                act.did(a.activation(nbe[:, :, :], Gc[:, :, :], ACT.Exp), "nbe")

                def scan_u(c):
                    if c >= 0:
                        for l in range(2):
                            pe.wait(a, f"u{c}_{l}")
                            act.did(a.activation(u[:, l].rearrange("p h n -> p (h n)"), ps[6 + l][:, 256:512], ACT.Copy), f"u{c}_{l}")

                def flat(x):
                    return x.rearrange("p h n -> p (h n)")

                for c in range(NT):
                    b = c % 2
                    for l in range(2):
                        pe.wait(a, f"Gb{c}_{l}")
                        dve.wait(a, f"R{c}_{l}")
                        if c > 0:
                            pool.wait(a, f"qg{c - 1}_{l}")
                        act.did(a.activation(flat(egb[:, l]), ps[3 * l + 1][:, 0:256], ACT.Exp), f"egb{c}_{l}")
                        act.did(a.activation(flat(D1[:, l]), flat(D1[:, l]), ACT.Exp))
                        act.did(a.activation(flat(D0[:, l]), flat(D0[:, l]), ACT.Exp, scale=-1.0), f"D{c}_{l}")
                    for l in range(2):
                        pe.wait(a, f"kTn{c}_{l}")
                        act.did(a.activation(flat(kTn[:, b, l]), ps[3 * l + 2][:, 0:256], ACT.Copy), f"kTn{c}_{l}")
                    scan_u(c - 1)
                    for l in range(2):
                        pe.wait(a, f"N{c}_{l}")
                        act.did(a.activation(flat(N[:, l]), ps[3 * l + 2][:, 0:256], ACT.Copy), f"N{c}_{l}")
                    for l in range(2):
                        pe.wait(a, f"NL2_{c}_{l}")
                        act.did(a.activation(NL2[:, l].rearrange("p k h n -> p (k h n)"), ps[3 * l][:, :], ACT.Copy), f"NL2_{c}_{l}")
                    for l in range(2):
                        pe.wait(a, f"NL4_{c}_{l}")
                        act.did(a.activation(NL4[:, l].rearrange("p k h n -> p (k h n)"), ps[3 * l][:, :], ACT.Copy), f"NL4_{c}_{l}")
                    for l in range(2):
                        pe.wait(a, f"L8_{c}_{l}")
                        act.did(a.activation(flat(L8[:, l]), ps[3 * l][:, 0:256], ACT.Copy), f"L8_{c}_{l}")
                    for l in range(2):
                        pe.wait(a, f"X{c}_{l}")
                        act.did(a.activation(flat(Xi[:, l]), ps[3 * l + 1][:, 0:256], ACT.Copy), f"X{c}_{l}")
                    for k in range(1, 4):
                        for l in range(2):
                            pe.wait(a, f"Z{k}_{c}_{l}")
                            act.did(a.activation(flat(Zi[:, l]), ps[3 * l][:, 0:256], ACT.Copy), f"Z{k}_{c}_{l}")
                scan_u(NT - 1)

            @block.vector
            def _(v):
                v.wait_ge(hp_land, 32)
                dve.did(v.tensor_tensor(sp_t[:, 0], gates[:, :, 4:8], bc(hp[:, 0, :], [P, 9, HEADS], 1), ALU.add), "absx")
                pool.wait(v, "masks")
                pe.wait(v, f"ss{2 * HEADS - 1}")
                dve.did(v.tensor_scalar(rn[:, 0:NT].rearrange("p i m -> p (i m)"), ps[0][:, 0:64], EPS, None, ALU.add))
                dve.did(v.tensor_scalar(rn[0:DEC, NT], ps[0][0:DEC, 64:72], EPS, None, ALU.add), "rs")
                act.wait(v, "rs")
                for rows, s in ((rn[:, 0:NT], P), (rn[0:DEC, NT:NT + 1], DEC)):
                    dve.did(v.reciprocal(rows, rows))
                    dve.drain(v)
                    dve.did(v.tensor_scalar(rows[:, :, 0:HEADS], rows[:, :, 0:HEADS], float(P) ** -0.5, None, ALU.mult), "rn")
                act.wait(v, "ln")
                dve.did(v.tensor_scalar(sp_t[:, 0], sp_t[:, 0], 0.0, None, ALU.max))
                dve.drain(v)
                dve.did(v.tensor_tensor(sp_t[:, 0], sp_t[:, 0], sp_t[:, 1], ALU.add))
                dve.drain(v)
                dve.did(v.scalar_tensor_tensor(out=gg[:, :, :], in0=sp_t[:, 0], scalar=-1.0, in1=bc(hp[:, 1, :], [P, 9, HEADS], 1),
                                               op0=ALU.mult, op1=ALU.mult), "gg")
                pe.wait(v, "G")
                dve.did(v.tensor_copy(Gc[:, :, :].rearrange("p c h -> p (c h)"), ps[1][:, 0:NT * HEADS]), "Gc")
                act.wait(v, "nbe")
                act.wait(v, "beta")
                dve.did(v.scalar_tensor_tensor(out=nbe[:, :, :], in0=nbe[:, :, :], scalar=-1.0, in1=beta[:, 0:NT, :], op0=ALU.mult, op1=ALU.mult))
                dve.drain(v)

                def two(ap):
                    return ap.rearrange("p (h n) -> p h n", h=2)

                def scan_r(c):
                    if c >= 0:
                        for l in range(2):
                            pe.wait(v, f"ks{c}_{l}")
                            for hh in range(2):
                                h = 2 * l + hh
                                dve.did(v.scalar_tensor_tensor(out=r[:, l, hh, :], in0=ps[6 + l][:, hh * P:(hh + 1) * P], scalar=nbe[:, c, h:h + 1],
                                                               in1=vb[:, c % 2, l, hh, :], op0=ALU.mult, op1=ALU.add), f"r{c}_{l}")

                def scan_s(c):
                    if c == 4:
                        v.wait_ge(zland, 16 * (SLOTS // 2 + 2))
                    if c >= 0:
                        for l in range(2):
                            pe.wait(v, f"o{c}_{l}")
                            dve.did(v.tensor_tensor(two(Og[:, c, l * 256:(l + 1) * 256]), two(ps[6 + l][:, 256:512]),
                                                    bc(rn[:, c, 2 * l:2 * l + 2], [P, 2, P]), ALU.mult))
                            for hh in range(2):
                                h = 2 * l + hh
                                dve.did(v.scalar_tensor_tensor(out=S[:, h, :], in0=S[:, h, :], scalar=egl[:, c % 2, h:h + 1],
                                                               in1=ps[6 + l][:, hh * P:(hh + 1) * P], op0=ALU.mult, op1=ALU.add), f"S{c}_{l}")

                for c in range(NT):
                    b = c % 2
                    for l in range(2):
                        hs = slice(2 * l, 2 * l + 2)
                        pe.wait(v, f"kv{c}_{l}")
                        if c > 0:
                            pool.wait(v, f"kd{c - 1}_{l}")
                        dve.did(v.tensor_tensor(kn[:, l], two(ps[3 * l][:, 0:256]), bc(rn[:, c, 4 + 2 * l:6 + 2 * l], [P, 2, P]), ALU.mult), f"kn{c}_{l}")
                        dve.did(v.tensor_tensor(vb[:, b, l], two(ps[3 * l][:, 256:512]), bc(beta[:, c, hs], [P, 2, P]), ALU.mult), f"vb{c}_{l}")
                        pe.wait(v, f"Gb{c}_{l}")
                        dve.did(v.tensor_tensor(R[:, l], two(ps[3 * l + 1][:, 0:256]), bc(Gc[:, c, hs], [P, 2, P]), ALU.subtract))
                        dve.drain(v)
                        dve.did(v.scalar_tensor_tensor(out=D1[:, l], in0=R[:, l], scalar=0.0, in1=bc(neg_lo[:, :], [P, 2, P], 1), op0=ALU.min, op1=ALU.add))
                        dve.did(v.scalar_tensor_tensor(out=D0[:, l], in0=R[:, l], scalar=0.0, in1=bc(big_up[:, :], [P, 2, P], 1), op0=ALU.max, op1=ALU.add), f"R{c}_{l}")
                    scan_r(c - 1)
                    for l in range(2):
                        pe.wait(v, f"kk{c}_{l}")
                        act.wait(v, f"D{c}_{l}")
                        if c > 0:
                            pool.wait(v, f"Lk3_{c - 1}_{l}")
                        for hh in range(2):
                            h = 2 * l + hh
                            dve.did(v.scalar_tensor_tensor(out=L[:, l, hh, :], in0=ps[3 * l][:, hh * P:(hh + 1) * P], scalar=beta[:, c, h:h + 1],
                                                           in1=D0[:, l, hh, :], op0=ALU.mult, op1=ALU.mult), f"L{c}_{l}")
                        dve.did(v.tensor_tensor(at[:, b, l], two(ps[3 * l][:, 256:512]), D1[:, l], ALU.mult), f"at{c}_{l}")
                    for l in range(2):
                        act.wait(v, f"N{c}_{l}")
                        dve.did(v.tensor_tensor(NL1[:, l, 0], N[:, l], bc(bd[:, 0, :], [P, 2, P], 1), ALU.mult))
                        dve.drain(v)
                        dve.did(v.tensor_tensor(Y[:, b, l], bc(ident[:, :], [P, 2, P], 1), NL1[:, l, 0], ALU.subtract), f"Y0_{c}_{l}")
                    scan_s(c - 1)

                    def add(name, bank, sign=ALU.add):
                        for l in range(2):
                            pe.wait(v, f"d{name}{c}_{l}")
                            dve.did(v.tensor_tensor(Y[:, b, l], Y[:, b, l], two(ps[3 * l + bank][:, 0:256]), sign), f"{name}{c}_{l}")
                    add("Ya", 1)
                    add("Yb", 1)
                    add("Yc", 2)
                    for k in range(1, 4):
                        for l in range(2):
                            pe.wait(v, f"dY{k}_{c}_{l}")
                            if k < 3:
                                dve.did(v.tensor_tensor(Xi[:, l], Xi[:, l], two(ps[3 * l + 2][:, 256:512]), ALU.subtract))
                            dve.did(v.tensor_tensor(Y[:, b, l], Y[:, b, l], two(ps[3 * l + 2][:, 0:256]), ALU.subtract), f"Y{k}_{c}_{l}")
                scan_r(NT - 1)
                scan_s(NT - 1)
        ad = small[0:DEC, 32:36]
        s_in_land = sem("gdn_state_in")
        pe, act, dve, pool = steps("s3d_pe"), steps("s3d_act"), steps("s3d_dve"), steps("s3d_pool")
        hflat = hT[:, :, :].rearrange("p k t -> p (k t)")
        Sd = qkvT[:, 0:DEC, 0:GW].rearrange("p b (h v) -> p b h v", h=HEADS)
        Km = hflat[0:DEC, 4096:8192].rearrange("p (h b n) -> p h b n", h=HEADS, b=DEC)
        d8 = sqT[:, 0:64].rearrange("p (b c) -> p b c", b=DEC)
        kcol = sqT[:, 64:320].rearrange("p (h b c) -> p h b c", h=HEADS, b=DEC)
        qcol = sqT[:, 320:576].rearrange("p (h b c) -> p h b c", h=HEADS, b=DEC)
        a8 = sqT[0:DEC, 576:608].rearrange("p (h b) -> p h b", h=HEADS)
        abc = sqT[:, 608:640].rearrange("p (h b) -> p h b", h=HEADS)
        ones8 = sqT[0:DEC, 640:768]
        ada_col = s3.enter_context(nc.sbuf_tensor("ada_col", [P, KD, 512], F32))
        ada_col_land = sem("ada_col_land")
        ADA_EARLY = 4
        vd = NL2[0:DEC, 0].rearrange("p a b n -> p (a b n)")
        knd = NL2[0:DEC, 1].rearrange("p a b n -> p (a b n)")
        ud = NL4[0:DEC, 0].rearrange("p a b n -> p (a b n)")
        with nc.Block() as block:
            @block.sync
            def _(sp):
                def load_ada(c):
                    sp.dma_start(ada_col[:, :, :], w_ada[:, :, (4 + c) * 512:(5 + c) * 512]).then_inc(ada_col_land, 16)

                load_ada(0)
                for b in range(DEC):
                    sp.dma_start(Sd[:, b], A["state_gdn"][0, b].rearrange("h k v -> k h v")).then_inc(s_in_land, 16)
                pe.wait(sp, "ada0")
                load_ada(1)
                for b in range(DEC):
                    dve.wait(sp, f"S{b}")
                    sp.dma_start(O["gdn_s"][0, b].rearrange("h k v -> k h v"), Sd[:, b]).then_inc(s_out, 16)
                for c in range(2, ADA_EARLY):
                    pe.wait(sp, f"ada{c - 1}")
                    load_ada(c)
                sp.wait_ge(s_out, 16 * (1 + DEC))

            @block.gpsimd
            def _(g):
                pool.did(g.memset(d8, 1.0))
                pool.did(g.memset(ones8, 1.0))
                pool.drain(g)
                pool.did(g.affine_select(out=d8, in_=d8, compare_op=ALU.is_equal, fill=0.0, base=0,
                                         pattern=[[1, DEC], [-1, DEC]], channel_multiplier=0))
                pool.drain(g)
                for h in range(HEADS):
                    for col, m in ((kcol, HEADS + h), (qcol, h)):
                        pool.did(g.tensor_tensor(col[:, h], bc(qkvT[:, m, SEQ:T], [P, DEC, DEC]), d8, ALU.mult), "cols")

            @block.scalar
            def _(a):
                act.did(a.activation(ad, gg[0:DEC, NT, :], ACT.Exp), "ad")
                dve.wait(a, "ssq")
                act.did(a.activation(sp_t[:, 0], sp_t[:, 0], ACT.Sqrt), "rms")
                for i in range(9):
                    n = P if i < NT else DEC
                    pe.wait(a, f"oT{i}")
                    act.did(a.activation(hT[:, 0:HEADS, i * P:i * P + n], ps[i % 4][:, :].rearrange("p (h n) -> p h n", h=HEADS)[:, :, 0:n],
                                         ACT.Copy, scale=vecT[:, GNG:GNG + 1]), f"oT{i}")

            @block.tensor
            def _(t):
                for h in range(HEADS):
                    t.transpose(ps[0][0:DEC, h * P:(h + 1) * P], qkvT[:, 2 * HEADS + h, SEQ:T], ident[:, :])
                    mm = t.transpose(ps[1][0:DEC, h * P:(h + 1) * P], qkvT[:, HEADS + h, SEQ:T], ident[:, :])
                pe.did(mm, "rows")
                dve.wait(t, "a8")
                pool.wait(t, "cols")
                def ada(c, bank):
                    t.wait_ge(ada_col_land, 16 * (c + 1))
                    for m in range(4):
                        for k in range(KD):
                            mm = t.matmul(ps[bank][:, m * 9:m * 9 + 9], ada_col[:, k, m * P:(m + 1) * P], cT[:, k, :],
                                          start=(k == 0), stop=(k == KD - 1))
                    pe.did(mm, f"ada{c}")

                pe.did(t.matmul(ps[2][:, 0:32], ones8, a8.rearrange("p h b -> p (h b)"), start=True, stop=True), "abc")
                ada(0, 7)
                t.wait_ge(s_in_land, 16 * DEC)
                pool.wait(t, "cols")
                for h in range(HEADS):
                    for b in range(DEC):
                        mm = t.matmul(ps[3][0:DEC, h * P:(h + 1) * P], kcol[:, h, b, :], Sd[:, b, h, :], start=(b == 0), stop=(b == DEC - 1))
                pe.did(mm, "kS")
                dve.wait(t, "ud")
                dve.wait(t, "mod0")
                for b in range(DEC):
                    if b >= 4:
                        dve.wait(t, f"S{b - 4}")
                    for h in range(HEADS):
                        mm = t.matmul(ps[4 + b % 4][:, h * P:(h + 1) * P], Km[:, h, b, :], ud[:, h * P:(h + 1) * P], start=True, stop=True)
                    pe.did(mm, f"outer{b}")
                ada(1, 0)
                dve.wait(t, "Snew")
                for h in range(HEADS):
                    for b in range(DEC):
                        mm = t.matmul(ps[2][0:DEC, h * P:(h + 1) * P], qcol[:, h, b, :], Sd[:, b, h, :], start=(b == 0), stop=(b == DEC - 1))
                pe.did(mm, "qS")
                ada(2, 7)
                dve.wait(t, "mod1")
                for i in range(9):
                    n = P if i < NT else DEC
                    dve.wait(t, f"on{i}")
                    if i >= 4:
                        act.wait(t, f"oT{i - 4}")
                    for h in range(HEADS):
                        mm = t.transpose(ps[i % 4][:, h * P:h * P + n], Og[0:n, i, h * P:(h + 1) * P], ident[0:n, 0:n])
                    pe.did(mm, f"oT{i}")
                ada(3, 6)

            @block.vector
            def _(v):
                def heads(ap):
                    return ap.rearrange("p (h n) -> p h n", h=HEADS)

                act.wait(v, "ad")
                dve.did(v.tensor_tensor(a8, bc(ad, [DEC, HEADS, DEC]), bc(ident[0:DEC, 0:DEC], [DEC, HEADS, DEC], 1), ALU.mult), "a8")
                pe.wait(v, "rows")
                dve.did(v.tensor_copy(vd, ps[0][0:DEC, :]))
                dve.did(v.tensor_tensor(heads(knd), heads(ps[1][0:DEC, :]), bc(rn[0:DEC, NT, 4:8], [DEC, HEADS, P]), ALU.mult))
                dve.drain(v)
                for h in range(HEADS):
                    dve.did(v.tensor_tensor(Km[:, h], bc(knd[:, h * P:(h + 1) * P], [DEC, DEC, P], 1), bc(ident[0:DEC, 0:DEC], [DEC, DEC, P]), ALU.mult))
                pe.wait(v, "abc")
                dve.did(v.tensor_copy(abc, ps[2][:, 0:32].rearrange("p (h b) -> p h b", h=HEADS)))
                dve.did(v.tensor_tensor(small[0:DEC, 36:40], ad, rn[0:DEC, NT, 4:8], ALU.mult))
                def mod(c, bank):
                    pe.wait(v, f"ada{c}")
                    m0 = 4 * (4 + c)
                    dve.did(v.tensor_tensor(modT[:, m0:m0 + 4, :], ps[bank][:, 0:36].rearrange("p (m n) -> p m n", m=4),
                                            vecT[:, B_ADA + m0:B_ADA + m0 + 4].unsqueeze(2).to_broadcast([P, 4, 9]), ALU.add), f"mod{c}")

                mod(0, 7)
                pe.wait(v, "kS")
                dve.drain(v)
                dve.did(v.tensor_tensor(heads(ud), heads(ps[3][0:DEC, :]), bc(small[0:DEC, 36:40], [DEC, HEADS, P]), ALU.mult))
                dve.drain(v)
                dve.did(v.tensor_tensor(ud, vd, ud, ALU.subtract))
                dve.drain(v)
                dve.did(v.tensor_tensor(heads(ud), heads(ud), bc(beta[0:DEC, NT, :], [DEC, HEADS, P]), ALU.mult), "ud")
                for b in range(DEC):
                    pe.wait(v, f"outer{b}")
                    for h in range(HEADS):
                        dve.did(v.scalar_tensor_tensor(out=Sd[:, b, h, :], in0=Sd[:, b, h, :], scalar=abc[:, h, b:b + 1],
                                                       in1=ps[4 + b % 4][:, h * P:(h + 1) * P], op0=ALU.mult, op1=ALU.add), f"S{b}")
                dve.at["Snew"] = dve.n
                mod(1, 0)
                pe.wait(v, "qS")
                dve.did(v.tensor_tensor(heads(Og[0:DEC, NT, :]), heads(ps[2][0:DEC, :]), bc(rn[0:DEC, NT, 0:4], [DEC, HEADS, P]), ALU.mult))
                dve.drain(v)
                sqv = qkvT[:, 0:9, GW:2 * GW]
                pe.wait(v, "rows")
                dve.did(v.tensor_tensor(sqv, Og[:, :, :], Og[:, :, :], ALU.mult))
                dve.drain(v)
                ms = sp_t[:, 0].rearrange("p i h -> p (i h)")
                dve.did(v.tensor_reduce(sp_t[:, 0], sqv.rearrange("p i (h n) -> p i h n", h=HEADS), AX.X, ALU.add))
                dve.drain(v)
                dve.did(v.tensor_scalar(ms, ms, 1.0 / P, EPS, ALU.mult, ALU.add), "ssq")
                act.wait(v, "rms")
                dve.did(v.reciprocal(ms, ms))
                dve.drain(v)
                for i in range(9):
                    n = P if i < NT else DEC
                    dve.did(v.tensor_tensor(heads(Og[0:n, i, :]), heads(Og[0:n, i, :]), bc(sp_t[0:n, 0, i, :], [n, HEADS, P]), ALU.mult))
                    dve.drain(v)
                    dve.did(v.tensor_tensor(Og[0:n, i, :], Og[0:n, i, :], Z[0:n, i, :], ALU.mult), f"on{i}")
                mod(2, 7)
                mod(3, 6)
        s3.close()
        if stages == 3:
            return finish_debug(nc, sem, dbg, locals())


        mid2.close()

        s4 = ctx.enter_context(ExitStack())
        t4 = lambda name, shape: s4.enter_context(nc.sbuf_tensor(name, shape, F32))
        y1T = t4("y1T", [P, 4, T])
        Yt = t4("Yt", [P, 9, GW])
        s4a = ctx.enter_context(ExitStack())
        t4 = lambda name, shape: s4a.enter_context(nc.sbuf_tensor(name, shape, F32))
        NG = 8
        lamrow = t4("lamrow", [GROUPS, 2, P])
        drow = t4("drow", [GROUPS, CH])
        lr, li, dtl = t4("lr", [P, GROUPS]), t4("li", [P, GROUPS]), t4("dtl", [P, GROUPS])
        D16 = t4("D16", [CH, GROUPS])
        B1, B2 = t4("B1", [P, GROUPS, CH]), t4("B2", [P, GROUPS, CH])
        Bb = t4("Bb", [P, GROUPS, CH])
        crow1, crow2 = t4("crow1", [P, 4, P]), t4("crow2", [P, 4, P])
        Q1, Q2 = t4("Q1", [P, 4, P]), t4("Q2", [P, 4, P])
        x0row = t4("x0row", [P, 2, P])
        X0 = t4("X0", [P, GROUPS, DEC])
        X0r, X0i = t4("X0r", [P, GROUPS, DEC]), t4("X0i", [P, GROUPS, DEC])
        X1 = t4("X1", [P, DEC, GROUPS])
        J = t4("J", [P, P])
        w4 = t4("w4", [P, 12, GROUPS])
        LC = t4("LC", [P, 2, GROUPS, LAGS + 1])
        LB = t4("LB", [P, 2, GROUPS, LAGS])
        rho, ph = t4("rho", [P, GROUPS]), t4("ph", [P, 2, GROUPS])
        Ec, Es = t4("Ec", [P, NG, NCH + 1]), t4("Es", [P, NG, NCH + 1])
        e1, e2 = t4("e1", [P, NG, NCH // 2]), t4("e2", [P, NG, NCH // 2])
        e3, e4 = t4("e3", [P, NG, NCH // 2]), t4("e4", [P, NG, NCH // 2])
        W = t4("W", [P, NG, LAGS, CH])
        Wt = t4("Wt", [P, NG, LAGS + 1, CH])
        CL = t4("CL", [P, NG, LAGS + 1, CH])
        CS = t4("CS", [P, NG, LAGS, CH])
        BM, BS = t4("BM", [P, NG, P]), t4("BS", [P, NG, P])
        Kt = t4("Kt", [CH, NG, LAGS, CH])
        TT = t4("TT", [P, NG, LAGS, CH])
        U = t4("U", [P, NG, P])
        Ud = t4("Ud", [P, NG, 2, DEC])
        Vq = t4("Vq", [DEC, NG, 2 * LAGS - 1, CH])
        zin = t4("zin", [P, NG, NCH])
        z2 = t4("z2", [P, NG, NCH])
        zs = t4("zs", [P, NG, NCH + 1])
        Zc, Zs = t4("Zc", [P, NG, NCH]), t4("Zs", [P, NG, NCH])
        ADA_LATE = 4
        MOD_LATE = 48 - 4 * ADA_LATE
        ada_late = [y1T[:, :, :].rearrange("p k n -> p (k n)")[:, 0:KD * 512].rearrange("p (k n) -> p k n", k=KD),
                    Yt[:, 0:KD, :]]
        ada_late_land = [sem("ada_late_land0"), sem("ada_late_land1")]
        zl = t4("zl", [P, 2, GROUPS])
        xrow = t4("xrow", [P, 2, P])
        prow = t4("prow", [GROUPS, P])
        s5_land, s5_x0, tt_land, s5_out = sem("s5_land"), sem("s5_x0"), sem("tt_land"), sem("s5_out")
        s5_c = sem("s5_c")
        pe, act, dve, pool = steps("s4_pe"), steps("s4_act"), steps("s4_dve"), steps("s4_pool")
        s5 = {n: A["s5_" + n][0] for n in ("lambda_re", "lambda_im", "log_dt", "b_re", "b_im", "c_re", "c_im", "d")}
        ROUND = 12582912.0

        with nc.Block() as block:
            @block.sync
            def _(sp):
                for n, name in enumerate(("lambda_re", "lambda_im")):
                    for rep in range(2):
                        sp.dma_start(lamrow[:, n, rep * ST:(rep + 1) * ST], s5[name]).then_inc(s5_land, 16)
                sp.dma_start(dtl[:, :], s5["log_dt"].unsqueeze(0).to_broadcast([P, GROUPS])).then_inc(s5_land, 16)
                sp.dma_start(drow[:, :], s5["d"].rearrange("(g c) -> g c", c=CH)).then_inc(s5_land, 16)
                b_re, b_im = (s5[n].rearrange("g p c -> p g c") for n in ("b_re", "b_im"))
                for dst, src in ((B1[0:ST], b_re), (B1[ST:P], b_im), (B2[0:ST], b_im), (B2[ST:P], b_re)):
                    sp.dma_start(dst, src).then_inc(s5_land, 16)
                c_re, c_im = (s5[n].rearrange("(q g) c p -> (g c) q p", q=4) for n in ("c_re", "c_im"))
                for dst, src in ((crow1[:, :, 0:ST], c_re), (crow1[:, :, ST:P], c_im), (crow2[:, :, 0:ST], c_im), (crow2[:, :, ST:P], c_re)):
                    sp.dma_start(dst, src).then_inc(s5_c, 16)
                for n, name in enumerate(("state_s5_re", "state_s5_im")):
                    sp.dma_start(x0row[:, :, n * ST:(n + 1) * ST], A[name][0].rearrange("(x b) g p -> (b g) x p", x=2)).then_inc(s5_x0, 16)
                for b in range(ADA_LATE):
                    if b >= 2:
                        pe.wait(sp, f"ada{b - 2}")
                    sp.dma_start(ada_late[b % 2], w_ada[:, :, (MOD_LATE // 4 + b) * 512:(MOD_LATE // 4 + b + 1) * 512]).then_inc(ada_late_land[b % 2], 16)
                for q in range(4):
                    dve.wait(sp, f"K{q}")
                    if q == 0:
                        pool.wait(sp, "clear")
                    else:
                        pe.wait(sp, f"y{q - 1}")
                    for j in range(LAGS):
                        sp.dma_start(TT[j * CH:(j + 1) * CH, :, j:LAGS, :], Kt[:, :, 0:LAGS - j, :]).then_inc(tt_land, 16)
                act.wait(sp, "states")
                for n, (p_out, s_out_) in enumerate((("re_p", "re_s"), ("im_p", "im_s"))):
                    sp.dma_start(O[p_out][0, 0], prow[:, n * ST:(n + 1) * ST]).then_inc(s5_out, 16)
                    sp.dma_start(O[s_out_][0].rearrange("(x b) g p -> (b g) x p", x=2), xrow[:, :, n * ST:(n + 1) * ST]).then_inc(s5_out, 16)
                sp.wait_ge(s5_out, 64)

            @block.gpsimd
            def _(g):
                pool.did(g.memset(J[:, :], 0.0))
                pool.did(g.memset(TT[:, :, :, :], 0.0))
                pool.did(g.memset(Vq[:, :, :, :], 0.0))
                pool.did(g.memset(zs[:, :, 0:1], 0.0))
                pool.did(g.memset(Ec[:, :, 0:1], 1.0))
                pool.did(g.memset(Es[:, :, 0:1], 0.0))
                pool.did(g.memset(LC[:, 0, :, 0:1], 1.0))
                pool.did(g.memset(LC[:, 1, :, 0:1], 0.0))
                pool.drain(g)
                pool.did(g.affine_select(out=J[:, :], in_=J[:, :], compare_op=ALU.not_equal, fill=-1.0, base=-ST,
                                         pattern=[[-1, P]], channel_multiplier=1))
                pool.drain(g)
                pool.did(g.affine_select(out=J[:, :], in_=J[:, :], compare_op=ALU.not_equal, fill=1.0, base=ST,
                                         pattern=[[-1, P]], channel_multiplier=1), "clear")
                for q in range(4):
                    gs = slice(q * NG, (q + 1) * NG)
                    if q > 0:
                        dve.wait(g, f"zc{q - 1}")
                        pool.drain(g)
                    dve.wait(g, "ph")
                    pool.did(g.tensor_copy(Es[:, :, 1:2], ph[:, 1, gs].unsqueeze(2)), f"e{q}_0")
                    w = 1
                    while w < NCH:
                        step = w.bit_length()
                        dve.wait(g, f"e{q}_{step - 1}")
                        pool.drain(g)
                        cw, sw = (x[:, :, w:w + 1].to_broadcast([P, NG, w]) for x in (Ec, Es))
                        pool.did(g.tensor_tensor(e3[:, :, 0:w], Ec[:, :, 1:w + 1], sw, ALU.mult))
                        pool.did(g.tensor_tensor(e4[:, :, 0:w], Es[:, :, 1:w + 1], cw, ALU.mult))
                        pool.drain(g)
                        pool.did(g.tensor_tensor(Es[:, :, w + 1:2 * w + 1], e3[:, :, 0:w], e4[:, :, 0:w], ALU.add), f"e{q}_{step}")
                        w *= 2
                    for bnk in range(2):
                        dve.wait(g, f"rot{q}_{bnk}")
                        part = slice(4 * bnk, 4 * bnk + 4)
                        pool.did(g.tensor_tensor(zin[:, part], zin[:, part], z2[:, part], ALU.add), f"zin{q}_{bnk}")
                    dve.wait(g, f"scan{q}")
                    if q > 0:
                        pe.wait(g, f"y{q - 1}")
                    pool.did(g.tensor_tensor(Zs[:, :, :], zs[:, :, 0:NCH], Es[:, :, 0:NCH], ALU.mult), f"zs{q}")
                    pool.did(g.tensor_tensor(zl[:, 1, gs], zs[:, :, NCH], Es[:, :, NCH], ALU.mult), f"zl{q}")

            @block.tensor
            def _(t):
                t.wait_ge(s5_land, 16 * 10)
                t.transpose(ps[0][:, 0:GROUPS], lamrow[:, 0, :], ident[0:GROUPS, 0:GROUPS])
                t.transpose(ps[0][:, GROUPS:2 * GROUPS], lamrow[:, 1, :], ident[0:GROUPS, 0:GROUPS])
                pe.did(t.transpose(ps[0][0:CH, 64:96], drow[:, :], ident[0:GROUPS, 0:GROUPS]), "lam")
                t.wait_ge(s5_x0, 32)
                for n in range(2):
                    mm = t.transpose(ps[1][:, n * P:(n + 1) * P], x0row[:, n, :], ident[:, :])
                pe.did(mm, "x0")
                dve.wait(t, "crow")
                for q in range(4):
                    t.transpose(ps[2][:, q * P:(q + 1) * P], crow1[:, q, :], ident[:, :])
                    mm = t.transpose(ps[3][:, q * P:(q + 1) * P], crow2[:, q, :], ident[:, :])
                pe.did(mm, "Q")
                for b in range(ADA_LATE):
                    t.wait_ge(ada_late_land[b % 2], 16 * (b // 2 + 1))
                    for m in range(4):
                        for k in range(KD):
                            mm = t.matmul(ps[4 + b][:, m * 9:m * 9 + 9], ada_late[b % 2][:, k, m * P:(m + 1) * P], cT[:, k, :],
                                          start=(k == 0), stop=(k == KD - 1))
                    pe.did(mm, f"ada{b}")
                dve.wait(t, "mods")
                dve.wait(t, "lam")
                act.wait(t, "Q")
                act.wait(t, "X0")
                pool.wait(t, "clear")
                for q in range(4):
                    gs = [q * NG + x for x in range(NG)]
                    if q > 0:
                        dve.wait(t, f"rot{q - 1}_1")
                    dve.wait(t, f"W{q}")
                    for x in range(NG):
                        mm = t.transpose(ps[x // 4][:, (x % 4) * P:(x % 4 + 1) * P], W[:, x].rearrange("p j c -> p (j c)"), ident[:, :])
                    pe.did(mm, f"BM{q}")
                    for x in range(NG):
                        mm = t.transpose(ps[2 + x // 4][:, (x % 4) * P:(x % 4 + 1) * P],
                                         V[:, gs[x]].rearrange("p j c -> p (j c)"), ident[:, :])
                    dve.wait(t, f"Vq{q}")
                    if q > 0:
                        act.wait(t, f"yd{q - 1}")
                    for x in range(NG):
                        for v_ in range(2):
                            sl = slice(LAGS - 1, 2 * LAGS - 1) if v_ == 0 else slice(0, LAGS)
                            mm = t.transpose(ps[6][:, (2 * x + v_) * DEC:(2 * x + v_ + 1) * DEC],
                                             Vq[:, x, sl, :].rearrange("b j c -> b (j c)"), ident[0:DEC, 0:DEC])
                    pe.did(mm, f"U{q}")
                    if q > 0:
                        act.wait(t, f"yp{q - 1}")
                    dve.wait(t, f"CL{q}")
                    for x in range(NG):
                        mm = t.matmul(ps[4 + x // 4][0:CH, (x % 4) * P:(x % 4 + 1) * P], Bb[:, gs[x], :],
                                      CL[:, x, 0:LAGS, :].rearrange("p k c -> p (k c)"), start=True, stop=True)
                    pe.did(mm, f"K{q}")
                    act.wait(t, f"BM{q}")
                    act.wait(t, f"U{q}")
                    for x in range(NG):
                        t.matmul(ps[x // 4][:, (x % 4) * P:(x % 4 + 1) * P], BM[:, x, :], U[:, x, :], start=True, stop=True)
                        mm = t.matmul(ps[2 + x // 4][:, (x % 4) * P:(x % 4 + 1) * P], BS[:, x, :], U[:, x, :], start=True, stop=True)
                    pe.did(mm, f"b{q}")
                    dve.wait(t, "x0")
                    if q > 0:
                        act.wait(t, f"x1_{q - 1}")
                    lo, hi = q * NG, (q + 1) * NG
                    reg = ps[7][:, 0:NG * DEC]
                    t.matmul(reg, ident[:, :], X0r[:, lo:hi, :].rearrange("p g b -> p (g b)"), start=True, stop=False, skip_group_check=True)
                    t.matmul(reg, J[:, :], X0i[:, lo:hi, :].rearrange("p g b -> p (g b)"), start=False, stop=False, skip_group_check=True)
                    for x in range(NG):
                        mm = t.matmul(ps[7][:, x * DEC:(x + 1) * DEC], BM[:, x, :], Ud[:, x, 1, :], start=False, stop=(x == NG - 1), skip_group_check=True)
                    pe.did(mm, f"x1_{q}")
                    dve.wait(t, f"zc{q}")
                    pool.wait(t, f"zs{q}")
                    dve.wait(t, f"K{q}")
                    t.wait_ge(tt_land, 16 * LAGS * (q + 1))
                    for x in range(NG):
                        dst = ps[4 + x // 4][:, (x % 4) * P:(x % 4 + 1) * P]
                        t.matmul(dst, U[:, x, :], TT[:, x].rearrange("p j c -> p (j c)"), start=True, stop=False)
                        t.matmul(dst, Zc[:, x, :], CL[:, x, 1:LAGS + 1, :].rearrange("p k c -> p (k c)"), start=False, stop=False)
                        mm = t.matmul(dst, Zs[:, x, :], CS[:, x].rearrange("p k c -> p (k c)"), start=False, stop=True)
                    pe.did(mm, f"yp{q}")
                    for x in range(NG):
                        dst = ps[6][0:DEC, x * CH:(x + 1) * CH]
                        t.matmul(dst, Ud[:, x, 0, :], TT[:, x, 0, :], start=True, stop=False)
                        mm = t.matmul(dst, X0[:, gs[x], :], CL[:, x, 1, :], start=False, stop=True)
                    pe.did(mm, f"y{q}")
                act.wait(t, "x1_3")
                pool.wait(t, "zl3")
                t.matmul(ps[0][0:GROUPS, 0:P], zl[:, 0, :], ident[:, :], start=True, stop=False)
                t.matmul(ps[0][0:GROUPS, 0:P], zl[:, 1, :], J[:, :], start=False, stop=True)
                for n in range(2):
                    mm = t.transpose(ps[1][:, n * P:(n + 1) * P], X1[:, 4 * n:4 * n + 4, :].rearrange("p b g -> p (b g)"), ident[:, :])
                pe.did(mm, "states")

            @block.scalar
            def _(a):
                a.wait_ge(s5_land, 16 * 10)
                act.did(a.activation(dtl[:, :], dtl[:, :], ACT.Exp), "dt")
                dve.wait(a, "xre")
                act.did(a.activation(w4[:, 2], w4[:, 0], ACT.Exp), "r1")
                act.did(a.activation(rho[:, :], w4[:, 0], ACT.Exp, scale=float(LAGS)))
                dve.wait(a, "red")
                act.did(a.activation(w4[:, 3], w4[:, 1], ACT.Sin))
                act.did(a.activation(w4[:, 4], w4[:, 1], ACT.Sin, scale=0.5), "sin")
                pe.wait(a, "Q")
                act.did(a.activation(Q1[:, :, :].rearrange("p q n -> p (q n)"), ps[2][:, :], ACT.Copy))
                act.did(a.activation(Q2[:, :, :].rearrange("p q n -> p (q n)"), ps[3][:, :], ACT.Copy), "Q")
                pe.wait(a, "x0")
                act.did(a.activation(X0[:, :, :].rearrange("p g (x b) -> p x b g", x=2),
                                     ps[1][:, 0:256].rearrange("p (x b g) -> p x b g", x=2, b=4), ACT.Copy), "X0")
                for q in range(4):
                    pe.wait(a, f"BM{q}")
                    if q > 0:
                        pe.wait(a, f"x1_{q - 1}")
                    for bnk in range(2):
                        src = ps[bnk][:, :].rearrange("p (g n) -> p g n", g=4)
                        part = slice(4 * bnk, 4 * bnk + 4)
                        act.did(a.activation(BM[:, part, :], src, ACT.Copy))
                        act.did(a.activation(BS[:, part, 0:ST], src[:, :, ST:P], ACT.Copy))
                        act.did(a.activation(BS[:, part, ST:P], src[:, :, 0:ST], ACT.Copy, scale=-1.0), f"BM{q}")
                    pe.wait(a, f"U{q}")
                    if q > 0:
                        pe.wait(a, f"y{q - 1}")
                    for bnk in range(2):
                        act.did(a.activation(U[:, 4 * bnk:4 * bnk + 4, :].rearrange("p g n -> p (g n)"), ps[2 + bnk][:, :], ACT.Copy))
                    act.did(a.activation(Ud[:, :, :, :].rearrange("p g v b -> p (g v b)"), ps[6][:, 0:2 * NG * DEC], ACT.Copy), f"U{q}")
                    pe.wait(a, f"x1_{q}")
                    act.did(a.activation(X1[:, :, q * NG:(q + 1) * NG].rearrange("p b g -> p g b"),
                                         ps[7][:, 0:NG * DEC].rearrange("p (g b) -> p g b", g=NG), ACT.Copy), f"x1_{q}")
                    pe.wait(a, f"yp{q}")
                    for bnk in range(2):
                        c0 = (q * NG + 4 * bnk) * CH
                        for x in range(4):
                            act.did(a.activation(Yt[:, 0:LAGS, c0 + x * CH:c0 + (x + 1) * CH],
                                                 ps[4 + bnk][:, x * P:(x + 1) * P].rearrange("p (j c) -> p j c", j=LAGS), ACT.Gelu_apprx_tanh), f"yp{q}")
                    pe.wait(a, f"y{q}")
                    act.did(a.activation(Yt[0:DEC, LAGS, q * P:(q + 1) * P], ps[6][0:DEC, 0:P], ACT.Gelu_apprx_tanh), f"yd{q}")
                pe.wait(a, "states")
                act.did(a.activation(prow[:, :], ps[0][0:GROUPS, 0:P], ACT.Copy))
                act.did(a.activation(xrow[:, :, :].rearrange("p x n -> p (x n)"), ps[1][:, 0:256], ACT.Copy), "states")

            @block.vector
            def _(v):
                w = lambda n: w4[:, n]

                def tt(out, x, y, op, name=None, wait=True):
                    if wait:
                        dve.drain(v)
                    dve.did(v.tensor_tensor(out, x, y, op), name)

                def ts(out, x, c1, c2, op1, op2, name=None):
                    dve.drain(v)
                    dve.did(v.tensor_scalar(out, x, c1, c2, op1, op2) if c2 is not None else v.tensor_scalar(out, x, c1, None, op1), name)

                v.wait_ge(s5_land, 16 * 10)
                v.wait_ge(s5_c, 64)
                dve.did(v.tensor_scalar(crow1[:, :, ST:P], crow1[:, :, ST:P], -1.0, None, ALU.mult))
                dve.did(v.tensor_scalar(crow2[:, :, :], crow2[:, :, :], -1.0, None, ALU.mult), "crow")
                dve.did(v.tensor_scalar(B2[0:ST], B2[0:ST], -1.0, None, ALU.mult))
                pe.wait(v, "lam")
                dve.did(v.tensor_copy(lr[:, :], ps[0][:, 0:GROUPS]))
                dve.did(v.tensor_copy(li[:, :], ps[0][:, GROUPS:2 * GROUPS]))
                dve.did(v.tensor_copy(D16[:, :], ps[0][0:CH, 64:96]), "lam")
                act.wait(v, "dt")
                tt(w(0), lr[:, :], dtl[:, :], ALU.mult, "xre")
                tt(w(1), li[:, :], dtl[:, :], ALU.mult)
                ts(w(5), w(1), 1.0 / PI2, ROUND, ALU.mult, ALU.add)
                ts(w(5), w(5), ROUND, None, ALU.subtract, None)
                dve.drain(v)
                dve.did(v.scalar_tensor_tensor(out=w(1), in0=w(5), scalar=-6.28125, in1=w(1), op0=ALU.mult, op1=ALU.add))
                dve.drain(v)
                dve.did(v.scalar_tensor_tensor(out=w(1), in0=w(5), scalar=-(PI2 - 6.28125), in1=w(1), op0=ALU.mult, op1=ALU.add))
                ts(w(1), w(1), 3.1415925, -3.1415925, ALU.min, ALU.max, "red")
                act.wait(v, "sin")
                tt(w(5), w(4), w(4), ALU.mult)
                ts(w(5), w(5), -2.0, 1.0, ALU.mult, ALU.add)
                tt(LC[:, 0, :, 1], w(2), w(5), ALU.mult)
                tt(LC[:, 1, :, 1], w(2), w(3), ALU.mult)
                ts(w(6), LC[:, 0, :, 1], -1.0, None, ALU.add, None)
                tt(w(7), lr[:, :], lr[:, :], ALU.mult)
                tt(w(8), li[:, :], li[:, :], ALU.mult)
                tt(w(7), w(7), w(8), ALU.add)
                dve.drain(v)
                dve.did(v.reciprocal(w(7), w(7)))
                tt(w(8), w(6), lr[:, :], ALU.mult)
                tt(w(9), LC[:, 1, :, 1], li[:, :], ALU.mult)
                tt(w(8), w(8), w(9), ALU.add)
                tt(w(8), w(8), w(7), ALU.mult)
                tt(w(9), LC[:, 1, :, 1], lr[:, :], ALU.mult)
                tt(w(10), w(6), li[:, :], ALU.mult)
                tt(w(9), w(9), w(10), ALU.subtract)
                tt(w(9), w(9), w(7), ALU.mult)
                full = [P, GROUPS, CH]
                wt = Wt[:, 0:4].rearrange("p g k c -> p (g k c)")[:, 0:GROUPS * CH].rearrange("p (g c) -> p g c", c=CH)
                tt(Bb[:, :, :], B1[:, :, :], bc(w(8), full), ALU.mult)
                tt(wt, B2[:, :, :], bc(w(9), full), ALU.mult)
                tt(Bb[:, :, :], Bb[:, :, :], wt, ALU.add)
                tt(B2[:, :, :], B2[:, :, :], bc(w(8), full), ALU.mult)
                tt(wt, B1[:, :, :], bc(w(9), full), ALU.mult)
                tt(B2[:, :, :], B2[:, :, :], wt, ALU.subtract)
                pool.wait(v, "clear")
                for k in range(2, LAGS + 1):
                    a_, b_ = LC[:, 0, :, k - 1], LC[:, 1, :, k - 1]
                    tt(w(6), a_, LC[:, 0, :, 1], ALU.mult)
                    tt(w(7), b_, LC[:, 1, :, 1], ALU.mult)
                    tt(LC[:, 0, :, k], w(6), w(7), ALU.subtract)
                    tt(w(6), a_, LC[:, 1, :, 1], ALU.mult)
                    tt(w(7), b_, LC[:, 0, :, 1], ALU.mult)
                    tt(LC[:, 1, :, k], w(6), w(7), ALU.add)
                dve.drain(v)
                for k in range(LAGS):
                    dve.did(v.tensor_copy(LB[:, :, :, k], LC[:, :, :, LAGS - 1 - k]))
                c_, s_ = w(5), w(3)
                for n in range(3):
                    co, so = (ph[:, 0, :], ph[:, 1, :]) if n == 2 else (w(5), w(3))
                    tt(w(6), c_, c_, ALU.mult)
                    tt(w(7), s_, s_, ALU.mult)
                    tt(w(8), c_, s_, ALU.mult)
                    tt(co, w(6), w(7), ALU.subtract)
                    ts(so, w(8), 2.0, None, ALU.mult, None, "ph")
                act.wait(v, "X0")
                tt(X0r[:, :, :], X0[:, :, :], bc(LC[:, 0, :, 1], [P, GROUPS, DEC]), ALU.mult)
                tt(X0i[:, :, :], X0[:, :, :], bc(LC[:, 1, :, 1], [P, GROUPS, DEC]), ALU.mult, "x0")
                act.wait(v, "Q")

                pe.wait(v, f"ada{ADA_LATE - 1}")
                for b in range(ADA_LATE):
                    m0 = MOD_LATE + 4 * b
                    dve.did(v.tensor_tensor(modT[:, m0:m0 + 4, :], ps[4 + b][:, 0:36].rearrange("p (m n) -> p m n", m=4),
                                            vecT[:, B_ADA + m0:B_ADA + m0 + 4].unsqueeze(2).to_broadcast([P, 4, 9]), ALU.add), "mods")
                for q in range(4):
                    gs = slice(q * NG, (q + 1) * NG)

                    def table(dst, tmp, lam, x, y, n, op, name, first=0):
                        shape = [P, NG, n, CH]
                        lr_, li_ = (lam[:, c, gs, first:first + n].unsqueeze(3).to_broadcast(shape) for c in range(2))
                        tt(dst, lr_, x.unsqueeze(2).to_broadcast(shape), ALU.mult)
                        tt(tmp, li_, y.unsqueeze(2).to_broadcast(shape), ALU.mult)
                        tt(dst, dst, tmp, op, name)
                    if q > 0:
                        pe.wait(v, f"BM{q - 1}")
                    table(W[:, :, :, :], Wt[:, :, 0:LAGS, :], LB, Bb[:, gs, :], B2[:, gs, :], LAGS, ALU.add, f"W{q}")
                    if q > 0:
                        pe.wait(v, f"U{q - 1}")
                    dve.did(v.tensor_copy(Vq[:, :, LAGS - 1, :], Vd[:, q * P:(q + 1) * P].rearrange("b (g c) -> b g c", c=CH)), f"Vq{q}")
                    if q > 0:
                        pe.wait(v, f"y{q - 1}")
                    q1, q2 = (x[:, q, :].rearrange("p (g c) -> p g c", c=CH) for x in (Q1, Q2))
                    table(CL[:, :, :, :], Wt[:, :, :, :], LC, q1, q2, LAGS + 1, ALU.add, f"CL{q}")
                    table(CS[:, :, :, :], Wt[:, :, 0:LAGS, :], LC, q2, q1, LAGS, ALU.subtract, None, first=1)
                    if q > 0:
                        pool.wait(v, f"zl{q - 1}")
                    dve.did(v.tensor_copy(Ec[:, :, 1:2], ph[:, 0, gs].unsqueeze(2)), f"e{q}_0")
                    wd = 1
                    while wd < NCH:
                        step = wd.bit_length()
                        pool.wait(v, f"e{q}_{step - 1}")
                        cw, sw = (x[:, :, wd:wd + 1].to_broadcast([P, NG, wd]) for x in (Ec, Es))
                        tt(e1[:, :, 0:wd], Ec[:, :, 1:wd + 1], cw, ALU.mult)
                        tt(e2[:, :, 0:wd], Es[:, :, 1:wd + 1], sw, ALU.mult, wait=False)
                        tt(Ec[:, :, wd + 1:2 * wd + 1], e1[:, :, 0:wd], e2[:, :, 0:wd], ALU.subtract, f"e{q}_{step}")
                        wd *= 2
                    pe.wait(v, f"K{q}")
                    if q > 0:
                        v.wait_ge(tt_land, 16 * LAGS * q)
                    for bnk in range(2):
                        dve.did(v.tensor_copy(Kt[:, 4 * bnk:4 * bnk + 4].rearrange("c g k n -> c (g k n)"), ps[4 + bnk][0:CH, :]))
                    sh = [CH, NG, CH]
                    dd = Wt[0:CH, :, 0, :]
                    tt(dd, bc(ident[0:CH, 0:CH], sh, 1), bc(D16[:, gs], sh), ALU.mult)
                    tt(Kt[:, :, 0, :], Kt[:, :, 0, :], dd, ALU.add, f"K{q}")
                    pe.wait(v, f"b{q}")
                    pool.wait(v, f"e{q}_7")
                    for bnk in range(2):
                        part = slice(4 * bnk, 4 * bnk + 4)
                        src, turned = (ps[x + bnk][:, :].rearrange("p (g n) -> p g n", g=4) for x in (0, 2))
                        tt(zin[:, part], src, Ec[:, part, 1:NCH + 1], ALU.mult)
                        tt(z2[:, part], turned, Es[:, part, 1:NCH + 1], ALU.mult, f"rot{q}_{bnk}")
                    for x in range(NG):
                        pool.wait(v, f"zin{q}_{x // 4}")
                        dve.did(v.tensor_tensor_scan(zs[:, x, 1:NCH + 1], rho[:, q * NG + x:q * NG + x + 1].to_broadcast([P, NCH]),
                                                     zin[:, x, :], 0.0, ALU.mult, ALU.add), f"scan{q}")
                    tt(Zc[:, :, :], zs[:, :, 0:NCH], Ec[:, :, 0:NCH], ALU.mult)
                    tt(zl[:, 0, gs], zs[:, :, NCH], Ec[:, :, NCH], ALU.mult, f"zc{q}")
        s4a.close()
        if stages == 4:
            return finish_debug(nc, sem, dbg, locals())


        X2 = sb("X2", [P, 9, D])
        combine = sb("combine", [P, 9, 2])
        pos = sb("pos", [P, 9, 2], U32)
        slot_t = sb("slot_t", [1, SLOTS, 3], I32)
        exp_t = sb("exp_t", [1, EXPERTS + 3], I32)
        w_out = sb("w_out", [P, KD, D])
        w_r = sb("w_r", [P, KD, EXPERTS])
        b_r = sb("b_r", [P, EXPERTS])
        land6, rland = sem("land6"), sem("rland")
        s5s = ctx.enter_context(ExitStack())
        t5 = lambda name, shape: s5s.enter_context(nc.sbuf_tensor(name, shape, F32))
        glu_w, glu_b = t5("glu_w", [P, 4, GW]), t5("glu_b", [P, GW])
        G = t5("G", [P, 9, GW])
        gsq = t5("gsq", [P, GW])
        g_land = sem("glu_land")
        pe, act, dve = steps("s5_pe"), steps("s5_act"), steps("s5_dve")
        with nc.Block() as block:
            @block.sync
            def _(sp):
                sp.dma_start(glu_w[:, :, :], A["s5_glu_w"][0].rearrange("(k p) n -> p k n", p=P)).then_inc(g_land, 16)
                sp.dma_start(glu_b[:, :], A["s5_glu_b"][0:1, :].to_broadcast([P, GW])).then_inc(g_land, 16)
                sp.dma_start(w_out[:, :, :], A["w_out"][0].rearrange("(k p) n -> p k n", p=P)).then_inc(land6, 16)
                sp.dma_start(X2[:, 0:NT, :], A["x_prompt"][0].rearrange("(i p) d -> p i d", p=P)).then_inc(land6, 16)
                sp.dma_start(X2[0:DEC, NT, :], A["x_sample"].rearrange("b o d -> (b o) d")).then_inc(land6, 16)
                sp.dma_start(w_r[:, :, :], A["w_router"].rearrange("(k p) e -> p k e", p=P)).then_inc(rland, 16)
                sp.dma_start(b_r[:, :], A["b_router"].unsqueeze(0).to_broadcast([P, EXPERTS])).then_inc(rland, 16)

            @block.tensor
            def _(t):
                for i in range(9):
                    n = P if i < NT else DEC
                    if i >= 2:
                        act.wait(t, f"y1T{i - 2}")
                    for k in range(4):
                        mm = t.transpose(ps[i % 2][:, k * P:k * P + n], Yt[0:n, i, k * P:(k + 1) * P], ident[0:n, 0:n])
                    pe.did(mm, f"y1T{i}")
                t.wait_ge(g_land, 32)
                for i in range(9):
                    n = P if i < NT else DEC
                    act.wait(t, f"y1T{i}")
                    if i >= 2:
                        dve.wait(t, f"G{i - 2}")
                    for k in range(4):
                        mm = t.matmul(ps[2 + i % 2][0:n, :], y1T[:, k, i * P:i * P + n], glu_w[:, k, :], start=(k == 0), stop=(k == 3))
                    pe.did(mm, f"glu{i}")
                for i in range(9):
                    n = P if i < NT else DEC
                    dve.wait(t, f"n{i}")
                    if i >= 2:
                        dve.wait(t, f"oT{i - 2}")
                    for k in range(4):
                        mm = t.transpose(ps[4 + i % 2][:, k * P:k * P + n], Yt[0:n, i, k * P:(k + 1) * P], ident[0:n, 0:n])
                    pe.did(mm, f"oT{i}")

            @block.scalar
            def _(a):
                for i in range(9):
                    n = P if i < NT else DEC
                    pe.wait(a, f"y1T{i}")
                    act.did(a.activation(y1T[:, :, i * P:i * P + n], ps[i % 2][:, :].rearrange("p (k n) -> p k n", k=4)[:, :, 0:n], ACT.Copy), f"y1T{i}")
                for i in range(9):
                    n = P if i < NT else DEC
                    dve.wait(a, f"G{i}")
                    act.did(a.activation(G[0:n, i, :], G[0:n, i, :], ACT.Sigmoid), f"sig{i}")
                for i in range(9):
                    n = P if i < NT else DEC
                    dve.wait(a, f"y{i}")
                    act.drain(a)
                    act.did(a.activation(gsq[0:n, :], Yt[0:n, i, :], ACT.Square, accum_out=small[0:n, i:i + 1]), "ss")
                dve.wait(a, "ms")
                act.did(a.activation(small[:, 10:19], small[:, 10:19], ACT.Sqrt), "rms")

            @block.vector
            def _(v):
                v.wait_ge(g_land, 32)
                for i in range(9):
                    n = P if i < NT else DEC
                    pe.wait(v, f"glu{i}")
                    dve.did(v.tensor_tensor(G[0:n, i, :], ps[2 + i % 2][0:n, :], glu_b[0:n, :], ALU.add), f"G{i}")
                for i in range(9):
                    n = P if i < NT else DEC
                    act.wait(v, f"sig{i}")
                    dve.did(v.tensor_tensor(Yt[0:n, i, :], Yt[0:n, i, :], G[0:n, i, :], ALU.mult), f"y{i}")
                act.wait(v, "ss")
                dve.did(v.tensor_scalar(small[:, 10:19], small[:, 0:9], 1.0 / GW, EPS, ALU.mult, ALU.add), "ms")
                act.wait(v, "rms")
                dve.did(v.reciprocal(small[:, 20:29], small[:, 10:19]))
                dve.drain(v)
                for i in range(9):
                    n = P if i < NT else DEC
                    dve.did(v.tensor_scalar(Yt[0:n, i, :], Yt[0:n, i, :], small[0:n, 20 + i:21 + i], None, ALU.mult), f"n{i}")
                for i in range(9):
                    n = P if i < NT else DEC
                    pe.wait(v, f"oT{i}")
                    dst = hT[:, 4:8, i:SEQ:LAGS] if i < NT else hT[:, 4:8, SEQ:T]
                    dve.did(v.tensor_tensor(dst, ps[4 + i % 2][:, :].rearrange("p (k n) -> p k n", k=4)[:, :, 0:n],
                                            bc(vecT[:, SNG:SNG + 4], [P, 4, n]), ALU.mult), f"oT{i}")
        s5s.close()
        if stages == 5:
            return finish_debug(nc, sem, dbg, {**locals(), "mixT": hT})

        s6 = ctx.enter_context(ExitStack())
        t6 = lambda name, shape, dt=F32: s6.enter_context(nc.sbuf_tensor(name, shape, dt))
        H2 = t6("H2", [P, 9, D])
        rowsP = V[:, :, :, :].rearrange("p g k c -> p (g k c)")[:, 0:3 * D].rearrange("p (n d) -> p n d", n=3)
        rowsD = Yt[0:DEC, :, :].rearrange("p i n -> p (i n)")[:, 0:3 * D].rearrange("p (n d) -> p n d", n=3)
        A2 = t6("A2", [P, KD, 9])
        h2T = V[:, :, :, :].rearrange("p g k c -> p (g k c)")[:, 3 * D:4 * D].rearrange("p (k n) -> p k n", k=KD)
        EE = [P, 9, EXPERTS]
        wgu = w_out[:, :, :].rearrange("p k n -> p (k n)").rearrange("p (b k n) -> p b k n", b=2, k=KD)
        wdn = y1T[:, :, :].rearrange("p k n -> p (k n)")[:, 0:4 * D].rearrange("p (b k n) -> p b k n", b=2, k=2)
        wg_v = A["w_gate"][0].rearrange("e (k p) f -> e p k f", p=P)
        wu_v = A["w_up"][0].rearrange("e (k p) f -> e p k f", p=P)
        wd_v = A["w_down"][0].rearrange("e (k p) d -> e p k d", p=P)
        gu_in, dn_in = ([sem(f"{n}_even"), sem(f"{n}_odd")] for n in ("gate_up_land", "down_land"))

        def load_gate_up(sp, e, b):
            for dst, src in ((wgu[:, b, :, 0:FE], wg_v), (wgu[:, b, :, FE:2 * FE], wu_v)):
                sp.dma_start(dst, src[bass.ds(e, 1)].rearrange("o p k f -> (o p) k f")).then_inc(gu_in[b], 16)

        def load_down(sp, e, b):
            sp.dma_start(wdn[:, b], wd_v[bass.ds(e, 1)].rearrange("o p k d -> (o p) k d")).then_inc(dn_in[b], 16)
        lg = t6("lg", EE)
        sel, m1, oh1, oh2, tmp = (t6(n, EE) for n in ("sel", "m1", "oh1", "oh2", "tmp"))
        g4 = t6("g4", [P, 6, 36])
        col = t6("col", [P, 8, 9])
        rank_e = t6("rank_e", [P, 16])
        sidx = t6("sidx", [P, SLOTS, EXPERTS])
        cmp_ = t6("cmp_", [P, SLOTS, EXPERTS])
        cnt = t6("cnt", EE)
        ex = t6("ex", [P, 4, EXPERTS])
        valid = t6("valid", [P, 1])
        upx = t6("upx", [P, P])
        ones_m = t6("ones_m", [P, P])
        scat = sem("scat")
        pe, act, dve, pool = steps("s6_pe"), steps("s6_act"), steps("s6_dve"), steps("s6_pool")
        GT1, SH2, SC2, GT2 = 16, 24, 32, 40

        with nc.Block() as block:
            @block.sync
            def _(sp):
                pe.wait(sp, "mix8_1")
                for e in range(2):
                    load_gate_up(sp, e, e)
                    load_down(sp, e, e)

            @block.gpsimd
            def _(g):
                pool.did(g.memset(upx[:, :], 1.0))
                pool.did(g.memset(ones_m[:, :], 1.0))
                pool.did(g.memset(lg[:, :, :], 0.0))
                pool.did(g.memset(valid[:, :], 0.0))
                pool.drain(g)
                pool.did(g.memset(valid[0:DEC, :], 1.0))
                for e in range(16):
                    pool.did(g.memset(rank_e[:, e:e + 1], float(16 - e)))
                pool.did(g.iota(sidx[:, :, :], pattern=[[1, SLOTS], [0, EXPERTS]], base=0, channel_multiplier=0,
                                allow_small_or_imprecise_dtypes=True))
                pool.drain(g)
                pool.did(g.affine_select(out=upx[:, :], in_=upx[:, :], compare_op=ALU.is_gt, fill=0.0, base=0,
                                         pattern=[[1, P]], channel_multiplier=-1), "consts")
                dve.wait(g, "pos")
                g.wait_ge(zland, 16 * (SLOTS // 2 + 2))
                for i in range(9):
                    n = P if i < NT else DEC
                    for j in range(2):
                        g.indirect_dma_start(xs_d, bass.IndirectOffsetOnAxis(ap=pos[0:n, i, j:j + 1], axis=0), H2[0:n, i, :], None).then_inc(scat, 16)
                g.wait_ge(scat, 16 * 18)

            def route_T(t, i):
                n = P if i < NT else DEC
                dve.wait(t, f"H2_{i}")
                if i >= 1:
                    act.wait(t, f"h2T{i - 1}")
                for k in range(KD):
                    mm = t.transpose(ps[4 + k // 4][:, (k % 4) * P:(k % 4) * P + n], H2[0:n, i, k * P:(k + 1) * P], ident[0:n, 0:n])
                pe.did(mm, f"h2T{i}")

            def route(t, i):
                n = P if i < NT else DEC
                act.wait(t, f"h2T{i}")
                if i >= 1:
                    dve.wait(t, f"lg{i - 1}")
                for k in range(KD):
                    mm = t.matmul(ps[6][0:n, 0:EXPERTS], h2T[:, k, 0:n], w_r[:, k, :], start=(k == 0), stop=(k == KD - 1))
                pe.did(mm, f"lg{i}")

            @block.tensor
            def _(t):
                dve.wait(t, "A2")
                for n, base in enumerate((GT1, None, SH2)):
                    for half_ in range(2):
                        b = 2 * n + half_
                        for k in range(4 * half_, 4 * half_ + 4):
                            src = A2[:, k, :] if base is None else modT[:, base + k, :]
                            mm = t.matmul(ps[b % 4][:, (k % 4) * P:(k % 4 + 1) * P], src[:, 0:1].to_broadcast([P, P]), ident[:, :], start=True, stop=True)
                        for k in range(4 * half_, 4 * half_ + 4):
                            src = A2[:, k, :] if base is None else modT[:, base + k, :]
                            mm = t.matmul(ps[4 + b % 4][0:DEC, (k % 4) * P:(k % 4 + 1) * P], src[:, 1:9], ident[:, :], start=True, stop=True)
                        pe.did(mm, f"row{b}")
                        if b >= 3:
                            act.wait(t, f"row{b - 3}")
                act.wait(t, "row5")
                t.wait_ge(land6, 48)
                t.wait_ge(rland, 32)
                for i in range(9):
                    n = P if i < NT else DEC
                    for half_ in range(2):
                        b = 2 * (i % 2) + half_
                        if i >= 2:
                            dve.wait(t, f"mix{i - 2}_{half_}")
                        for k in range(KD):
                            mm = t.matmul(ps[b][0:n, :], hT[:, k, i * P:i * P + n], w_out[:, k, half_ * 512:(half_ + 1) * 512], start=(k == 0), stop=(k == KD - 1))
                        pe.did(mm, f"mix{i}_{half_}")
                        if half_ == 0 and i >= 2:
                            route(t, i - 2)
                    if i >= 1:
                        route_T(t, i - 1)
                route(t, 7)
                route_T(t, 8)
                route(t, 8)
                dve.wait(t, "oh")
                t.matmul(ps[4][:, 0:144], upx[:, :], cnt[:, :, :].rearrange("p i e -> p (i e)"), start=True, stop=True)
                pe.did(t.matmul(ps[5][:, 0:144], ones_m[:, :], cnt[:, :, :].rearrange("p i e -> p (i e)"), start=True, stop=True), "cnt")

            @block.scalar
            def _(a):
                for b in range(6):
                    n, half_ = b // 2, b % 2
                    pe.wait(a, f"row{b}")
                    act.did(a.activation(rowsP[:, n, half_ * 512:(half_ + 1) * 512], ps[b % 4][:, :], ACT.Copy))
                    act.did(a.activation(rowsD[:, n, half_ * 512:(half_ + 1) * 512], ps[4 + b % 4][0:DEC, :], ACT.Copy), f"row{b}")
                def route_copy(i):
                    n = P if i < NT else DEC
                    pe.wait(a, f"h2T{i}")
                    if i >= 1:
                        pe.wait(a, f"lg{i - 1}")
                    for half_ in range(2):
                        act.did(a.activation(h2T[:, 4 * half_:4 * half_ + 4, 0:n],
                                             ps[4 + half_][:, :].rearrange("p (k n) -> p k n", k=4)[:, :, 0:n], ACT.Copy), f"h2T{i}")

                for i in range(9):
                    n = P if i < NT else DEC
                    if i >= 2:
                        route_copy(i - 2)
                    dve.wait(a, f"x1_{i}")
                    act.did(a.activation(H2[0:n, i, :], X2[0:n, i, :], ACT.Square, accum_out=small[0:n, i:i + 1]), f"ss{i}")
                    dve.wait(a, f"ms{i}")
                    act.did(a.activation(small[0:n, 10 + i:11 + i], small[0:n, 10 + i:11 + i], ACT.Sqrt), f"rms{i}")
                route_copy(7)
                route_copy(8)
                dve.wait(a, "lg8")
                act.did(a.activation(lg[:, :, :], lg[:, :, :], ACT.Sigmoid), "scores")

            @block.vector
            def _(v):
                def tt(out, x, y, op, name=None):
                    dve.drain(v)
                    dve.did(v.tensor_tensor(out, x, y, op), name)

                dve.did(v.tensor_scalar(A2[:, :, :], modT[:, SC2:SC2 + 8, :], 1.0, None, ALU.add))
                tt(A2[:, :, :], A2[:, :, :], bc(vecT[:, N2G:N2G + 8], [P, 8, 9]), ALU.mult, "A2")
                act.wait(v, "row5")
                v.wait_ge(land6, 48)
                pool.wait(v, "consts")
                def copy_lg(i):
                    n = P if i < NT else DEC
                    pe.wait(v, f"lg{i}")
                    dve.did(v.tensor_copy(lg[0:n, i, :], ps[6][0:n, 0:EXPERTS]), f"lg{i}")

                for i in range(9):
                    if i < 9:
                        n = P if i < NT else DEC
                        row = rowsP if i < NT else rowsD
                        for half_ in range(2):
                            b, c0 = 2 * (i % 2) + half_, half_ * 512
                            if half_ == 1 and i >= 2:
                                copy_lg(i - 2)
                            pe.wait(v, f"mix{i}_{half_}")
                            dve.did(v.tensor_tensor(H2[0:n, i, c0:c0 + 512], ps[b][0:n, :], row[0:n, 0, c0:c0 + 512], ALU.mult), f"mix{i}_{half_}")
                        tt(X2[0:n, i, :], X2[0:n, i, :], H2[0:n, i, :], ALU.add, f"x1_{i}")
                        act.wait(v, f"ss{i}")
                        dve.did(v.tensor_scalar(small[0:n, 10 + i:11 + i], small[0:n, i:i + 1], 1.0 / D, EPS, ALU.mult, ALU.add), f"ms{i}")
                        act.wait(v, f"rms{i}")
                        dve.did(v.reciprocal(small[0:n, 20 + i:21 + i], small[0:n, 10 + i:11 + i]))
                        dve.drain(v)
                        dve.did(v.scalar_tensor_tensor(out=H2[0:n, i, :], in0=X2[0:n, i, :], scalar=small[0:n, 20 + i:21 + i], in1=row[0:n, 1, :],
                                                       op0=ALU.mult, op1=ALU.mult))
                        tt(H2[0:n, i, :], H2[0:n, i, :], row[0:n, 2, :], ALU.add, f"H2_{i}")
                for i in (7, 8):
                    copy_lg(i)
                act.wait(v, "scores")
                b4 = lambda c: c.unsqueeze(2).to_broadcast(EE)
                tt(sel[:, :, :], lg[:, :, :], bc(b_r[:, :], EE, 1), ALU.add)
                q4 = sel[:, :, :].rearrange("p i (g r) -> p (i g) r", r=4)
                for n, (x, y) in enumerate(((0, 1), (0, 2), (0, 3), (1, 2), (1, 3), (2, 3))):
                    tt(g4[:, n, :], q4[:, :, x], q4[:, :, y], ALU.add)
                for n in range(1, 6):
                    tt(g4[:, 0, :], g4[:, 0, :], g4[:, n, :], ALU.max)
                gs_ = g4[:, 0, :].rearrange("p (i g) -> p i g", g=4)
                g4s = [P, 9, 4]
                dve.drain(v)
                dve.did(v.tensor_reduce(col[:, 0, :], gs_, AX.X, ALU.max))
                v1, v2 = (g4[:, n, :].rearrange("p (i g) -> p i g", g=4) for n in (1, 2))
                tt(v1, gs_, bc(col[:, 0, :], g4s), ALU.is_equal)
                tt(v1, v1, bc(rank_e[:, 12:16], g4s, 1), ALU.mult)
                dve.drain(v)
                dve.did(v.tensor_reduce(col[:, 0, :], v1, AX.X, ALU.max))
                tt(v2, v1, bc(col[:, 0, :], g4s), ALU.is_equal)
                ing = v2.rearrange("p i g -> p (i g)").unsqueeze(2).to_broadcast([P, 36, 4])
                t4_ = tmp[:, :, :].rearrange("p i (g r) -> p (i g) r", r=4)
                s4_ = sel[:, :, :].rearrange("p i (g r) -> p (i g) r", r=4)
                tt(s4_, q4, ing, ALU.mult)
                dve.drain(v)
                dve.did(v.tensor_scalar(v1, v2, 1e30, -1e30, ALU.mult, ALU.add))
                tt(s4_, s4_, v1.rearrange("p i g -> p (i g)").unsqueeze(2).to_broadcast([P, 36, 4]), ALU.add)

                def first_max(oh):
                    dve.drain(v)
                    dve.did(v.tensor_reduce(col[:, 1, :], sel[:, :, :], AX.X, ALU.max))
                    tt(m1[:, :, :], sel[:, :, :], b4(col[:, 1, :]), ALU.is_equal)
                    tt(m1[:, :, :], m1[:, :, :], bc(rank_e[:, :], EE, 1), ALU.mult)
                    dve.drain(v)
                    dve.did(v.tensor_reduce(col[:, 1, :], m1[:, :, :], AX.X, ALU.max))
                    tt(oh[:, :, :], m1[:, :, :], b4(col[:, 1, :]), ALU.is_equal)

                first_max(oh1)
                dve.drain(v)
                dve.did(v.scalar_tensor_tensor(out=sel[:, :, :].rearrange("p i e -> p (i e)"), in0=oh1[:, :, :].rearrange("p i e -> p (i e)"), scalar=-2e30,
                                               in1=sel[:, :, :].rearrange("p i e -> p (i e)"), op0=ALU.mult, op1=ALU.add))
                first_max(oh2)
                tt(cnt[:, :, :], oh1[:, :, :], oh2[:, :, :], ALU.add)
                dve.drain(v)
                dve.did(v.tensor_scalar(cnt[:, NT, :], cnt[:, NT, :], valid[:, :], None, ALU.mult), "oh")
                for n, oh in enumerate((oh1, oh2)):
                    tt(tmp[:, :, :], oh[:, :, :], lg[:, :, :], ALU.mult)
                    dve.drain(v)
                    dve.did(v.tensor_reduce(col[:, 2 + n, :], tmp[:, :, :], AX.X, ALU.add))
                tt(col[:, 4, :], col[:, 2, :], col[:, 3, :], ALU.add)
                dve.drain(v)
                dve.did(v.reciprocal(col[:, 4, :], col[:, 4, :]))
                for n in range(2):
                    tt(combine[:, :, n], col[:, 2 + n, :], col[:, 4, :], ALU.mult)
                pe.wait(v, "cnt")
                tot = m1
                dve.did(v.tensor_copy(tot[:, :, :].rearrange("p i e -> p (i e)"), ps[5][:, 0:144]))
                dve.did(v.tensor_copy(sel[:, :, :].rearrange("p i e -> p (i e)"), ps[4][:, 0:144]))
                dve.drain(v)
                dve.did(v.tensor_copy(ex[:, 0, :], tot[:, 0, :]))
                for i in range(1, 9):
                    tt(sel[:, i, :], sel[:, i, :], ex[:, 0, :], ALU.add)
                    tt(ex[:, 0, :], ex[:, 0, :], tot[:, i, :], ALU.add)
                dve.drain(v)
                dve.did(v.tensor_scalar(ex[:, 0, :], ex[:, 0, :], 1.0 / P, 127.0 / P - 127.0 / 256, ALU.mult, ALU.add))
                dve.drain(v)
                dve.did(v.tensor_scalar(ex[:, 0, :], ex[:, 0, :], ROUND, -ROUND, ALU.add, ALU.add))
                dve.drain(v)
                dve.did(v.tensor_scalar(ex[:, 0, :], ex[:, 0, :], 1.0, None, ALU.max))
                dve.did(v.memset(ex[:, 3, :], 1.0))
                dve.drain(v)
                dve.did(v.tensor_tensor_scan(ex[:, 1, :], ex[:, 3, :], ex[:, 0, :], 0.0, ALU.mult, ALU.add))
                tt(ex[:, 2, :], ex[:, 1, :], ex[:, 0, :], ALU.subtract)
                dve.drain(v)
                dve.did(v.tensor_copy(exp_t[:, 0:EXPERTS], ex[0:1, 2, :]))
                dve.drain(v)
                dve.did(v.tensor_scalar(ex[:, 2, :], ex[:, 2, :], float(P), None, ALU.mult))
                tt(sel[:, :, :], sel[:, :, :], bc(ex[:, 2, :], EE, 1), ALU.add)
                for n, oh in enumerate((oh1, oh2)):
                    tt(tmp[:, :, :], oh[:, :, :], sel[:, :, :], ALU.mult)
                    dve.drain(v)
                    dve.did(v.tensor_reduce(col[:, 5 + n, :], tmp[:, :, :], AX.X, ALU.add))
                dve.drain(v)
                dve.did(v.tensor_copy(pos[:, :, :], col[:, 5:7, :].rearrange("p n i -> p i n")), "pos")
                tt(cmp_[:, :, :], bc(ex[:, 1, :], [P, SLOTS, EXPERTS], 1), sidx[:, :, :], ALU.is_le)
                dve.drain(v)
                dve.did(v.tensor_reduce(sidx[:, :, 0], cmp_[:, :, :], AX.X, ALU.add))
                dve.drain(v)
                dve.did(v.tensor_scalar(sidx[:, :, 0], sidx[:, :, 0], float(EXPERTS - 1), None, ALU.min))
                dve.drain(v)
                e_, half_e, par = (x[0:1, :, 0:1] for x in (sidx, cmp_, sidx[:, :, 1:2]))

                def ts(out, x, c1, c2):
                    dve.drain(v)
                    dve.did(v.tensor_scalar(out, x, c1, c2, ALU.mult, ALU.add))
                ts(half_e, e_, 0.5, -0.25)
                dve.drain(v)
                dve.did(v.tensor_scalar(half_e, half_e, ROUND, -ROUND, ALU.add, ALU.add))
                dve.drain(v)
                dve.did(v.scalar_tensor_tensor(out=par, in0=half_e, scalar=-2.0, in1=e_, op0=ALU.mult, op1=ALU.add))
                tt(e_, half_e, par, ALU.add)
                dve.drain(v)
                dve.did(v.tensor_copy(slot_t[:, :, 0:1], par))
                ts(slot_t[:, :, 1:2], half_e, 16.0, 16.0)
                dve.drain(v)
                dve.did(v.tensor_scalar(e_, e_, 1.0, 16.0, ALU.max, ALU.mult))
                dve.drain(v)
                dve.did(v.tensor_copy(slot_t[:, :, 2:3], e_))
                ts(ex[0:1, 3, 0:1], ex[0:1, 1, EXPERTS - 1:EXPERTS], 0.5, 0.25)
                dve.drain(v)
                dve.did(v.tensor_scalar(ex[0:1, 3, 0:1], ex[0:1, 3, 0:1], ROUND, -ROUND, ALU.add, ALU.add))
                dve.drain(v)
                dve.did(v.tensor_copy(exp_t[:, EXPERTS:EXPERTS + 1], ex[0:1, 3, 0:1]))
                ts(exp_t[:, EXPERTS + 1:EXPERTS + 2], ex[0:1, 3, 0:1], 1.0, -1.0)
                ts(exp_t[:, EXPERTS + 2:EXPERTS + 3], ex[0:1, 3, 0:1], 2.0, -1.0)
                dve.at["slots"] = dve.n
        s6.close()
        if stages == 6:
            return finish_debug(nc, sem, dbg, {**locals(), "X": X2})

        s7 = ctx.enter_context(ExitStack())
        t7 = lambda name, shape: s7.enter_context(nc.sbuf_tensor(name, shape, F32))
        xin = [t7(f"xin{p}", [P, D]) for p in range(2)]
        xT = [t7(f"xT{p}", [P, KD, P]) for p in range(2)]
        sg = [t7(f"sg{p}", [P, FE]) for p in range(2)]
        hh_ = [t7(f"hh{p}", [P, FE]) for p in range(2)]
        aT = [t7(f"aT{p}", [P, 2, P]) for p in range(2)]
        yo = [t7(f"yo{p}", [P, D]) for p in range(2)]
        x_in, y_out = ([sem(f"{n}{p}") for p in range(2)] for n in ("x_in", "y_out"))
        y_half, xT_half = sem("y_half"), sem("xT_half")
        xT_ps, xT_sb, gu_ps, silu_sb, h_sb, aT_ps, aT_sb, dn_ps, y_sb = (sem(n) for n in (
            "xT_ps", "xT_sb", "gu_ps", "silu_sb", "h_sb", "aT_ps", "aT_sb", "dn_ps", "y_sb"))
        xs_v = ys_v = xs_d.rearrange("(s p) d -> s p d", p=P)
        PAIRS = SLOTS // 2

        def pairs(eng, body, tail=None):
            used = eng.value_load(exp_t[0:1, EXPERTS:EXPERTS + 1], min_val=EXPERTS // 2, max_val=PAIRS)
            body(0)
            with eng.Fori(1, PAIRS) as it:
                with eng.If(it < used):
                    body(it)
            if tail is not None:
                tail(*(eng.value_load(exp_t[0:1, EXPERTS + n:EXPERTS + n + 1], min_val=n * EXPERTS // 2 - 1, max_val=n * PAIRS - 1) for n in (1, 2)))

        with nc.Block() as block:
            @block.sync
            def _(sp):
                with sp.Fori(1, EXPERTS // 2) as it:
                    for b in range(2):
                        done = sp.value_load(exp_t[0:1, bass.ds(it * 2 + (b - 1), 1)], min_val=1, max_val=SLOTS)
                        sp.wait_ge(gu_ps, done)
                        load_gate_up(sp, it * 2 + b, b)
                        sp.wait_ge(dn_ps, done)
                        load_down(sp, it * 2 + b, b)

            @block.gpsimd
            def _(g):
                def load(s, p):
                    g.dma_start(xin[p][:, :], xs_v[bass.ds(s, 1)].rearrange("o p d -> p (o d)")).then_inc(x_in[p], 16)

                def body(it):
                    if isinstance(it, int):
                        load(1, 1)
                    else:
                        g.wait_ge(xT_ps, it * 2)
                        load(it * 2 + 1, 1)
                    g.wait_ge(xT_ps, it * 2 + 1)
                    load(it * 2 + 2, 0)
                load(0, 0)
                pairs(g, body)

            @block.tensor
            def _(t):
                def buffer(s):
                    return (t.value_load(slot_t[0:1, bass.ds(s, 1), 0], min_val=0, max_val=1),
                            *(t.value_load(slot_t[0:1, bass.ds(s, 1), n], min_val=0, max_val=16 * EXPERTS // 2) for n in (1, 2)))

                def transposes(it, p, s):
                    t.wait_ge(x_in[p], (it + 1) * 16)
                    if not (isinstance(s, int) and s == 0):
                        t.wait_ge(xT_sb, s)
                    for k in range(KD):
                        mm = t.transpose(ps[k // 4][:, (k % 4) * P:(k % 4 + 1) * P], xin[p][:, k * P:(k + 1) * P], ident[:, :])
                    mm.then_inc(xT_ps, 1)

                def act_transposes(p, s):
                    t.wait_ge(h_sb, s + 1)
                    for k in range(2):
                        mm = t.transpose(ps[4][:, k * P:(k + 1) * P], hh_[p][:, k * P:(k + 1) * P], ident[:, :])
                    mm.then_inc(aT_ps, 1)

                def down(p, s):
                    buf, even, odd = buffer(s)
                    t.wait_ge(aT_sb, s + 1)
                    t.wait_ge(dn_in[0], even)
                    t.wait_ge(dn_in[1], odd)
                    if not (isinstance(s, int) and s == 0):
                        t.wait_ge(y_sb, s)
                    for half_ in range(2):
                        for k in range(2):
                            mm = t.matmul(ps[5 + half_][:, :], aT[p][:, k, :],
                                          wdn[:, bass.ds(buf, 1), k, half_ * 512:(half_ + 1) * 512].rearrange("p o n -> p (o n)"),
                                          start=(k == 0), stop=(k == 1))
                    mm.then_inc(dn_ps, 1)

                def body(it):
                    for p in range(2):
                        s = it * 2 + p
                        static = isinstance(it, int)
                        buf, even, odd = buffer(s)
                        t.wait_ge(xT_sb, s + 1)
                        t.wait_ge(gu_in[0], even * 2)
                        t.wait_ge(gu_in[1], odd * 2)
                        if not (static and s < 2):
                            t.wait_ge(h_sb, s - 1)
                        for k in range(KD):
                            mm = t.matmul(ps[2 + p][:, :], xT[p][:, k, :], wgu[:, bass.ds(buf, 1), k, :].rearrange("p o n -> p (o n)"),
                                          start=(k == 0), stop=(k == KD - 1))
                        mm.then_inc(gu_ps, 1)
                        if not (static and s == 0):
                            act_transposes(1 - p, s - 1)
                        transposes(it + p, 1 - p, s + 1)
                        if not (static and s == 0):
                            down(1 - p, s - 1)

                def tail(it, s):
                    act_transposes(1, s)
                    down(1, s)
                transposes(0, 0, 0)
                pairs(t, body, tail)

            @block.scalar
            def _(a):
                def out(it, p, s):
                    a.wait_ge(dn_ps, s + 1)
                    if not (isinstance(it, int) and it == 0):
                        a.wait_ge(y_out[p], it * 16)
                    a.activation(yo[p][:, 0:512], ps[5][:, :], ACT.Copy).then_inc(y_half, 1)
                    a.activation(yo[p][:, 512:D], ps[6][:, :], ACT.Copy).then_inc(y_sb, 1)
                    a.wait_ge(y_half, s + 1)
                    a.wait_ge(y_sb, s + 1)
                    a.dma_start(ys_v[bass.ds(s, 1)].rearrange("o p d -> (o p) d"), yo[p][:, :]).then_inc(y_out[p], 16)

                def body(it):
                    for p in range(2):
                        s = it * 2 + p
                        static = isinstance(it, int)
                        a.wait_ge(gu_ps, s + 1)
                        if not (static and s < 2):
                            a.wait_ge(h_sb, s - 1)
                        a.activation(sg[p][:, :], ps[2 + p][:, 0:FE], ACT.Silu).then_inc(silu_sb, 1)
                        if not (static and s == 0):
                            out(it - 1 + p, 1 - p, s - 1)

                def tail(it, s):
                    out(it, 1, s)
                    for p in range(2):
                        a.wait_ge(y_out[p], it * 16 + 16)
                        a.activation(sg[p][:, 0:1], sg[p][:, 0:1], ACT.Copy).then_inc(silu_sb, 1)
                pairs(a, body, tail)

            @block.vector
            def _(v):
                def x_copy(p, s):
                    v.wait_ge(xT_ps, s + 1)
                    if not (isinstance(s, int) and s < 2):
                        v.wait_ge(gu_ps, s - 1)
                    v.tensor_copy(xT[p][:, 0:4, :].rearrange("p k n -> p (k n)"), ps[0][:, :]).then_inc(xT_half, 1)
                    v.wait_ge(xT_half, s + 1)
                    v.tensor_copy(xT[p][:, 4:8, :].rearrange("p k n -> p (k n)"), ps[1][:, :]).then_inc(xT_sb, 1)

                def body(it):
                    for p in range(2):
                        s = it * 2 + p
                        static = isinstance(it, int)
                        v.wait_ge(silu_sb, s + 1)
                        if not (static and s < 2):
                            v.wait_ge(aT_ps, s - 1)
                        v.tensor_tensor(hh_[p][:, :], sg[p][:, :], ps[2 + p][:, FE:2 * FE], ALU.mult).then_inc(h_sb, 1)
                        if not (static and s == 0):
                            a_copy(1 - p, s - 1, None if static and s < 3 else s - 2)
                        x_copy(1 - p, s + 1)

                def a_copy(p, s, down_done):
                    v.wait_ge(aT_ps, s + 1)
                    if down_done is not None:
                        v.wait_ge(dn_ps, down_done)
                    v.tensor_copy(aT[p][:, :, :].rearrange("p k n -> p (k n)"), ps[4][:, 0:FE]).then_inc(aT_sb, 1)

                x_copy(0, 0)
                pairs(v, body, lambda it, s: a_copy(1, s, it * 2))
        s7.close()

        s8 = ctx.enter_context(ExitStack())
        t8 = lambda name, shape: s8.enter_context(nc.sbuf_tensor(name, shape, F32))
        gt2P, gt2D, fg = t8("gt2P", [P, D]), Yt[0:DEC, 0:2, :].rearrange("p i n -> p (i n)"), t8("fg", [P, D])
        ya = t8("ya", [P, 3, 2, D])
        sq8 = t8("sq8", [P, 2, D])
        yn = V[:, :, :, :].rearrange("p g k c -> p (g k c)")[:, 0:2 * D].rearrange("p (b d) -> p b d", b=2)
        fland, ygot, y_fin = sem("fland"), [sem(f"ygot{n}") for n in range(3)], [sem(f"y_fin{n}") for n in range(2)]
        pe, act, dve = steps("s8_pe"), steps("s8_act"), steps("s8_dve")
        with nc.Block() as block:
            @block.sync
            def _(sp):
                sp.dma_start(fg[:, :], A["final_g"].unsqueeze(0).to_broadcast([P, D])).then_inc(fland, 16)
                for i in range(9):
                    dve.wait(sp, f"yn{i}")
                    if i < NT:
                        sp.dma_start(O["y_p"][0, i * P:(i + 1) * P, :], yn[:, i % 2, :]).then_inc(y_fin[i % 2], 16)
                    else:
                        sp.dma_start(O["y_s"][:, 0, :], yn[0:DEC, i % 2, :]).then_inc(y_fin[i % 2], 16)
                sp.wait_ge(y_fin[0], 16 * 5)
                sp.wait_ge(y_fin[1], 16 * 4)

            @block.gpsimd
            def _(g):
                for i in range(9):
                    n = P if i < NT else DEC
                    if i >= 3:
                        dve.wait(g, f"c{i - 3}")
                    for j in range(2):
                        g.indirect_dma_start(ya[0:n, i % 3, j, :], None, ys_d, bass.IndirectOffsetOnAxis(ap=pos[0:n, i, j:j + 1], axis=0)).then_inc(ygot[i % 3], 16)

            @block.tensor
            def _(t):
                for half_ in range(2):
                    for k in range(4):
                        mm = t.matmul(ps[half_][:, k * P:(k + 1) * P], modT[:, GT2 + 4 * half_ + k, 0:1].to_broadcast([P, P]), ident[:, :], start=True, stop=True)
                        mm = t.matmul(ps[2 + half_][0:DEC, k * P:(k + 1) * P], modT[:, GT2 + 4 * half_ + k, 1:9], ident[:, :], start=True, stop=True)
                pe.did(mm, "gt2")

            @block.scalar
            def _(a):
                pe.wait(a, "gt2")
                for half_ in range(2):
                    c = slice(half_ * 512, (half_ + 1) * 512)
                    act.did(a.activation(gt2P[:, c], ps[half_][:, :], ACT.Copy))
                    act.did(a.activation(gt2D[:, c], ps[2 + half_][0:DEC, :], ACT.Copy), "gt2")
                for i in range(9):
                    n = P if i < NT else DEC
                    dve.wait(a, f"x{i}")
                    act.drain(a)
                    act.did(a.activation(sq8[0:n, 1, :], X2[0:n, i, :], ACT.Square, accum_out=small[0:n, i:i + 1]), f"ss{i}")
                    dve.wait(a, f"ms{i}")
                    act.did(a.activation(small[0:n, 10 + i:11 + i], small[0:n, 10 + i:11 + i], ACT.Sqrt), f"rms{i}")

            @block.vector
            def _(v):
                act.wait(v, "gt2")
                v.wait_ge(fland, 16)
                for i in range(10):
                    if i < 9:
                        n = P if i < NT else DEC
                        gt = gt2P if i < NT else gt2D
                        v.wait_ge(ygot[i % 3], 32 * (i // 3 + 1))
                        y0, y1 = ya[0:n, i % 3, 0, :], ya[0:n, i % 3, 1, :]
                        dve.drain(v)
                        dve.did(v.tensor_scalar(sq8[0:n, 0, :], y0, combine[0:n, i, 0:1], None, ALU.mult))
                        dve.drain(v)
                        dve.did(v.scalar_tensor_tensor(out=sq8[0:n, 0, :], in0=y1, scalar=combine[0:n, i, 1:2], in1=sq8[0:n, 0, :], op0=ALU.mult, op1=ALU.add), f"c{i}")
                        dve.drain(v)
                        dve.did(v.tensor_tensor(sq8[0:n, 0, :], sq8[0:n, 0, :], gt[0:n, :], ALU.mult))
                        dve.drain(v)
                        dve.did(v.tensor_tensor(X2[0:n, i, :], X2[0:n, i, :], sq8[0:n, 0, :], ALU.add), f"x{i}")
                        act.wait(v, f"ss{i}")
                        dve.did(v.tensor_scalar(small[0:n, 10 + i:11 + i], small[0:n, i:i + 1], 1.0 / D, EPS, ALU.mult, ALU.add), f"ms{i}")
                    if i >= 1:
                        i -= 1
                        n = P if i < NT else DEC
                        act.wait(v, f"rms{i}")
                        dve.did(v.reciprocal(small[0:n, 20 + i:21 + i], small[0:n, 10 + i:11 + i]))
                        dve.drain(v)
                        if i >= 2:
                            v.wait_ge(y_fin[i % 2], 16 * (i // 2))
                        dve.did(v.scalar_tensor_tensor(out=yn[0:n, i % 2, :], in0=X2[0:n, i, :], scalar=small[0:n, 20 + i:21 + i], in1=fg[0:n, :],
                                                       op0=ALU.mult, op1=ALU.mult), f"yn{i}")


def finish_debug(nc, sem, dbg, env):
    s = sem("dbg")
    with nc.Block() as block:
        @block.sync
        def _(sp):
            n = 0
            for name, out in dbg.items():
                src = env[name]
                idx = tuple(slice(None) for _ in src.shape)
                sp.dma_start(out, src[idx]).then_inc(s, 16)
                n += 16
            sp.wait_ge(s, n)


_INS = ["x_prompt", "x_sample", "c_prompt", "c_sample", "state_conv", "state_gdn", "state_s5_re", "state_s5_im",
        "norm1_g", "norm2_g", "w_ada", "b_ada", "w_in", "conv_w", "a_log", "dt_bias", "gdn_norm_g",
        "s5_lambda_re", "s5_lambda_im", "s5_log_dt", "s5_b_re", "s5_b_im", "s5_c_re", "s5_c_im", "s5_d",
        "s5_glu_w", "s5_glu_b", "s5_norm_g", "w_out", "w_router", "b_router", "w_gate", "w_up", "w_down", "final_g"]
_OUTS = [("y_p", (1, SEQ, D)), ("y_s", (DEC, 1, D)), ("conv_p", (1, 1, CW - 1, QKV)), ("gdn_p", (1, 1, HEADS, P, P)),
         ("re_p", (1, 1, GROUPS, ST)), ("im_p", (1, 1, GROUPS, ST)), ("conv_s", (1, DEC, CW - 1, QKV)),
         ("gdn_s", (1, DEC, HEADS, P, P)), ("re_s", (1, DEC, GROUPS, ST)), ("im_s", (1, DEC, GROUPS, ST))]


def program(new_core, shapes):
    marks = {}
    for _ in range(2):
        nc = new_core()
        A = {n: nc.dram_tensor("in_" + n, shape, F32, kind="ExternalInput").ap() for n, shape in shapes}
        O = {n: nc.dram_tensor("out_" + n, shape, F32, kind="ExternalOutput").ap() for n, shape in _OUTS}
        emit(nc, A, O, marks)
    return nc


def kernel(**inputs):
    import numpy as np
    import concourse.bacc as bacc
    from concourse.bass_utils import run_bass_kernel_spmd

    arrays = {"in_" + n: np.ascontiguousarray(inputs[n]) for n in _INS}
    nc = program(lambda: bacc.Bacc("TRN2", target_bir_lowering=False, num_devices=1),
                 [(n, arrays["in_" + n].shape) for n in _INS])
    r = run_bass_kernel_spmd(nc, [arrays], core_ids=[0])
    return tuple(r.results[0]["out_" + n] for n, _ in _OUTS)
```

```python
from contextlib import ExitStack

import concourse.bass as bass
from concourse import mybir

ALU = mybir.AluOpType
ACT = mybir.ActivationFunctionType
AX = mybir.AxisListType
F32 = mybir.dt.float32
I32 = mybir.dt.int32
U32 = mybir.dt.uint32

P = 128
D = 1024
KD = D // P
SEQ = 1024
NT = SEQ // P
DEC = 8
T = SEQ + DEC
HEADS = 4
GW = 512
QKV = 3 * GW
MQ = QKV // P
CW = 4
GROUPS = 32
CH = 16
ST = 64
LAGS = 8
NCH = SEQ // LAGS
EXPERTS = 16
FE = 256
EPS = 1e-6
SEG = T // 3
PI2 = 6.283185307179586


class Steps:

    def __init__(self, sem, at):
        self.sem, self.at, self.n = sem, at, 0

    def did(self, ins, name=None):
        ins.then_inc(self.sem, 1)
        self.n += 1
        if name is not None:
            self.at[name] = self.n

    def wait(self, eng, name):
        eng.wait_ge(self.sem, self.at.get(name, 1))

    def drain(self, eng):
        if self.n:
            eng.wait_ge(self.sem, self.n)


def emit(nc, A, O, marks):
    ctx = ExitStack()

    def sem(name):
        return ctx.enter_context(nc.semaphore(name))

    def steps(name):
        return Steps(sem(name), marks.setdefault(name, {}))

    def dram(name, shape, dt=F32):
        return nc.dram_tensor(name, shape, dt, kind="Internal").ap()

    with ctx:
        sb = lambda name, shape, dt=F32: ctx.enter_context(nc.sbuf_tensor(name, shape, dt))
        ps = [ctx.enter_context(nc.psum_tensor(f"bank{i}", [P, 512], F32)) for i in range(8)]

        ident = sb("ident", [P, P])
        vecT = sb("vecT", [P, 117])
        modT = sb("modT", [P, 48, 9])
        hT = sb("hT", [P, KD, T])
        tail = sb("tail", [P, MQ, 3 + DEC])
        small = sb("small", [P, 64])
        cT = sb("cT", [P, KD, 9])
        B_ADA, N1G, N2G, CONVW, GNG, SNG = 0, 48, 56, 64, 112, 113

        def bc(ap, shape, axis=2):
            return ap.unsqueeze(axis).to_broadcast(shape)

        def room(flat):
            at = [0]

            def part(rows, *shape):
                size = 1
                for n in shape:
                    size *= n
                v = flat[0:rows, at[0]:at[0] + size]
                at[0] += size
                assert at[0] <= flat.shape[1]
                if len(shape) == 2:
                    v = v.rearrange("p (a b) -> p a b", b=shape[1])
                elif len(shape) == 3:
                    v = v.rearrange("p (a b c) -> p a b c", b=shape[1], c=shape[2])
                return v
            return part

        front = ctx.enter_context(ExitStack())
        fsb = lambda name, shape, dt=F32: front.enter_context(nc.sbuf_tensor(name, shape, dt))

        loads1, x_land = sem("loads1"), sem("x_land")
        ada_land = [sem(f"ada_land{q}") for q in range(4)]
        pe, act, dve, pool = steps("s1_pe"), steps("s1_act"), steps("s1_dve"), steps("s1_pool")
        ada_in = fsb("ada_in", [P, 4, KD, 512])
        X = fsb("X", [P, 9, D])
        crow = fsb("crow", [9, D])
        vrow = fsb("vrow", [117, P])
        sq = fsb("sq", [P, D])
        A1 = fsb("A1", [P, KD, 9])
        ada_row = fsb("ada_row", [9, 4, 512])
        w_ada = A["w_ada"][0].rearrange("(k p) n -> p k n", p=P)
        rows = [(A["b_ada"][0], 48), (A["norm1_g"][0], 8), (A["norm2_g"][0], 8),
                (A["conv_w"][0].rearrange("i n -> (i n)"), 48), (A["gdn_norm_g"][0], 1),
                (A["s5_norm_g"][0], 4)]
        def load_rows(eng, some, at):
            for v, n in some:
                eng.dma_start(vrow[at:at + n, :], v.rearrange("(m p) -> m p", p=P)).then_inc(loads1, 16)
                at += n

        with nc.Block() as block:
            @block.sync
            def _(sp):
                sp.dma_start(crow[0:1, :], A["c_prompt"]).then_inc(loads1, 16)
                sp.dma_start(crow[1:9, :], A["c_sample"]).then_inc(loads1, 16)
                load_rows(sp, rows[0:2], 0)

            @block.gpsimd
            def _(g):
                pool.did(g.memset(ident[:, :], 0.0))
                pool.drain(g)
                pool.did(g.affine_select(out=ident[:, :], in_=ident[:, :], compare_op=ALU.not_equal, fill=1.0,
                                         base=0, pattern=[[-1, P]], channel_multiplier=1), "ident")

            @block.scalar
            def _(a):
                load_rows(a, rows[2:6], B_ADA + N2G)
                for q in (0, 2):
                    a.dma_start(ada_in[:, q], w_ada[:, :, q * 512:(q + 1) * 512]).then_inc(ada_land[q], 16)
                a.dma_start(X[:, 0:NT, :], A["x_prompt"][0].rearrange("(i p) d -> p i d", p=P)).then_inc(x_land, 16)
                a.dma_start(X[0:DEC, NT, :], A["x_sample"].rearrange("b o d -> (b o) d")).then_inc(x_land, 16)
                for q in (1, 3):
                    a.dma_start(ada_in[:, q], w_ada[:, :, q * 512:(q + 1) * 512]).then_inc(ada_land[q], 16)
                a.wait_ge(loads1, 16 * 8)
                act.did(a.activation(crow[:, :], crow[:, :], ACT.Silu), "silu_c")
                a.wait_ge(x_land, 32)
                dve.wait(a, "clear_ss")
                for i in range(9):
                    n = P if i < NT else DEC
                    act.drain(a)
                    act.did(a.activation(sq[0:n, :], X[0:n, i, :], ACT.Square, accum_out=small[0:n, i:i + 1]), "ss")
                dve.wait(a, "ms")
                act.did(a.activation(small[:, 10:19], small[:, 10:19], ACT.Sqrt), "rms")
                dve.wait(a, "A1_0")
                for i in range(NT):
                    pe.wait(a, f"xT0_{i}")
                    for k in range(4):
                        act.did(a.activation(hT[:, k, i * P:(i + 1) * P], ps[i % 3][:, k * P:(k + 1) * P],
                                             ACT.Identity, scale=A1[:, k, 0:1], bias=modT[:, k, 0:1]), f"hT0_{i}")
                dve.wait(a, "A1_1")
                for i in range(0, NT, 2):
                    pe.wait(a, f"xT1_{i}")
                    for k in range(4, KD):
                        act.did(a.activation(hT[:, k, i * P:(i + 1) * P], ps[i % 3 + 3][:, (k - 4) * P:(k - 3) * P],
                                             ACT.Identity, scale=A1[:, k, 0:1], bias=modT[:, k, 0:1]), f"hT1_{i}")

            @block.tensor
            def _(t):
                pool.wait(t, "ident")
                t.wait_ge(loads1, 16 * 8)
                act.wait(t, "silu_c")
                for k in range(KD):
                    mm = t.transpose(ps[7][:, k * 9:k * 9 + 9], crow[:, k * P:(k + 1) * P], ident[0:9, 0:9])
                mm = t.transpose(ps[7][:, 128:128 + 117], vrow[:, :], ident[0:117, 0:117])
                pe.did(mm, "vec")
                dve.wait(t, "cT")
                def ada(q):
                    t.wait_ge(ada_land[q], 16)
                    for k in range(KD):
                        mm = t.matmul(ps[(6, 5, 7, 4)[q]][0:9, :], cT[:, k, :], ada_in[:, q, k, :], start=(k == 0), stop=(k == KD - 1))
                    pe.did(mm, f"ada{q}")

                def ada_transposes(half_):
                    dve.wait(t, f"ada_row{2 + half_}")
                    for n in range(2):
                        for m in range(4):
                            mm = t.transpose(ps[6 + half_][:, 36 * n + 9 * m:36 * n + 9 * m + 9], ada_row[:, half_ + 2 * n, m * P:(m + 1) * P], ident[0:9, 0:9])
                    pe.did(mm, f"adaT{half_}")

                def x_transpose(half_, i):
                    n, b = P if i < NT else DEC, i % 3 + 3 * half_
                    dve.wait(t, f"xs{i}")
                    if i >= 3:
                        (dve if half_ and (i - 3) % 2 else act).wait(t, f"hT{half_}_{i - 3}")
                    for k in range(4):
                        mm = t.transpose(ps[b][:, k * P:k * P + n], X[0:n, i, (4 * half_ + k) * P:(4 * half_ + k + 1) * P], ident[0:n, 0:n])
                    pe.did(mm, f"xT{half_}_{i}")

                dve.wait(t, "vecT")
                ada(0)
                ada(2)
                ada_transposes(0)
                ada(1)
                for i in range(9):
                    x_transpose(0, i)
                ada(3)
                ada_transposes(1)
                for i in range(9):
                    x_transpose(1, i)

            @block.vector
            def _(v):
                dve.did(v.memset(small[:, :], 1.0), "clear_ss")
                pe.wait(v, "vec")
                dve.did(v.tensor_copy(cT[:, :, :].rearrange("p k n -> p (k n)"), ps[7][:, 0:72]), "cT")
                dve.did(v.tensor_copy(vecT[:, :], ps[7][:, 128:128 + 117]), "vecT")

                def rows_copy(q):
                    pe.wait(v, f"ada{q}")
                    dve.did(v.tensor_copy(ada_row[:, q, :], ps[(6, 5, 7, 4)[q]][0:9, :]), f"ada_row{q}")

                def modulation(half_):
                    pe.wait(v, f"adaT{half_}")
                    for n in range(2):
                        m0 = 8 * n + 4 * half_
                        dve.did(v.tensor_tensor(modT[:, m0:m0 + 4, :], ps[6 + half_][:, 36 * n:36 * n + 36].rearrange("p (m n) -> p m n", m=4),
                                                bc(vecT[:, B_ADA + m0:B_ADA + m0 + 4], [P, 4, 9]), ALU.add))
                    dve.drain(v)
                    ks = slice(4 * half_, 4 * half_ + 4)
                    dve.did(v.tensor_scalar(A1[:, ks, :], modT[:, 8 + 4 * half_:12 + 4 * half_, :], 1.0, None, ALU.add))
                    dve.drain(v)
                    dve.did(v.tensor_tensor(A1[:, ks, :], A1[:, ks, :], bc(vecT[:, N1G + 4 * half_:N1G + 4 * half_ + 4], [P, 4, 9]), ALU.mult), f"A1_{half_}")
                    dve.drain(v)
                rows_copy(0)
                rows_copy(2)
                modulation(0)
                act.wait(v, "ss")
                dve.did(v.tensor_scalar(small[:, 10:19], small[:, 0:9], 1.0 / D, EPS, ALU.mult, ALU.add), "ms")
                act.wait(v, "rms")
                dve.did(v.reciprocal(small[:, 20:29], small[:, 10:19]))
                dve.drain(v)

                for i in range(9):
                    n = P if i < NT else DEC
                    dve.did(v.tensor_scalar(X[0:n, i, :], X[0:n, i, :], small[0:n, 20 + i:21 + i], None, ALU.mult), f"xs{i}")
                for half_ in range(2):
                    ks = slice(4 * half_, 4 * half_ + 4)
                    if half_ == 1:
                        rows_copy(1)
                        rows_copy(3)
                        modulation(1)
                    for i in range(9):
                        if i < NT and (half_ == 0 or i % 2 == 0):
                            continue
                        pe.wait(v, f"xT{half_}_{i}")
                        if i < NT:
                            for k in range(4, KD):
                                dve.did(v.tensor_scalar(hT[:, k, i * P:(i + 1) * P], ps[i % 3 + 3][:, (k - 4) * P:(k - 3) * P],
                                                        A1[:, k, 0:1], modT[:, k, 0:1], ALU.mult, ALU.add), f"hT1_{i}")
                        else:
                            src = ps[i % 3 + 3 * half_][:, :].rearrange("p (k n) -> p k n", k=4)[:, :, 0:DEC]
                            dve.did(v.tensor_tensor(hT[:, ks, SEQ:T], src, A1[:, ks, 1:9], ALU.mult))
                            dve.drain(v)
                            dve.did(v.tensor_tensor(hT[:, ks, SEQ:T], hT[:, ks, SEQ:T], modT[:, ks, 1:9], ALU.add))
        front.close()

        mid = ctx.enter_context(ExitStack())
        msb = lambda name, shape, dt=F32: mid.enter_context(nc.sbuf_tensor(name, shape, dt))
        V = msb("V", [P, GROUPS, LAGS, CH])
        Vd = msb("Vd", [DEC, GW])
        NG = 8
        small_room = msb("small_room", [P, 3648])
        s5_room = room(small_room[:, :])
        D16 = s5_room(CH, GROUPS)
        Bb, B2 = s5_room(P, GROUPS, CH), s5_room(P, GROUPS, CH)
        Q1, Q2 = s5_room(P, 4, P), s5_room(P, 4, P)
        X0 = s5_room(P, GROUPS, DEC)
        J = s5_room(P, P)
        LC = s5_room(P, 2, GROUPS, LAGS + 1)
        LB = s5_room(P, 2, GROUPS, LAGS)
        rho, ph = s5_room(P, GROUPS), s5_room(P, 2, GROUPS)
        s5 = {n: A["s5_" + n][0] for n in ("lambda_re", "lambda_im", "log_dt", "b_re", "b_im", "c_re", "c_im", "d")}
        ROUND = 12582912.0
        mid2 = ctx.enter_context(ExitStack())
        msb = lambda name, shape, dt=F32: mid2.enter_context(nc.sbuf_tensor(name, shape, dt))
        Z = msb("Z", [P, 9, GW])
        gates = msb("gates", [P, 9, 8])
        Og = msb("Og", [P, 9, GW])
        qkvT = msb("qkvT", [P, MQ, T])
        upper = msb("upper", [P, P])
        neg_lo = msb("neg_lo", [P, P])
        big_up = msb("big_up", [P, P])
        bd = msb("bd", [P, 4, P])
        pick = msb("pick", [P, 8, 8])
        s2 = ctx.enter_context(ExitStack())
        w_ring = s2.enter_context(nc.sbuf_tensor("w_ring", [P, 2, KD, 512], F32))
        w_gates = s2.enter_context(nc.sbuf_tensor("w_gates", [P, KD, 8], F32))
        pre = s2.enter_context(nc.sbuf_tensor("pre", [P, 2, 3 + T], F32))
        convd = s2.enter_context(nc.sbuf_tensor("convd", [P, MQ, 3, DEC], F32))
        crows = s2.enter_context(nc.sbuf_tensor("crows", [3 * DEC, QKV], F32))
        newrows = crows[0:11, :]
        scratch = room(Og[:, :, :].rearrange("p i n -> p (i n)"))
        lamrow = scratch(GROUPS, 2, P)
        drow = scratch(GROUPS, CH)
        lr, li, dtl = (scratch(P, GROUPS) for _ in range(3))
        B1, wt = scratch(P, GROUPS, CH), scratch(P, GROUPS, CH)
        crow1, crow2 = scratch(P, 4, P), scratch(P, 4, P)
        x0row = scratch(P, 2, P)
        w4 = scratch(P, 12, GROUPS)
        gate_rows = scratch(8, T)
        s5_land, s5_x0, s5_c = sem("s5_land"), sem("s5_x0"), sem("s5_c")
        w_in_v = A["w_in"][0].rearrange("(k p) n -> p k n", p=P)
        BIG = 1e30
        w_cols = [0, 512, 1024, QKV, QKV + GW + 8]
        w_land, w_first = [sem("w_in_a"), sem("w_in_b")], sem("w_first")
        gate_land, conv_land, conv_out = sem("gate_land"), sem("conv_land"), sem("conv_out")
        pe, act, dve, pool = steps("s2_pe"), steps("s2_act"), steps("s2_dve"), steps("s2_pool")
        with nc.Block() as block:
            @block.sync
            def _(sp):
                with nc.allow_non_contiguous_dma(reason="eight gate columns"):
                    sp.dma_start(w_gates[:, :, :], w_in_v[:, :, QKV + GW:QKV + GW + 8]).then_inc(gate_land, 16)
                sp.dma_start(crows[:, :], A["state_conv"][0].rearrange("b i n -> (b i) n")).then_inc(conv_land, 16)
                for q in range(1, 5):
                    if q >= 2:
                        pe.wait(sp, f"chunk{q - 2}")
                    sp.dma_start(w_ring[:, q % 2], w_in_v[:, :, w_cols[q]:w_cols[q] + 512]).then_inc(w_land[q % 2], 16)
                for n, name in enumerate(("lambda_re", "lambda_im")):
                    for rep in range(2):
                        sp.dma_start(lamrow[:, n, rep * ST:(rep + 1) * ST], s5[name]).then_inc(s5_land, 16)
                sp.dma_start(dtl[:, :], s5["log_dt"].unsqueeze(0).to_broadcast([P, GROUPS])).then_inc(s5_land, 16)
                sp.dma_start(drow[:, :], s5["d"].rearrange("(g c) -> g c", c=CH)).then_inc(s5_land, 16)
                b_re, b_im = (s5[n].rearrange("g p c -> p g c") for n in ("b_re", "b_im"))
                for dst, src in ((B1[0:ST], b_re), (B1[ST:P], b_im), (B2[0:ST], b_im), (B2[ST:P], b_re)):
                    sp.dma_start(dst, src).then_inc(s5_land, 16)
                c_re, c_im = (s5[n].rearrange("(q g) c p -> (g c) q p", q=4) for n in ("c_re", "c_im"))
                for dst, src in ((crow1[:, :, 0:ST], c_re), (crow1[:, :, ST:P], c_im), (crow2[:, :, 0:ST], c_im), (crow2[:, :, ST:P], c_re)):
                    sp.dma_start(dst, src).then_inc(s5_c, 16)
                for n, name in enumerate(("state_s5_re", "state_s5_im")):
                    sp.dma_start(x0row[:, :, n * ST:(n + 1) * ST], A[name][0].rearrange("(x b) g p -> (b g) x p", x=2)).then_inc(s5_x0, 16)
                dve.wait(sp, "newrows")
                sp.dma_start(O["conv_p"][0, 0], newrows[0:3, :]).then_inc(conv_out, 16)
                sp.dma_start(O["conv_s"][0, :, 2, :], newrows[3:11, :]).then_inc(conv_out, 16)
                sp.dma_start(O["conv_s"][0, :, 0:2, :], A["state_conv"][0, :, 1:3, :]).then_inc(conv_out, 16)
                sp.wait_ge(conv_out, 48)

            @block.tensor
            def _(t):
                def conv_state():
                    t.wait_ge(conv_land, 16)
                    for x in range(MQ):
                        mm = t.transpose(ps[7][:, x * 24:x * 24 + 24], crows[:, x * P:(x + 1) * P], ident[0:24, 0:24])
                    pe.did(mm, "conv_state")

                for m in range(MQ):
                    q = m // 4
                    if m % 4 == 0:
                        t.wait_ge(w_first if q == 0 else w_land[q % 2], 16 * (q // 2 + 1))
                    if m == 1:
                        conv_state()
                    if m == 2:
                        t.wait_ge(w_land[0], 16)
                    if m >= 2:
                        act.wait(t, f"pre{m - 2}")
                    for s in range(3):
                        for k in range(KD):
                            mm = t.matmul(ps[3 * (m % 2) + s][:, 0:SEG], w_ring[:, q % 2, k, (m % 4) * P:(m % 4 + 1) * P],
                                          hT[:, k, s * SEG:(s + 1) * SEG], start=(k == 0), stop=(k == KD - 1))
                    pe.did(mm, f"qkv{m}")
                    if m % 4 == 3:
                        pe.at[f"chunk{q}"] = pe.n
                t.wait_ge(gate_land, 16)
                act.wait(t, f"pre{MQ - 2}")
                for x in range(3):
                    for k in range(KD):
                        mm = t.matmul(ps[x][0:8, 0:SEG], w_gates[:, k, :], hT[:, k, x * SEG:(x + 1) * SEG], start=(k == 0), stop=(k == KD - 1))
                pe.did(mm, "gate_rows")
                act.wait(t, f"pre{MQ - 1}")
                dve.wait(t, "conv_state")
                t.wait_ge(s5_land, 16 * 10)
                t.transpose(ps[7][:, 0:GROUPS], lamrow[:, 0, :], ident[0:GROUPS, 0:GROUPS])
                t.transpose(ps[7][:, GROUPS:2 * GROUPS], lamrow[:, 1, :], ident[0:GROUPS, 0:GROUPS])
                pe.did(t.transpose(ps[7][0:CH, 64:96], drow[:, :], ident[0:GROUPS, 0:GROUPS]), "lam")
                t.wait_ge(s5_x0, 32)
                for n in range(2):
                    mm = t.transpose(ps[4][:, n * P:(n + 1) * P], x0row[:, n, :], ident[:, :])
                pe.did(mm, "x0")
                dve.wait(t, "gate_rows")
                for step in range(2):
                    q = 3 + step
                    t.wait_ge(w_land[q % 2], 16 * (q // 2 + 1))
                    for i in range(9):
                        n = P if i < NT else DEC
                        b = 9 * step + i
                        if b >= 4:
                            act.wait(t, f"zu{b - 4}")
                        for k in range(KD):
                            if i == NT:
                                tok = hT[:, k, SEQ:T]
                            elif step == 0:
                                tok = hT[:, k, i * P:(i + 1) * P]
                            else:
                                tok = hT[:, k, i:SEQ:LAGS]
                            mm = t.matmul(ps[b % 4][0:n, :], tok, w_ring[:, q % 2, k, :],
                                          start=(k == 0), stop=(k == KD - 1))
                        pe.did(mm, f"zu{b}")
                        if b == 1:
                            dve.wait(t, "crow")
                            dve.wait(t, "lam")
                            for q4 in range(4):
                                t.transpose(ps[5][:, q4 * P:(q4 + 1) * P], crow1[:, q4, :], ident[:, :])
                                mm = t.transpose(ps[7][:, q4 * P:(q4 + 1) * P], crow2[:, q4, :], ident[:, :])
                            pe.did(mm, "Q")
                            for x in range(9):
                                m = P if x < NT else DEC
                                mm = t.transpose(ps[6][0:m, x * 8:x * 8 + 8], gate_rows[:, x * P:x * P + m], ident[0:8, 0:8])
                            pe.did(mm, "gates")
                dve.wait(t, "gates")
                act.wait(t, "Q")
                for m in range(MQ):
                    dst = ps[4 + m // 4]
                    mm = t.transpose(dst[0:11, (m % 4) * P:(m % 4 + 1) * P], tail[:, m, :], ident[:, :])
                pe.did(mm, "newrows")

            @block.scalar
            def _(a):
                for x, landed in enumerate((w_first, w_land[0])):
                    a.dma_start(w_ring[:, 0, :, x * 256:(x + 1) * 256], w_in_v[:, :, x * 256:(x + 1) * 256]).then_inc(landed, 16)
                for m in range(MQ):
                    pe.wait(a, f"qkv{m}")
                    if m >= 2:
                        dve.wait(a, f"conv{m - 2}")
                    else:
                        pool.wait(a, "pad")
                    for s in range(3):
                        act.did(a.activation(pre[:, m % 2, 3 + s * SEG:3 + (s + 1) * SEG],
                                             ps[3 * (m % 2) + s][:, 0:SEG], ACT.Copy), f"pre{m}")
                    if m >= 1:
                        dve.wait(a, f"conv{m - 1}")
                        act.did(a.activation(qkvT[:, m - 1, :], qkvT[:, m - 1, :], ACT.Silu))
                dve.wait(a, f"conv{MQ - 1}")
                act.did(a.activation(qkvT[:, MQ - 1, :], qkvT[:, MQ - 1, :], ACT.Silu))
                a.wait_ge(s5_land, 16 * 10)
                act.did(a.activation(dtl[:, :], dtl[:, :], ACT.Exp), "dt")
                for b in range(18):
                    if b == 2:
                        dve.wait(a, "xre")
                        act.did(a.activation(w4[:, 2], w4[:, 0], ACT.Exp), "r1")
                        act.did(a.activation(rho[:, :], w4[:, 0], ACT.Exp, scale=float(LAGS)))
                        dve.wait(a, "red")
                        act.did(a.activation(w4[:, 3], w4[:, 1], ACT.Sin))
                        act.did(a.activation(w4[:, 4], w4[:, 1], ACT.Sin, scale=0.5), "sin")
                    elif b == 3:
                        pe.wait(a, "Q")
                        act.did(a.activation(Q1[:, :, :].rearrange("p q n -> p (q n)"), ps[5][:, :], ACT.Copy))
                        act.did(a.activation(Q2[:, :, :].rearrange("p q n -> p (q n)"), ps[7][:, :], ACT.Copy), "Q")
                        pe.wait(a, "x0")
                        act.did(a.activation(X0[:, :, :].rearrange("p g (x b) -> p x b g", x=2),
                                             ps[4][:, 0:256].rearrange("p (x b g) -> p x b g", x=2, b=4), ACT.Copy), "X0")
                    i, n = b % 9, P if b % 9 < NT else DEC
                    pe.wait(a, f"zu{b}")
                    if b < 9:
                        act.did(a.activation(Z[0:n, i, :], ps[b % 4][0:n, :], ACT.Silu), f"zu{b}")
                    elif i < NT:
                        act.did(a.activation(V[:, :, i, :], ps[b % 4][:, :].rearrange("p (g c) -> p g c", c=CH), ACT.Copy), f"zu{b}")
                    else:
                        act.did(a.activation(Vd[:, :], ps[b % 4][0:n, :], ACT.Copy), f"zu{b}")

            @block.gpsimd
            def _(g):
                pool.did(g.memset(Z[:, NT, :], 0.0))
                pool.did(g.memset(gates[:, NT, :], 0.0))
                pool.did(g.memset(pre[:, :, 0:3], 0.0), "pad")
                pool.did(g.memset(J[:, :], 0.0))
                pool.did(g.memset(LC[:, 0, :, 0:1], 1.0))
                pool.did(g.memset(LC[:, 1, :, 0:1], 0.0))
                pool.drain(g)
                pool.did(g.affine_select(out=J[:, :], in_=J[:, :], compare_op=ALU.not_equal, fill=-1.0, base=-ST,
                                         pattern=[[-1, P]], channel_multiplier=1))
                pool.drain(g)
                pool.did(g.affine_select(out=J[:, :], in_=J[:, :], compare_op=ALU.not_equal, fill=1.0, base=ST,
                                         pattern=[[-1, P]], channel_multiplier=1), "clear")
                pool.did(g.memset(pick[:, :, :], 0.0))
                pool.drain(g)
                pool.did(g.affine_select(out=pick[:, :, :], in_=pick[:, :, :], compare_op=ALU.not_equal, fill=1.0,
                                         base=0, pattern=[[1, 8], [-1, 8]], channel_multiplier=0))
                pool.did(g.memset(upper[:, :], 1.0))
                pool.did(g.memset(neg_lo[:, :], 0.0))
                pool.did(g.memset(big_up[:, :], BIG))
                pool.did(g.memset(bd[:, :, :], 1.0))
                pool.drain(g)
                pool.did(g.affine_select(out=upper[:, :], in_=upper[:, :], compare_op=ALU.is_ge, fill=0.0,
                                         base=0, pattern=[[1, P]], channel_multiplier=-1))
                pool.did(g.affine_select(out=neg_lo[:, :], in_=neg_lo[:, :], compare_op=ALU.is_ge, fill=-BIG,
                                         base=0, pattern=[[1, P]], channel_multiplier=-1))
                pool.did(g.affine_select(out=big_up[:, :], in_=big_up[:, :], compare_op=ALU.is_ge, fill=0.0,
                                         base=0, pattern=[[1, P]], channel_multiplier=-1))
                for j, b in enumerate((16, 32, 64)):
                    blocks = bd[:, j, :].rearrange("p (n b) -> p n b", b=b)
                    pool.drain(g)
                    pool.did(g.affine_select(out=blocks, in_=blocks, compare_op=ALU.is_ge, fill=0.0,
                                             base=0, pattern=[[-b, P // b], [0, b]], channel_multiplier=1))
                    pool.drain(g)
                    pool.did(g.affine_select(out=blocks, in_=blocks, compare_op=ALU.is_ge, fill=0.0,
                                             base=b - 1, pattern=[[b, P // b], [0, b]], channel_multiplier=-1))
                for j in (3, 2, 1):
                    pool.drain(g)
                    pool.did(g.tensor_tensor(bd[:, j, :], bd[:, j, :], bd[:, j - 1, :], ALU.subtract))

            @block.vector
            def _(v):
                pe.wait(v, "conv_state")
                dve.did(v.tensor_copy(convd[:, :, :, :].rearrange("p m i b -> p m b i"),
                                      ps[7][:, 0:24 * MQ].rearrange("p (m b i) -> p m b i", m=MQ, i=3)), "conv_state")
                dve.drain(v)
                for m in range(MQ):
                    act.wait(v, f"pre{m}")
                    w = [vecT[:, CONVW + i * MQ + m:CONVW + i * MQ + m + 1] for i in range(CW)]
                    y, yd = qkvT[:, m, 0:SEQ], qkvT[:, m, SEQ:T]
                    dve.did(v.tensor_copy(tail[:, m, :], pre[:, m % 2, SEQ:3 + T]))
                    dve.did(v.tensor_scalar(yd, convd[:, m, 0, :], w[0], None, ALU.mult))
                    dve.did(v.tensor_scalar(y, pre[:, m % 2, 0:SEQ], w[0], None, ALU.mult))
                    for i in range(1, CW):
                        dve.drain(v)
                        old = convd[:, m, i, :] if i < 3 else pre[:, m % 2, 3 + SEQ:3 + T]
                        dve.did(v.scalar_tensor_tensor(out=yd, in0=old, scalar=w[i], in1=yd, op0=ALU.mult, op1=ALU.add))
                        dve.did(v.scalar_tensor_tensor(out=y, in0=pre[:, m % 2, i:i + SEQ], scalar=w[i], in1=y,
                                                       op0=ALU.mult, op1=ALU.add), f"conv{m}")
                pe.wait(v, "gate_rows")
                for x in range(3):
                    dve.did(v.tensor_copy(gate_rows[:, x * SEG:(x + 1) * SEG], ps[x][0:8, 0:SEG]), "gate_rows")

                w = lambda n: w4[:, n]

                def tt(out, x, y, op, name=None, wait=True):
                    if wait:
                        dve.drain(v)
                    dve.did(v.tensor_tensor(out, x, y, op), name)

                def ts(out, x, c1, c2, op1, op2, name=None):
                    dve.drain(v)
                    dve.did(v.tensor_scalar(out, x, c1, c2, op1, op2) if c2 is not None else v.tensor_scalar(out, x, c1, None, op1), name)

                v.wait_ge(s5_land, 16 * 10)
                v.wait_ge(s5_c, 64)
                dve.did(v.tensor_scalar(crow1[:, :, ST:P], crow1[:, :, ST:P], -1.0, None, ALU.mult))
                dve.did(v.tensor_scalar(crow2[:, :, :], crow2[:, :, :], -1.0, None, ALU.mult), "crow")
                dve.did(v.tensor_scalar(B2[0:ST], B2[0:ST], -1.0, None, ALU.mult))
                pe.wait(v, "lam")
                dve.did(v.tensor_copy(lr[:, :], ps[7][:, 0:GROUPS]))
                dve.did(v.tensor_copy(li[:, :], ps[7][:, GROUPS:2 * GROUPS]))
                dve.did(v.tensor_copy(D16[:, :], ps[7][0:CH, 64:96]), "lam")
                act.wait(v, "dt")
                tt(w(0), lr[:, :], dtl[:, :], ALU.mult, "xre")
                tt(w(1), li[:, :], dtl[:, :], ALU.mult)
                ts(w(5), w(1), 1.0 / PI2, ROUND, ALU.mult, ALU.add)
                ts(w(5), w(5), ROUND, None, ALU.subtract, None)
                dve.drain(v)
                dve.did(v.scalar_tensor_tensor(out=w(1), in0=w(5), scalar=-6.28125, in1=w(1), op0=ALU.mult, op1=ALU.add))
                dve.drain(v)
                dve.did(v.scalar_tensor_tensor(out=w(1), in0=w(5), scalar=-(PI2 - 6.28125), in1=w(1), op0=ALU.mult, op1=ALU.add))
                ts(w(1), w(1), 3.1415925, -3.1415925, ALU.min, ALU.max, "red")
                act.wait(v, "sin")
                tt(w(5), w(4), w(4), ALU.mult)
                ts(w(5), w(5), -2.0, 1.0, ALU.mult, ALU.add)
                tt(LC[:, 0, :, 1], w(2), w(5), ALU.mult)
                tt(LC[:, 1, :, 1], w(2), w(3), ALU.mult)
                ts(w(6), LC[:, 0, :, 1], -1.0, None, ALU.add, None)
                tt(w(7), lr[:, :], lr[:, :], ALU.mult)
                tt(w(8), li[:, :], li[:, :], ALU.mult)
                tt(w(7), w(7), w(8), ALU.add)
                dve.drain(v)
                dve.did(v.reciprocal(w(7), w(7)))
                tt(w(8), w(6), lr[:, :], ALU.mult)
                tt(w(9), LC[:, 1, :, 1], li[:, :], ALU.mult)
                tt(w(8), w(8), w(9), ALU.add)
                tt(w(8), w(8), w(7), ALU.mult)
                tt(w(9), LC[:, 1, :, 1], lr[:, :], ALU.mult)
                tt(w(10), w(6), li[:, :], ALU.mult)
                tt(w(9), w(9), w(10), ALU.subtract)
                tt(w(9), w(9), w(7), ALU.mult)
                full = [P, GROUPS, CH]
                tt(Bb[:, :, :], B1[:, :, :], bc(w(8), full), ALU.mult)
                tt(wt, B2[:, :, :], bc(w(9), full), ALU.mult)
                tt(Bb[:, :, :], Bb[:, :, :], wt, ALU.add)
                tt(B2[:, :, :], B2[:, :, :], bc(w(8), full), ALU.mult)
                tt(wt, B1[:, :, :], bc(w(9), full), ALU.mult)
                tt(B2[:, :, :], B2[:, :, :], wt, ALU.subtract)
                pool.wait(v, "clear")
                for k in range(2, LAGS + 1):
                    a_, b_ = LC[:, 0, :, k - 1], LC[:, 1, :, k - 1]
                    tt(w(6), a_, LC[:, 0, :, 1], ALU.mult)
                    tt(w(7), b_, LC[:, 1, :, 1], ALU.mult)
                    tt(LC[:, 0, :, k], w(6), w(7), ALU.subtract)
                    tt(w(6), a_, LC[:, 1, :, 1], ALU.mult)
                    tt(w(7), b_, LC[:, 0, :, 1], ALU.mult)
                    tt(LC[:, 1, :, k], w(6), w(7), ALU.add)
                dve.drain(v)
                for k in range(LAGS):
                    dve.did(v.tensor_copy(LB[:, :, :, k], LC[:, :, :, LAGS - 1 - k]))
                c_, s_ = w(5), w(3)
                for n in range(3):
                    co, so = (ph[:, 0, :], ph[:, 1, :]) if n == 2 else (w(5), w(3))
                    tt(w(6), c_, c_, ALU.mult)
                    tt(w(7), s_, s_, ALU.mult)
                    tt(w(8), c_, s_, ALU.mult)
                    tt(co, w(6), w(7), ALU.subtract)
                    ts(so, w(8), 2.0, None, ALU.mult, None, "ph")
                pe.wait(v, "gates")
                pool.wait(v, "pad")
                dve.did(v.tensor_copy(gates[:, 0:8, :].rearrange("p i n -> p (i n)"), ps[6][:, 0:64]))
                dve.did(v.tensor_copy(gates[0:DEC, 8, :], ps[6][0:DEC, 64:72]), "gates")
                pe.wait(v, "newrows")
                for b in range(3):
                    dve.did(v.tensor_copy(newrows[:, b * 512:(b + 1) * 512], ps[4 + b][0:11, :]), "newrows")
        s2.close()

        s3 = ctx.enter_context(ExitStack())
        t3 = lambda name, shape: s3.enter_context(nc.sbuf_tensor(name, shape, F32))
        beta = t3("beta", [P, 9, HEADS])
        gg = t3("gg", [P, 9, HEADS])
        sp_t = t3("sp_t", [P, 2, 9, HEADS])
        hp = t3("hp", [P, 2, HEADS])
        Gc = t3("Gc", [P, NT, HEADS])
        nbe = t3("nbe", [P, NT, HEADS])
        rn = t3("rn", [P, 9, 2 * HEADS])
        sqT = t3("sqT", [P, T])
        half = [P, 2, 2, P]
        kn = t3("kn", half)
        R = t3("R", half)
        D0, D1 = t3("D0", half), t3("D1", half)
        L, N = t3("L", half), t3("N", half)
        NL1 = t3("NL1", [P, 2, 2, 2, P])
        NL2, NL4 = t3("NL2", [P, 2, 2, 2, P]), t3("NL4", [P, 2, 2, 2, P])
        L8, Xi, Zi, Lk = t3("L8", half), t3("Xi", half), t3("Zi", half), t3("Lk", half)
        egb = t3("egb", half)
        Y, vb, kTn, at, qg, kd = (hT[:, :, :].rearrange("p k t -> p (k t)")[:, n * 1024:(n + 1) * 1024]
                                  .rearrange("p (b l h n) -> p b l h n", b=2, l=2, h=2) for n in range(6))
        egl = t3("egl", [P, 2, HEADS])
        r, u = t3("r", half), t3("u", half)
        S = t3("S", [P, HEADS, P])
        zland = sem("zland")
        SLOTS = 2 * T // P + EXPERTS
        xs_d = dram("xs_d", ((SLOTS + 4) * P, D))
        ys_d = xs_d
        hp_land, s_out = sem("hp_land"), sem("gdn_out")
        pe, act, dve, pool = steps("s3_pe"), steps("s3_act"), steps("s3_dve"), steps("s3_pool")

        def chunk(m, c):
            return qkvT[:, m, c * P:(c + 1) * P]

        with nc.Block() as block:
            @block.sync
            def _(sp):
                sp.dma_start(hp[:, 0, :], A["dt_bias"][0:1, :].to_broadcast([P, HEADS])).then_inc(hp_land, 16)
                sp.dma_start(hp[:, 1, :], A["a_log"][0:1, :].to_broadcast([P, HEADS])).then_inc(hp_land, 16)
                pool.wait(sp, "zeros")
                for n in range(SLOTS // 2 + 2):
                    sp.dma_start(xs_d[n * 2 * P:(n + 1) * 2 * P, :].rearrange("(a p) d -> p a d", p=P),
                                 Og[:, 4:8, :].rearrange("p i n -> p (i n)").rearrange("p (a d) -> p a d", a=2)).then_inc(zland, 16)
                dve.wait(sp, "S7_1")
                sp.dma_start(O["gdn_p"][0, 0].rearrange("h k v -> k h v"), S[:, :, :]).then_inc(s_out, 16)
                sp.wait_ge(s_out, 16)

            @block.gpsimd
            def _(g):
                pool.did(g.memset(Og[:, 4:9, :], 0.0), "zeros")
                pool.did(g.memset(S[:, :, :], 0.0))
                pool.drain(g)
                pool.did(g.memset(sp_t[:, 1, :, :], 0.0), "masks")
                for c in range(NT):
                    b = c % 2
                    for l in range(2):
                        act.wait(g, f"egb{c}_{l}")
                        if c >= 2:
                            pe.wait(g, f"o{c - 2}_{l}")
                        for hh in range(2):
                            pool.did(g.tensor_tensor(qg[:, b, l, hh, :], chunk(2 * l + hh, c), egb[:, l, hh, :], ALU.mult))
                        pool.did(g.tensor_copy(egl[:, b, 2 * l:2 * l + 2], egb[:, l, :, P - 1]), f"qg{c}_{l}")
                        dve.wait(g, f"kn{c}_{l}")
                        act.wait(g, f"D{c}_{l}")
                        pool.did(g.tensor_tensor(kd[:, b, l], kn[:, l], D1[:, l, :, P - 1:P].to_broadcast([P, 2, P]), ALU.mult), f"kd{c}_{l}")
                    for l in range(2):
                        dve.wait(g, f"L{c}_{l}")
                        pool.did(g.tensor_tensor(NL1[:, l, 1], L[:, l], bc(bd[:, 0, :], [P, 2, P], 1), ALU.mult), f"Ld{c}_{l}")
                    for k in range(1, 4):
                        for l in range(2):
                            if k > 1:
                                pe.wait(g, f"Z{k - 1}_{c}_{l}")
                            elif c > 0:
                                pe.wait(g, f"Z3_{c - 1}_{l}")
                            pool.did(g.tensor_tensor(Lk[:, l], L[:, l], bc(bd[:, k, :], [P, 2, P], 1), ALU.mult), f"Lk{k}_{c}_{l}")

            @block.tensor
            def _(t):
                for m in range(2 * HEADS):
                    (dve if m % 2 else act).wait(t, f"sq{m}")
                    for x in range(3):
                        mm = t.matmul(ps[2 + x][0:8, 0:SEG], pick[:, m, :], hT[:, m, x * SEG:(x + 1) * SEG], start=(m == 0), stop=(m == 2 * HEADS - 1))
                pe.did(mm, "ss_rows")
                act.wait(t, "ss_rows")
                for i in range(9):
                    n = P if i < NT else DEC
                    mm = t.transpose(ps[0][0:n, i * 8:i * 8 + 8], sqT[0:8, i * P:i * P + n], ident[0:8, 0:8])
                pe.did(mm, f"ss{2 * HEADS - 1}")
                dve.wait(t, "gg")
                pe.did(t.matmul(ps[1][:, 0:NT * HEADS], upper[:, :], gg[:, 0:NT, :], start=True, stop=True), "G")
                dve.wait(t, "rn")
                dve.wait(t, "Gc")

                def scan_step(c, l, step):
                    b = c % 2
                    bank = ps[6 + l]
                    for hh in range(2):
                        h = 2 * l + hh
                        lo, hi = bank[:, hh * P:(hh + 1) * P], bank[:, 256 + hh * P:256 + (hh + 1) * P]
                        if step == 0:
                            if hh == 0:
                                if c > 0:
                                    dve.wait(t, f"S{c - 1}_{l}")
                            mm = t.matmul(lo, kTn[:, b, l, hh, :], S[:, h, :], start=True, stop=True)
                        elif step == 1:
                            if hh == 0:
                                dve.wait(t, f"r{c}_{l}")
                            mm = t.matmul(hi, Y[:, b, l, hh, :], r[:, l, hh, :], start=True, stop=True)
                        else:
                            if hh == 0:
                                act.wait(t, f"u{c}_{l}")
                                pool.wait(t, f"kd{c}_{l}")
                            t.matmul(lo, kd[:, b, l, hh, :], u[:, l, hh, :], start=True, stop=True)
                            t.matmul(hi, qg[:, b, l, hh, :], S[:, h, :], start=True, stop=False)
                            mm = t.matmul(hi, at[:, b, l, hh, :], u[:, l, hh, :], start=False, stop=True)
                    pe.did(mm, f"{('ks', 'u', 'o')[step]}{c}_{l}")

                def scan(c, step):
                    if c >= 0:
                        for l in range(2):
                            scan_step(c, l, step)

                for c in range(NT):
                    b = c % 2
                    for l in range(2):
                        if c > 0:
                            dve.wait(t, f"Y3_{c - 1}_{l}")
                        for hh in range(2):
                            t.transpose(ps[3 * l][:, hh * P:(hh + 1) * P], chunk(HEADS + 2 * l + hh, c), ident[:, :])
                            mm = t.transpose(ps[3 * l][:, 256 + hh * P:256 + (hh + 1) * P], chunk(2 * HEADS + 2 * l + hh, c), ident[:, :])
                        pe.did(mm, f"kv{c}_{l}")
                        for hh in range(2):
                            h = 2 * l + hh
                            mm = t.matmul(ps[3 * l + 1][:, hh * P:(hh + 1) * P], gg[:, c, h:h + 1].to_broadcast([P, P]), upper[:, :], start=True, stop=True)
                        pe.did(mm, f"Gb{c}_{l}")
                    for l in range(2):
                        dve.wait(t, f"kn{c}_{l}")
                        for hh in range(2):
                            mm = t.transpose(ps[3 * l + 2][:, hh * P:(hh + 1) * P], kn[:, l, hh, :], ident[:, :])
                        pe.did(mm, f"kTn{c}_{l}")
                    scan(c - 1, 0)
                    for l in range(2):
                        act.wait(t, f"kTn{c}_{l}")
                        dve.wait(t, f"vb{c}_{l}")
                        for hh in range(2):
                            t.matmul(ps[3 * l][:, hh * P:(hh + 1) * P], kTn[:, b, l, hh, :], kTn[:, b, l, hh, :], start=True, stop=True)
                            mm = t.matmul(ps[3 * l][:, 256 + hh * P:256 + (hh + 1) * P], kTn[:, b, l, hh, :], chunk(2 * l + hh, c), start=True, stop=True)
                        pe.did(mm, f"kk{c}_{l}")
                    scan(c - 1, 1)
                    for l in range(2):
                        dve.wait(t, f"L{c}_{l}")
                        for hh in range(2):
                            mm = t.transpose(ps[3 * l + 2][:, hh * P:(hh + 1) * P], L[:, l, hh, :], ident[:, :])
                        pe.did(mm, f"N{c}_{l}")
                    scan(c - 1, 2)
                    for l in range(2):
                        dve.wait(t, f"Y0_{c}_{l}")
                        pool.wait(t, f"Ld{c}_{l}")
                        for hh in range(2):
                            t.matmul(ps[3 * l][:, hh * P:(hh + 1) * P], NL1[:, l, 1, hh, :], NL1[:, l, 0, hh, :], start=True, stop=True)
                            mm = t.matmul(ps[3 * l][:, 256 + hh * P:256 + (hh + 1) * P], NL1[:, l, 0, hh, :], NL1[:, l, 1, hh, :], start=True, stop=True)
                        pe.did(mm, f"NL2_{c}_{l}")
                    for l in range(2):
                        act.wait(t, f"NL2_{c}_{l}")
                        for hh in range(2):
                            t.matmul(ps[3 * l][:, hh * P:(hh + 1) * P], NL2[:, l, 1, hh, :], NL2[:, l, 0, hh, :], start=True, stop=True)
                            mm = t.matmul(ps[3 * l][:, 256 + hh * P:256 + (hh + 1) * P], NL2[:, l, 0, hh, :], NL2[:, l, 1, hh, :], start=True, stop=True)
                        pe.did(mm, f"NL4_{c}_{l}")
                        for hh in range(2):
                            mm = t.matmul(ps[3 * l + 1][:, hh * P:(hh + 1) * P], NL2[:, l, 1, hh, :], Y[:, b, l, hh, :], start=True, stop=True)
                        pe.did(mm, f"dYa{c}_{l}")
                    for l in range(2):
                        act.wait(t, f"NL4_{c}_{l}")
                        for hh in range(2):
                            mm = t.matmul(ps[3 * l][:, hh * P:(hh + 1) * P], NL4[:, l, 0, hh, :], NL4[:, l, 1, hh, :], start=True, stop=True)
                        pe.did(mm, f"L8_{c}_{l}")
                        dve.wait(t, f"Ya{c}_{l}")
                        for hh in range(2):
                            mm = t.matmul(ps[3 * l + 1][:, hh * P:(hh + 1) * P], NL4[:, l, 1, hh, :], Y[:, b, l, hh, :], start=True, stop=True)
                        pe.did(mm, f"dYb{c}_{l}")
                    for l in range(2):
                        act.wait(t, f"L8_{c}_{l}")
                        dve.wait(t, f"Yb{c}_{l}")
                        for hh in range(2):
                            mm = t.matmul(ps[3 * l + 2][:, hh * P:(hh + 1) * P], L8[:, l, hh, :], Y[:, b, l, hh, :], start=True, stop=True)
                        pe.did(mm, f"dYc{c}_{l}")
                    for l in range(2):
                        dve.wait(t, f"Yc{c}_{l}")
                        for hh in range(2):
                            mm = t.transpose(ps[3 * l + 1][:, hh * P:(hh + 1) * P], Y[:, b, l, hh, :], ident[:, :])
                        pe.did(mm, f"X{c}_{l}")
                    for k in range(1, 4):
                        for l in range(2):
                            pool.wait(t, f"Lk{k}_{c}_{l}")
                            if k > 1:
                                dve.wait(t, f"Y{k - 1}_{c}_{l}")
                            for hh in range(2):
                                mm = t.matmul(ps[3 * l][:, hh * P:(hh + 1) * P], Lk[:, l, hh, :], Y[:, b, l, hh, :], start=True, stop=True)
                            pe.did(mm, f"Z{k}_{c}_{l}")
                        for l in range(2):
                            act.wait(t, f"Z{k}_{c}_{l}")
                            if k == 1:
                                act.wait(t, f"X{c}_{l}")
                            for hh in range(2):
                                mm = t.matmul(ps[3 * l + 2][:, hh * P:(hh + 1) * P], Xi[:, l, hh, :], Zi[:, l, hh, :], start=True, stop=True)
                            if k < 3:
                                for hh in range(2):
                                    mm = t.matmul(ps[3 * l + 2][:, 256 + hh * P:256 + (hh + 1) * P], Zi[:, l, hh, :], Xi[:, l, hh, :], start=True, stop=True)
                            pe.did(mm, f"dY{k}_{c}_{l}")
                for step in range(3):
                    if step == 0:
                        for l in range(2):
                            dve.wait(t, f"Y3_{NT - 1}_{l}")
                    scan(NT - 1, step)

            @block.scalar
            def _(a):
                for m in range(0, 2 * HEADS, 2):
                    act.did(a.activation(hT[:, m, :], qkvT[:, m, :], ACT.Square), f"sq{m}")
                act.did(a.activation(beta[:, :, :], gates[:, :, 0:HEADS], ACT.Sigmoid), "beta")
                dve.wait(a, "absx")
                a.wait_ge(hp_land, 32)
                act.did(a.activation(hp[:, 1, :], hp[:, 1, :], ACT.Exp))
                pool.wait(a, "masks")
                act.did(a.activation(sp_t[:, 1], sp_t[:, 0], ACT.Abs))
                act.drain(a)
                act.did(a.activation(sp_t[:, 1], sp_t[:, 1], ACT.Exp, scale=-1.0))
                act.drain(a)
                act.did(a.activation(sp_t[:, 1], sp_t[:, 1], ACT.Ln, bias=1.0), "ln")
                pe.wait(a, "ss_rows")
                for x in range(3):
                    act.did(a.activation(sqT[0:8, x * SEG:(x + 1) * SEG], ps[2 + x][0:8, 0:SEG], ACT.Copy), "ss_rows")
                dve.wait(a, "rs")
                act.did(a.activation(rn[:, 0:NT], rn[:, 0:NT], ACT.Sqrt))
                act.did(a.activation(rn[0:DEC, NT], rn[0:DEC, NT], ACT.Sqrt), "rs")
                dve.wait(a, "Gc")
                act.did(a.activation(nbe[:, :, :], Gc[:, :, :], ACT.Exp), "nbe")

                def scan_u(c):
                    if c >= 0:
                        for l in range(2):
                            pe.wait(a, f"u{c}_{l}")
                            act.did(a.activation(u[:, l].rearrange("p h n -> p (h n)"), ps[6 + l][:, 256:512], ACT.Copy), f"u{c}_{l}")

                def flat(x):
                    return x.rearrange("p h n -> p (h n)")

                for c in range(NT):
                    b = c % 2
                    for l in range(2):
                        pe.wait(a, f"Gb{c}_{l}")
                        dve.wait(a, f"R{c}_{l}")
                        if c > 0:
                            pool.wait(a, f"qg{c - 1}_{l}")
                        act.did(a.activation(flat(egb[:, l]), ps[3 * l + 1][:, 0:256], ACT.Exp), f"egb{c}_{l}")
                        act.did(a.activation(flat(D1[:, l]), flat(D1[:, l]), ACT.Exp))
                        act.did(a.activation(flat(D0[:, l]), flat(D0[:, l]), ACT.Exp, scale=-1.0), f"D{c}_{l}")
                    for l in range(2):
                        pe.wait(a, f"kTn{c}_{l}")
                        act.did(a.activation(flat(kTn[:, b, l]), ps[3 * l + 2][:, 0:256], ACT.Copy), f"kTn{c}_{l}")
                    scan_u(c - 1)
                    for l in range(2):
                        pe.wait(a, f"N{c}_{l}")
                        act.did(a.activation(flat(N[:, l]), ps[3 * l + 2][:, 0:256], ACT.Copy), f"N{c}_{l}")
                    for l in range(2):
                        pe.wait(a, f"NL2_{c}_{l}")
                        act.did(a.activation(NL2[:, l].rearrange("p k h n -> p (k h n)"), ps[3 * l][:, :], ACT.Copy), f"NL2_{c}_{l}")
                    for l in range(2):
                        pe.wait(a, f"NL4_{c}_{l}")
                        act.did(a.activation(NL4[:, l].rearrange("p k h n -> p (k h n)"), ps[3 * l][:, :], ACT.Copy), f"NL4_{c}_{l}")
                    for l in range(2):
                        pe.wait(a, f"L8_{c}_{l}")
                        act.did(a.activation(flat(L8[:, l]), ps[3 * l][:, 0:256], ACT.Copy), f"L8_{c}_{l}")
                    for l in range(2):
                        pe.wait(a, f"X{c}_{l}")
                        act.did(a.activation(flat(Xi[:, l]), ps[3 * l + 1][:, 0:256], ACT.Copy), f"X{c}_{l}")
                    for k in range(1, 4):
                        for l in range(2):
                            pe.wait(a, f"Z{k}_{c}_{l}")
                            act.did(a.activation(flat(Zi[:, l]), ps[3 * l][:, 0:256], ACT.Copy), f"Z{k}_{c}_{l}")
                scan_u(NT - 1)

            @block.vector
            def _(v):
                v.wait_ge(hp_land, 32)
                dve.did(v.tensor_tensor(sp_t[:, 0], gates[:, :, 4:8], bc(hp[:, 0, :], [P, 9, HEADS], 1), ALU.add), "absx")
                for m in range(1, 2 * HEADS, 2):
                    dve.did(v.tensor_tensor(hT[:, m, :], qkvT[:, m, :], qkvT[:, m, :], ALU.mult), f"sq{m}")
                act.wait(v, "ln")
                dve.did(v.tensor_scalar(sp_t[:, 0], sp_t[:, 0], 0.0, None, ALU.max))
                dve.drain(v)
                dve.did(v.tensor_tensor(sp_t[:, 0], sp_t[:, 0], sp_t[:, 1], ALU.add))
                dve.drain(v)
                dve.did(v.scalar_tensor_tensor(out=gg[:, :, :], in0=sp_t[:, 0], scalar=-1.0, in1=bc(hp[:, 1, :], [P, 9, HEADS], 1),
                                               op0=ALU.mult, op1=ALU.mult), "gg")
                pool.wait(v, "masks")
                pe.wait(v, f"ss{2 * HEADS - 1}")
                dve.did(v.tensor_scalar(rn[:, 0:NT].rearrange("p i m -> p (i m)"), ps[0][:, 0:64], EPS, None, ALU.add))
                dve.did(v.tensor_scalar(rn[0:DEC, NT], ps[0][0:DEC, 64:72], EPS, None, ALU.add), "rs")
                act.wait(v, "rs")
                for rows, s in ((rn[:, 0:NT], P), (rn[0:DEC, NT:NT + 1], DEC)):
                    dve.did(v.reciprocal(rows, rows))
                    dve.drain(v)
                    dve.did(v.tensor_scalar(rows[:, :, 0:HEADS], rows[:, :, 0:HEADS], float(P) ** -0.5, None, ALU.mult), "rn")
                pe.wait(v, "G")
                dve.did(v.tensor_copy(Gc[:, :, :].rearrange("p c h -> p (c h)"), ps[1][:, 0:NT * HEADS]), "Gc")
                act.wait(v, "nbe")
                act.wait(v, "beta")
                dve.did(v.scalar_tensor_tensor(out=nbe[:, :, :], in0=nbe[:, :, :], scalar=-1.0, in1=beta[:, 0:NT, :], op0=ALU.mult, op1=ALU.mult))
                dve.drain(v)

                def two(ap):
                    return ap.rearrange("p (h n) -> p h n", h=2)

                def scan_r(c):
                    if c >= 0:
                        for l in range(2):
                            pe.wait(v, f"ks{c}_{l}")
                            for hh in range(2):
                                h = 2 * l + hh
                                dve.did(v.scalar_tensor_tensor(out=r[:, l, hh, :], in0=ps[6 + l][:, hh * P:(hh + 1) * P], scalar=nbe[:, c, h:h + 1],
                                                               in1=vb[:, c % 2, l, hh, :], op0=ALU.mult, op1=ALU.add), f"r{c}_{l}")

                def scan_s(c):
                    if c == 4:
                        v.wait_ge(zland, 16 * (SLOTS // 2 + 2))
                    if c >= 0:
                        for l in range(2):
                            pe.wait(v, f"o{c}_{l}")
                            dve.did(v.tensor_tensor(two(Og[:, c, l * 256:(l + 1) * 256]), two(ps[6 + l][:, 256:512]),
                                                    bc(rn[:, c, 2 * l:2 * l + 2], [P, 2, P]), ALU.mult))
                            for hh in range(2):
                                h = 2 * l + hh
                                dve.did(v.scalar_tensor_tensor(out=S[:, h, :], in0=S[:, h, :], scalar=egl[:, c % 2, h:h + 1],
                                                               in1=ps[6 + l][:, hh * P:(hh + 1) * P], op0=ALU.mult, op1=ALU.add), f"S{c}_{l}")

                for c in range(NT):
                    b = c % 2
                    for l in range(2):
                        hs = slice(2 * l, 2 * l + 2)
                        pe.wait(v, f"kv{c}_{l}")
                        if c > 0:
                            pool.wait(v, f"kd{c - 1}_{l}")
                        dve.did(v.tensor_tensor(kn[:, l], two(ps[3 * l][:, 0:256]), bc(rn[:, c, 4 + 2 * l:6 + 2 * l], [P, 2, P]), ALU.mult), f"kn{c}_{l}")
                        dve.did(v.tensor_tensor(vb[:, b, l], two(ps[3 * l][:, 256:512]), bc(beta[:, c, hs], [P, 2, P]), ALU.mult), f"vb{c}_{l}")
                        pe.wait(v, f"Gb{c}_{l}")
                        dve.did(v.tensor_tensor(R[:, l], two(ps[3 * l + 1][:, 0:256]), bc(Gc[:, c, hs], [P, 2, P]), ALU.subtract))
                        dve.drain(v)
                        dve.did(v.scalar_tensor_tensor(out=D1[:, l], in0=R[:, l], scalar=0.0, in1=bc(neg_lo[:, :], [P, 2, P], 1), op0=ALU.min, op1=ALU.add))
                        dve.did(v.scalar_tensor_tensor(out=D0[:, l], in0=R[:, l], scalar=0.0, in1=bc(big_up[:, :], [P, 2, P], 1), op0=ALU.max, op1=ALU.add), f"R{c}_{l}")
                    scan_r(c - 1)
                    for l in range(2):
                        pe.wait(v, f"kk{c}_{l}")
                        act.wait(v, f"D{c}_{l}")
                        if c > 0:
                            pool.wait(v, f"Lk3_{c - 1}_{l}")
                        for hh in range(2):
                            h = 2 * l + hh
                            dve.did(v.scalar_tensor_tensor(out=L[:, l, hh, :], in0=ps[3 * l][:, hh * P:(hh + 1) * P], scalar=beta[:, c, h:h + 1],
                                                           in1=D0[:, l, hh, :], op0=ALU.mult, op1=ALU.mult), f"L{c}_{l}")
                        dve.did(v.tensor_tensor(at[:, b, l], two(ps[3 * l][:, 256:512]), D1[:, l], ALU.mult), f"at{c}_{l}")
                    for l in range(2):
                        act.wait(v, f"N{c}_{l}")
                        dve.did(v.tensor_tensor(NL1[:, l, 0], N[:, l], bc(bd[:, 0, :], [P, 2, P], 1), ALU.mult))
                        dve.drain(v)
                        dve.did(v.tensor_tensor(Y[:, b, l], bc(ident[:, :], [P, 2, P], 1), NL1[:, l, 0], ALU.subtract), f"Y0_{c}_{l}")
                    scan_s(c - 1)

                    def add(name, bank, sign=ALU.add):
                        for l in range(2):
                            pe.wait(v, f"d{name}{c}_{l}")
                            dve.did(v.tensor_tensor(Y[:, b, l], Y[:, b, l], two(ps[3 * l + bank][:, 0:256]), sign), f"{name}{c}_{l}")
                    add("Ya", 1)
                    add("Yb", 1)
                    add("Yc", 2)
                    for k in range(1, 4):
                        for l in range(2):
                            pe.wait(v, f"dY{k}_{c}_{l}")
                            if k < 3:
                                dve.did(v.tensor_tensor(Xi[:, l], Xi[:, l], two(ps[3 * l + 2][:, 256:512]), ALU.subtract))
                            dve.did(v.tensor_tensor(Y[:, b, l], Y[:, b, l], two(ps[3 * l + 2][:, 0:256]), ALU.subtract), f"Y{k}_{c}_{l}")
                scan_r(NT - 1)
                scan_s(NT - 1)
        ad = small[0:DEC, 32:36]
        s_in_land = sem("gdn_state_in")
        pe, act, dve, pool = steps("s3d_pe"), steps("s3d_act"), steps("s3d_dve"), steps("s3d_pool")
        hflat = hT[:, :, :].rearrange("p k t -> p (k t)")
        Sd = qkvT[:, 0:DEC, 0:GW].rearrange("p b (h v) -> p b h v", h=HEADS)
        Km = qkvT[0:DEC, 2 * HEADS:MQ, 0:SEQ].rearrange("p h (b n) -> p h b n", b=DEC)
        d8 = sqT[:, 0:64].rearrange("p (b c) -> p b c", b=DEC)
        kcol = sqT[:, 64:320].rearrange("p (h b c) -> p h b c", h=HEADS, b=DEC)
        qcol = sqT[:, 320:576].rearrange("p (h b c) -> p h b c", h=HEADS, b=DEC)
        a8 = sqT[0:DEC, 576:608].rearrange("p (h b) -> p h b", h=HEADS)
        abc = sqT[:, 608:640].rearrange("p (h b) -> p h b", h=HEADS)
        ones8 = sqT[0:DEC, 640:768]
        vd = NL2[0:DEC, 0].rearrange("p a b n -> p (a b n)")
        knd = NL2[0:DEC, 1].rearrange("p a b n -> p (a b n)")
        ud = NL4[0:DEC, 0].rearrange("p a b n -> p (a b n)")
        with nc.Block() as block:
            @block.sync
            def _(sp):
                for b in range(DEC):
                    sp.dma_start(Sd[:, b], A["state_gdn"][0, b].rearrange("h k v -> k h v")).then_inc(s_in_land, 16)
                for b in range(DEC):
                    dve.wait(sp, f"S{b}")
                    sp.dma_start(O["gdn_s"][0, b].rearrange("h k v -> k h v"), Sd[:, b]).then_inc(s_out, 16)
                sp.wait_ge(s_out, 16 * (1 + DEC))

            @block.gpsimd
            def _(g):
                pool.did(g.memset(d8, 1.0))
                pool.did(g.memset(ones8, 1.0))
                pool.drain(g)
                pool.did(g.affine_select(out=d8, in_=d8, compare_op=ALU.is_equal, fill=0.0, base=0,
                                         pattern=[[1, DEC], [-1, DEC]], channel_multiplier=0))
                pool.drain(g)
                for h in range(HEADS):
                    for col, m in ((kcol, HEADS + h), (qcol, h)):
                        pool.did(g.tensor_tensor(col[:, h], bc(qkvT[:, m, SEQ:T], [P, DEC, DEC]), d8, ALU.mult), "cols")

            @block.scalar
            def _(a):
                act.did(a.activation(ad, gg[0:DEC, NT, :], ACT.Exp), "ad")
                dve.wait(a, "ssq")
                act.did(a.activation(sp_t[:, 0, 0:NT], sp_t[:, 0, 0:NT], ACT.Sqrt), "rms")
                for i in range(9):
                    n = P if i < NT else DEC
                    if i == NT:
                        dve.wait(a, "ssq8")
                        act.did(a.activation(sp_t[0:DEC, 0, NT], sp_t[0:DEC, 0, NT], ACT.Sqrt), "rms8")
                    pe.wait(a, f"oT{i}")
                    act.did(a.activation(hT[:, 0:HEADS, i * P:i * P + n], ps[i % 4][:, :].rearrange("p (h n) -> p h n", h=HEADS)[:, :, 0:n],
                                         ACT.Copy, scale=vecT[:, GNG:GNG + 1]), f"oT{i}")

            @block.tensor
            def _(t):
                def out_transposes(i):
                    n = P if i < NT else DEC
                    dve.wait(t, f"on{i}")
                    if i >= 4:
                        act.wait(t, f"oT{i - 4}")
                    for h in range(HEADS):
                        mm = t.transpose(ps[i % 4][:, h * P:h * P + n], Og[0:n, i, h * P:(h + 1) * P], ident[0:n, 0:n])
                    pe.did(mm, f"oT{i}")

                for h in range(HEADS):
                    t.transpose(ps[0][0:DEC, h * P:(h + 1) * P], qkvT[:, 2 * HEADS + h, SEQ:T], ident[:, :])
                    mm = t.transpose(ps[1][0:DEC, h * P:(h + 1) * P], qkvT[:, HEADS + h, SEQ:T], ident[:, :])
                pe.did(mm, "rows")
                dve.wait(t, "a8")
                pool.wait(t, "cols")
                pe.did(t.matmul(ps[2][:, 0:32], ones8, a8.rearrange("p h b -> p (h b)"), start=True, stop=True), "abc")
                t.wait_ge(s_in_land, 16 * DEC)
                pool.wait(t, "cols")
                for h in range(HEADS):
                    for b in range(DEC):
                        mm = t.matmul(ps[3][0:DEC, h * P:(h + 1) * P], kcol[:, h, b, :], Sd[:, b, h, :], start=(b == 0), stop=(b == DEC - 1))
                pe.did(mm, "kS")
                dve.wait(t, "ud")
                for b in range(DEC):
                    if b >= 2:
                        out_transposes(b - 2)
                    if b >= 4:
                        dve.wait(t, f"S{b - 4}")
                    for h in range(HEADS):
                        mm = t.matmul(ps[4 + b % 4][:, h * P:(h + 1) * P], Km[:, h, b, :], ud[:, h * P:(h + 1) * P], start=True, stop=True)
                    pe.did(mm, f"outer{b}")
                out_transposes(6)
                out_transposes(7)
                dve.wait(t, "Snew")
                act.wait(t, "oT6")
                for h in range(HEADS):
                    for b in range(DEC):
                        mm = t.matmul(ps[2][0:DEC, h * P:(h + 1) * P], qcol[:, h, b, :], Sd[:, b, h, :], start=(b == 0), stop=(b == DEC - 1))
                pe.did(mm, "qS")
                out_transposes(8)

            @block.vector
            def _(v):
                def heads(ap):
                    return ap.rearrange("p (h n) -> p h n", h=HEADS)

                sqv = qkvT[:, 0:NT, GW:2 * GW]
                sqd = kn[:, :].rearrange("p l h n -> p (l h) n")

                def squares(tiles, n, name):
                    x = Og[0:n, tiles, :].rearrange("p i (h n) -> p i h n", h=HEADS)
                    y = sqv.rearrange("p i (h n) -> p i h n", h=HEADS) if n == P else sqd[0:n].unsqueeze(1)
                    ms = sp_t[0:n, 0, tiles, :]
                    if n == P:
                        dve.did(v.tensor_tensor(sqv, Og[:, tiles, :], Og[:, tiles, :], ALU.mult))
                        dve.drain(v)
                        dve.did(v.tensor_reduce(ms, y, AX.X, ALU.add))
                    else:
                        dve.did(v.tensor_tensor(sqd[0:n], heads(Og[0:n, NT, :]), heads(Og[0:n, NT, :]), ALU.mult))
                        dve.drain(v)
                        dve.did(v.tensor_reduce(sp_t[0:n, 0, NT, :], sqd[0:n], AX.X, ALU.add))
                    dve.drain(v)
                    dve.did(v.tensor_scalar(ms, ms, 1.0 / P, EPS, ALU.mult, ALU.add), name)

                def inverse(tiles, n):
                    dve.did(v.reciprocal(sp_t[0:n, 0, tiles, :], sp_t[0:n, 0, tiles, :]))
                    dve.drain(v)

                def gated_norm(i):
                    n = P if i < NT else DEC
                    dve.did(v.tensor_tensor(heads(Og[0:n, i, :]), heads(Og[0:n, i, :]), bc(sp_t[0:n, 0, i, :], [n, HEADS, P]), ALU.mult))
                    dve.drain(v)
                    dve.did(v.tensor_tensor(Og[0:n, i, :], Og[0:n, i, :], Z[0:n, i, :], ALU.mult), f"on{i}")

                act.wait(v, "ad")
                dve.did(v.tensor_tensor(a8, bc(ad, [DEC, HEADS, DEC]), bc(ident[0:DEC, 0:DEC], [DEC, HEADS, DEC], 1), ALU.mult), "a8")
                pe.wait(v, "rows")
                dve.did(v.tensor_copy(vd, ps[0][0:DEC, :]))
                dve.did(v.tensor_tensor(heads(knd), heads(ps[1][0:DEC, :]), bc(rn[0:DEC, NT, 4:8], [DEC, HEADS, P]), ALU.mult))
                dve.drain(v)
                for h in range(HEADS):
                    dve.did(v.tensor_tensor(Km[:, h], bc(knd[:, h * P:(h + 1) * P], [DEC, DEC, P], 1), bc(ident[0:DEC, 0:DEC], [DEC, DEC, P]), ALU.mult))
                pe.wait(v, "abc")
                dve.did(v.tensor_copy(abc, ps[2][:, 0:32].rearrange("p (h b) -> p h b", h=HEADS)))
                squares(slice(0, NT), P, "ssq")
                dve.did(v.tensor_tensor(small[0:DEC, 36:40], ad, rn[0:DEC, NT, 4:8], ALU.mult))
                pe.wait(v, "kS")
                dve.drain(v)
                dve.did(v.tensor_tensor(heads(ud), heads(ps[3][0:DEC, :]), bc(small[0:DEC, 36:40], [DEC, HEADS, P]), ALU.mult))
                dve.drain(v)
                dve.did(v.tensor_tensor(ud, vd, ud, ALU.subtract))
                dve.drain(v)
                dve.did(v.tensor_tensor(heads(ud), heads(ud), bc(beta[0:DEC, NT, :], [DEC, HEADS, P]), ALU.mult), "ud")
                for b in range(DEC):
                    pe.wait(v, f"outer{b}")
                    for h in range(HEADS):
                        dve.did(v.scalar_tensor_tensor(out=Sd[:, b, h, :], in0=Sd[:, b, h, :], scalar=abc[:, h, b:b + 1],
                                                       in1=ps[4 + b % 4][:, h * P:(h + 1) * P], op0=ALU.mult, op1=ALU.add), f"S{b}")
                    if b == 0:
                        act.wait(v, "rms")
                        inverse(slice(0, NT), P)
                    gated_norm(b)
                dve.at["Snew"] = dve.at["S7"]
                pe.wait(v, "qS")
                dve.did(v.tensor_tensor(heads(Og[0:DEC, NT, :]), heads(ps[2][0:DEC, :]), bc(rn[0:DEC, NT, 0:4], [DEC, HEADS, P]), ALU.mult))
                dve.drain(v)
                squares(slice(NT, 9), DEC, "ssq8")
                act.wait(v, "rms8")
                inverse(slice(NT, 9), DEC)
                gated_norm(NT)
        s3.close()

        mid2.close()

        s4 = ctx.enter_context(ExitStack())
        t4 = lambda name, shape: s4.enter_context(nc.sbuf_tensor(name, shape, F32))
        y1T = t4("y1T", [P, 4, T])
        Yt = t4("Yt", [P, 9, GW])
        s4a = ctx.enter_context(ExitStack())
        t4 = lambda name, shape: s4a.enter_context(nc.sbuf_tensor(name, shape, F32))
        X0r, X0i = t4("X0r", [P, GROUPS, DEC]), t4("X0i", [P, GROUPS, DEC])
        X1 = t4("X1", [P, DEC, GROUPS])
        Ec2, Es2 = t4("Ec", [P, 2, NG, NCH + 1]), t4("Es", [P, 2, NG, NCH + 1])
        e1, e2 = t4("e1", [P, NG, NCH // 2]), t4("e2", [P, NG, NCH // 2])
        e3, e4 = t4("e3", [P, NG, NCH // 2]), t4("e4", [P, NG, NCH // 2])
        W = t4("W", [P, NG, LAGS, CH])
        Wt = t4("Wt", [P, NG, LAGS + 1, CH])
        CL2 = t4("CL", [P, 2, NG, LAGS + 1, CH])
        CS2 = t4("CS", [P, 2, NG, LAGS, CH])
        BM, BS = t4("BM", [P, NG, P]), t4("BS", [P, NG, P])
        Kt = t4("Kt", [CH, NG, LAGS, CH])
        TT = t4("TT", [P, NG, LAGS, CH])
        U = t4("U", [P, NG, P])
        Ud = t4("Ud", [P, NG, 2, DEC])
        Vq = t4("Vq", [DEC, NG, 2 * LAGS - 1, CH])
        zin = t4("zin", [P, NG, NCH])
        z2 = t4("z2", [P, NG, NCH])
        zs = t4("zs", [P, NG, NCH + 1])
        Zc, Zs = t4("Zc", [P, NG, NCH]), t4("Zs", [P, NG, NCH])
        ada_col = [y1T[:, :, :].rearrange("p k n -> p (k n)")[:, 0:KD * 512].rearrange("p (k n) -> p k n", k=KD), 
                   hT[:, 4:8, :].rearrange("p k n -> p (k n)")[:, 0:KD * 512].rearrange("p (k n) -> p k n", k=KD)]
        ada_col_land = [sem("ada_col_land0"), sem("ada_col_land1")]
        ada_row = z2[0:9, :, :].rearrange("p g n -> p (g n)")

        def load_ada(sp, c):
            sp.dma_start(ada_col[c % 2][:, :, :], w_ada[:, :, (4 + c) * 512:(5 + c) * 512]).then_inc(ada_col_land[c % 2], 16)

        zl = t4("zl", [P, 2, GROUPS])
        xrow = t4("xrow", [P, 2, P])
        prow = t4("prow", [GROUPS, P])
        tt_land, s5_out = sem("tt_land"), sem("s5_out")
        pe, act, dve, pool = steps("s4_pe"), steps("s4_act"), steps("s4_dve"), steps("s4_pool")

        with nc.Block() as block:
            @block.sync
            def _(sp):
                for c in range(2):
                    load_ada(sp, c)
                for q in range(4):
                    dve.wait(sp, f"K{q}")
                    if q == 0:
                        pool.wait(sp, "clear")
                    else:
                        pe.wait(sp, f"y{q - 1}")
                    for j in range(LAGS):
                        sp.dma_start(TT[j * CH:(j + 1) * CH, :, j:LAGS, :], Kt[:, :, 0:LAGS - j, :]).then_inc(tt_land, 16)
                    for c in (2 * q + 2, 2 * q + 3):
                        if c < 8:
                            pe.wait(sp, f"ada{c - 2}")
                            load_ada(sp, c)
                act.wait(sp, "states")
                for n, (p_out, s_out_) in enumerate((("re_p", "re_s"), ("im_p", "im_s"))):
                    sp.dma_start(O[p_out][0, 0], prow[:, n * ST:(n + 1) * ST]).then_inc(s5_out, 16)
                    sp.dma_start(O[s_out_][0].rearrange("(x b) g p -> (b g) x p", x=2), xrow[:, :, n * ST:(n + 1) * ST]).then_inc(s5_out, 16)
                sp.wait_ge(s5_out, 64)

            @block.gpsimd
            def _(g):
                pool.did(g.memset(TT[:, :, :, :], 0.0))
                pool.did(g.memset(Vq[:, :, :, :], 0.0))
                pool.did(g.memset(zs[:, :, 0:1], 0.0))
                pool.did(g.memset(Ec2[:, :, :, 0:1], 1.0))
                pool.did(g.memset(Es2[:, :, :, 0:1], 0.0), "clear")
                def phases(q):
                    Ec, Es = Ec2[:, q % 2], Es2[:, q % 2]
                    if q >= 2:
                        dve.wait(g, f"zc{q - 2}")
                    pool.drain(g)
                    pool.did(g.tensor_copy(Es[:, :, 1:2], ph[:, 1, q * NG:(q + 1) * NG].unsqueeze(2)), f"e{q}_0")
                    w = 1
                    while w < NCH:
                        step = w.bit_length()
                        dve.wait(g, f"e{q}_{step - 1}")
                        pool.drain(g)
                        cw, sw = (x[:, :, w:w + 1].to_broadcast([P, NG, w]) for x in (Ec, Es))
                        pool.did(g.tensor_tensor(e3[:, :, 0:w], Ec[:, :, 1:w + 1], sw, ALU.mult))
                        pool.did(g.tensor_tensor(e4[:, :, 0:w], Es[:, :, 1:w + 1], cw, ALU.mult))
                        pool.drain(g)
                        pool.did(g.tensor_tensor(Es[:, :, w + 1:2 * w + 1], e3[:, :, 0:w], e4[:, :, 0:w], ALU.add), f"e{q}_{step}")
                        w *= 2
                phases(0)
                for q in range(4):
                    gs, Es = slice(q * NG, (q + 1) * NG), Es2[:, q % 2]
                    for bnk in range(2):
                        dve.wait(g, f"rot{q}_{bnk}")
                        part = slice(4 * bnk, 4 * bnk + 4)
                        pool.did(g.tensor_tensor(zin[:, part], zin[:, part], z2[:, part], ALU.add), f"zin{q}_{bnk}")
                    dve.wait(g, f"scan{q}")
                    if q > 0:
                        pe.wait(g, f"y{q - 1}")
                    pool.did(g.tensor_tensor(Zs[:, :, :], zs[:, :, 0:NCH], Es[:, :, 0:NCH], ALU.mult), f"zs{q}")
                    pool.did(g.tensor_tensor(zl[:, 1, gs], zs[:, :, NCH], Es[:, :, NCH], ALU.mult), f"zl{q}")
                    if q < 3:
                        phases(q + 1)

            @block.tensor
            def _(t):
                pool.wait(t, "clear")
                for q in range(4):
                    gs, CL, CS = [q * NG + x for x in range(NG)], CL2[:, q % 2], CS2[:, q % 2]
                    if q > 0:
                        dve.wait(t, f"rot{q - 1}_1")
                    dve.wait(t, f"W{q}")
                    for x in range(NG):
                        mm = t.transpose(ps[x // 4][:, (x % 4) * P:(x % 4 + 1) * P], W[:, x].rearrange("p j c -> p (j c)"), ident[:, :])
                    pe.did(mm, f"BM{q}")
                    for x in range(NG):
                        mm = t.transpose(ps[2 + x // 4][:, (x % 4) * P:(x % 4 + 1) * P],
                                         V[:, gs[x]].rearrange("p j c -> p (j c)"), ident[:, :])
                    dve.wait(t, f"Vq{q}")
                    if q > 0:
                        act.wait(t, f"yd{q - 1}")
                    for x in range(NG):
                        for v_ in range(2):
                            sl = slice(LAGS - 1, 2 * LAGS - 1) if v_ == 0 else slice(0, LAGS)
                            mm = t.transpose(ps[6][:, (2 * x + v_) * DEC:(2 * x + v_ + 1) * DEC],
                                             Vq[:, x, sl, :].rearrange("b j c -> b (j c)"), ident[0:DEC, 0:DEC])
                    pe.did(mm, f"U{q}")
                    if q > 0:
                        act.wait(t, f"yp{q - 1}")
                    dve.wait(t, f"CL{q}")
                    for x in range(NG):
                        mm = t.matmul(ps[4 + x // 4][0:CH, (x % 4) * P:(x % 4 + 1) * P], Bb[:, gs[x], :],
                                      CL[:, x, 0:LAGS, :].rearrange("p k c -> p (k c)"), start=True, stop=True)
                    pe.did(mm, f"K{q}")
                    act.wait(t, f"BM{q}")
                    act.wait(t, f"U{q}")
                    for x in range(NG):
                        t.matmul(ps[x // 4][:, (x % 4) * P:(x % 4 + 1) * P], BM[:, x, :], U[:, x, :], start=True, stop=True)
                        mm = t.matmul(ps[2 + x // 4][:, (x % 4) * P:(x % 4 + 1) * P], BS[:, x, :], U[:, x, :], start=True, stop=True)
                    pe.did(mm, f"b{q}")
                    dve.wait(t, "x0")
                    if q > 0:
                        act.wait(t, f"x1_{q - 1}")
                        dve.wait(t, f"mod{q - 1}")
                    lo, hi = q * NG, (q + 1) * NG
                    reg = ps[7][:, 0:NG * DEC]
                    t.matmul(reg, ident[:, :], X0r[:, lo:hi, :].rearrange("p g b -> p (g b)"), start=True, stop=False, skip_group_check=True)
                    t.matmul(reg, J[:, :], X0i[:, lo:hi, :].rearrange("p g b -> p (g b)"), start=False, stop=False, skip_group_check=True)
                    for x in range(NG):
                        mm = t.matmul(ps[7][:, x * DEC:(x + 1) * DEC], BM[:, x, :], Ud[:, x, 1, :], start=False, stop=(x == NG - 1), skip_group_check=True)
                    pe.did(mm, f"x1_{q}")
                    if q > 0:
                        act.wait(t, f"yp{q - 1}")
                    dve.wait(t, f"K{q}")
                    for c in (2 * q, 2 * q + 1):
                        t.wait_ge(ada_col_land[c % 2], 16 * (q + 1))
                        for k in range(KD):
                            mm = t.matmul(ps[4 + c % 2][0:9, :], cT[:, k, :], ada_col[c % 2][:, k, :], start=(k == 0), stop=(k == KD - 1))
                        pe.did(mm, f"ada{c}")
                    act.wait(t, f"ada_row{q}")
                    dve.wait(t, f"zc{q}")
                    pool.wait(t, f"zs{q}")
                    dve.wait(t, f"K{q}")
                    t.wait_ge(tt_land, 16 * LAGS * (q + 1))
                    for x in range(NG):
                        dst = ps[4 + x // 4][:, (x % 4) * P:(x % 4 + 1) * P]
                        t.matmul(dst, U[:, x, :], TT[:, x].rearrange("p j c -> p (j c)"), start=True, stop=False)
                        t.matmul(dst, Zc[:, x, :], CL[:, x, 1:LAGS + 1, :].rearrange("p k c -> p (k c)"), start=False, stop=False)
                        mm = t.matmul(dst, Zs[:, x, :], CS[:, x].rearrange("p k c -> p (k c)"), start=False, stop=True)
                    pe.did(mm, f"yp{q}")
                    act.wait(t, f"x1_{q}")
                    for n in range(8):
                        mm = t.transpose(ps[7][:, 256 + 9 * n:256 + 9 * n + 9], ada_row[:, n * P:(n + 1) * P], ident[0:9, 0:9])
                    pe.did(mm, f"adaT{q}")
                    for x in range(NG):
                        dst = ps[6][0:DEC, x * CH:(x + 1) * CH]
                        t.matmul(dst, Ud[:, x, 0, :], TT[:, x, 0, :], start=True, stop=False)
                        mm = t.matmul(dst, X0[:, gs[x], :], CL[:, x, 1, :], start=False, stop=True)
                    pe.did(mm, f"y{q}")
                act.wait(t, "x1_3")
                pool.wait(t, "zl3")
                t.matmul(ps[0][0:GROUPS, 0:P], zl[:, 0, :], ident[:, :], start=True, stop=False)
                t.matmul(ps[0][0:GROUPS, 0:P], zl[:, 1, :], J[:, :], start=False, stop=True)
                for n in range(2):
                    mm = t.transpose(ps[1][:, n * P:(n + 1) * P], X1[:, 4 * n:4 * n + 4, :].rearrange("p b g -> p (b g)"), ident[:, :])
                pe.did(mm, "states")

            @block.scalar
            def _(a):
                for q in range(4):
                    pe.wait(a, f"BM{q}")
                    if q > 0:
                        pe.wait(a, f"x1_{q - 1}")
                    for bnk in range(2):
                        src = ps[bnk][:, :].rearrange("p (g n) -> p g n", g=4)
                        part = slice(4 * bnk, 4 * bnk + 4)
                        act.did(a.activation(BM[:, part, :], src, ACT.Copy))
                        act.did(a.activation(BS[:, part, 0:ST], src[:, :, ST:P], ACT.Copy))
                        act.did(a.activation(BS[:, part, ST:P], src[:, :, 0:ST], ACT.Copy, scale=-1.0), f"BM{q}")
                    pe.wait(a, f"U{q}")
                    if q > 0:
                        pe.wait(a, f"y{q - 1}")
                    for bnk in range(2):
                        act.did(a.activation(U[:, 4 * bnk:4 * bnk + 4, :].rearrange("p g n -> p (g n)"), ps[2 + bnk][:, :], ACT.Copy))
                    act.did(a.activation(Ud[:, :, :, :].rearrange("p g v b -> p (g v b)"), ps[6][:, 0:2 * NG * DEC], ACT.Copy), f"U{q}")
                    pe.wait(a, f"x1_{q}")
                    act.did(a.activation(X1[:, :, q * NG:(q + 1) * NG].rearrange("p b g -> p g b"),
                                         ps[7][:, 0:NG * DEC].rearrange("p (g b) -> p g b", g=NG), ACT.Copy), f"x1_{q}")
                    pool.wait(a, f"zin{q}_1")
                    for c in range(2):
                        pe.wait(a, f"ada{2 * q + c}")
                        act.did(a.activation(ada_row[:, c * 512:(c + 1) * 512], ps[4 + c][0:9, :], ACT.Copy), f"ada_row{q}")
                    pe.wait(a, f"yp{q}")
                    for bnk in range(2):
                        c0 = (q * NG + 4 * bnk) * CH
                        for x in range(4):
                            act.did(a.activation(Yt[:, 0:LAGS, c0 + x * CH:c0 + (x + 1) * CH],
                                                 ps[4 + bnk][:, x * P:(x + 1) * P].rearrange("p (j c) -> p j c", j=LAGS), ACT.Gelu_apprx_tanh), f"yp{q}")
                    pe.wait(a, f"y{q}")
                    act.did(a.activation(Yt[0:DEC, LAGS, q * P:(q + 1) * P], ps[6][0:DEC, 0:P], ACT.Gelu_apprx_tanh), f"yd{q}")
                pe.wait(a, "states")
                act.did(a.activation(prow[:, :], ps[0][0:GROUPS, 0:P], ACT.Copy))
                act.did(a.activation(xrow[:, :, :].rearrange("p x n -> p (x n)"), ps[1][:, 0:256], ACT.Copy), "states")

            @block.vector
            def _(v):
                def tt(out, x, y, op, name=None, wait=True):
                    if wait:
                        dve.drain(v)
                    dve.did(v.tensor_tensor(out, x, y, op), name)

                tt(X0r[:, :, :], X0[:, :, :], bc(LC[:, 0, :, 1], [P, GROUPS, DEC]), ALU.mult)
                tt(X0i[:, :, :], X0[:, :, :], bc(LC[:, 1, :, 1], [P, GROUPS, DEC]), ALU.mult, "x0")
                def tables(q):
                    gs = slice(q * NG, (q + 1) * NG)
                    CL, CS, Ec, Es = CL2[:, q % 2], CS2[:, q % 2], Ec2[:, q % 2], Es2[:, q % 2]

                    def table(dst, tmp, lam, x, y, n, op, name, first=0):
                        shape = [P, NG, n, CH]
                        lr_, li_ = (lam[:, c, gs, first:first + n].unsqueeze(3).to_broadcast(shape) for c in range(2))
                        tt(dst, lr_, x.unsqueeze(2).to_broadcast(shape), ALU.mult)
                        tt(tmp, li_, y.unsqueeze(2).to_broadcast(shape), ALU.mult)
                        tt(dst, dst, tmp, op, name)
                    if q > 0:
                        pe.wait(v, f"BM{q - 1}")
                    table(W[:, :, :, :], Wt[:, :, 0:LAGS, :], LB, Bb[:, gs, :], B2[:, gs, :], LAGS, ALU.add, f"W{q}")
                    if q > 0:
                        pe.wait(v, f"U{q - 1}")
                    else:
                        pool.wait(v, "clear")
                    dve.did(v.tensor_copy(Vq[:, :, LAGS - 1, :], Vd[:, q * P:(q + 1) * P].rearrange("b (g c) -> b g c", c=CH)), f"Vq{q}")
                    if q >= 2:
                        pe.wait(v, f"y{q - 2}")
                    q1, q2 = (x[:, q, :].rearrange("p (g c) -> p g c", c=CH) for x in (Q1, Q2))
                    table(CL, Wt[:, :, :, :], LC, q1, q2, LAGS + 1, ALU.add, f"CL{q}")
                    table(CS, Wt[:, :, 0:LAGS, :], LC, q2, q1, LAGS, ALU.subtract, None, first=1)
                    if q >= 2:
                        pool.wait(v, f"zl{q - 2}")
                    dve.did(v.tensor_copy(Ec[:, :, 1:2], ph[:, 0, gs].unsqueeze(2)), f"e{q}_0")
                    wd = 1
                    while wd < NCH:
                        step = wd.bit_length()
                        pool.wait(v, f"e{q}_{step - 1}")
                        cw, sw = (x[:, :, wd:wd + 1].to_broadcast([P, NG, wd]) for x in (Ec, Es))
                        tt(e1[:, :, 0:wd], Ec[:, :, 1:wd + 1], cw, ALU.mult)
                        tt(e2[:, :, 0:wd], Es[:, :, 1:wd + 1], sw, ALU.mult, wait=False)
                        tt(Ec[:, :, wd + 1:2 * wd + 1], e1[:, :, 0:wd], e2[:, :, 0:wd], ALU.subtract, f"e{q}_{step}")
                        wd *= 2

                tables(0)
                for q in range(4):
                    gs, Ec, Es = slice(q * NG, (q + 1) * NG), Ec2[:, q % 2], Es2[:, q % 2]
                    pe.wait(v, f"K{q}")
                    if q > 0:
                        v.wait_ge(tt_land, 16 * LAGS * q)
                    for bnk in range(2):
                        dve.did(v.tensor_copy(Kt[:, 4 * bnk:4 * bnk + 4].rearrange("c g k n -> c (g k n)"), ps[4 + bnk][0:CH, :]))
                    sh = [CH, NG, CH]
                    dd = Wt[0:CH, :, 0, :]
                    tt(dd, bc(ident[0:CH, 0:CH], sh, 1), bc(D16[:, gs], sh), ALU.mult)
                    tt(Kt[:, :, 0, :], Kt[:, :, 0, :], dd, ALU.add, f"K{q}")
                    pe.wait(v, f"b{q}")
                    pool.wait(v, f"e{q}_7")
                    for bnk in range(2):
                        part = slice(4 * bnk, 4 * bnk + 4)
                        src, turned = (ps[x + bnk][:, :].rearrange("p (g n) -> p g n", g=4) for x in (0, 2))
                        tt(zin[:, part], src, Ec[:, part, 1:NCH + 1], ALU.mult)
                        tt(z2[:, part], turned, Es[:, part, 1:NCH + 1], ALU.mult, f"rot{q}_{bnk}")
                    if q > 0:
                        pool.wait(v, f"zl{q - 1}")
                    for x in range(NG):
                        pool.wait(v, f"zin{q}_{x // 4}")
                        dve.did(v.tensor_tensor_scan(zs[:, x, 1:NCH + 1], rho[:, q * NG + x:q * NG + x + 1].to_broadcast([P, NCH]),
                                                     zin[:, x, :], 0.0, ALU.mult, ALU.add), f"scan{q}")
                    if q > 0:
                        pe.wait(v, f"y{q - 1}")
                    tt(Zc[:, :, :], zs[:, :, 0:NCH], Ec[:, :, 0:NCH], ALU.mult)
                    tt(zl[:, 0, gs], zs[:, :, NCH], Ec[:, :, NCH], ALU.mult, f"zc{q}")
                    if q < 3:
                        tables(q + 1)
                    pe.wait(v, f"adaT{q}")
                    m0 = 16 + 8 * q
                    dve.did(v.tensor_tensor(modT[:, m0:m0 + 8, :], ps[7][:, 256:328].rearrange("p (m n) -> p m n", m=8),
                                            bc(vecT[:, B_ADA + m0:B_ADA + m0 + 8], [P, 8, 9]), ALU.add), f"mod{q}")
        s4a.close()

        X2 = sb("X2", [P, 9, D])
        combine = sb("combine", [P, 9, 2])
        pos = sb("pos", [P, 9, 2], U32)
        slot_t = sb("slot_t", [1, SLOTS, 3], I32)
        exp_t = sb("exp_t", [1, EXPERTS + 3], I32)
        w_out = sb("w_out", [P, KD, D])
        w_r = sb("w_r", [P, KD, EXPERTS])
        b_r = sb("b_r", [P, EXPERTS])
        land6, rland = sem("land6"), sem("rland")
        s5s = ctx.enter_context(ExitStack())
        t5 = lambda name, shape: s5s.enter_context(nc.sbuf_tensor(name, shape, F32))
        glu_w, glu_b = t5("glu_w", [P, 4, GW]), t5("glu_b", [P, GW])
        G = t5("G", [P, 9, GW])
        gsq = t5("gsq", [P, GW])
        g_land = sem("glu_land")
        pe, act, dve = steps("s5_pe"), steps("s5_act"), steps("s5_dve")
        with nc.Block() as block:
            @block.sync
            def _(sp):
                sp.dma_start(glu_w[:, :, :], A["s5_glu_w"][0].rearrange("(k p) n -> p k n", p=P)).then_inc(g_land, 16)
                sp.dma_start(glu_b[:, :], A["s5_glu_b"][0:1, :].to_broadcast([P, GW])).then_inc(g_land, 16)
                sp.dma_start(w_out[:, :, :], A["w_out"][0].rearrange("(k p) n -> p k n", p=P)).then_inc(land6, 16)
                sp.dma_start(X2[:, 0:NT, :], A["x_prompt"][0].rearrange("(i p) d -> p i d", p=P)).then_inc(land6, 16)
                sp.dma_start(X2[0:DEC, NT, :], A["x_sample"].rearrange("b o d -> (b o) d")).then_inc(land6, 16)
                sp.dma_start(w_r[:, :, :], A["w_router"].rearrange("(k p) e -> p k e", p=P)).then_inc(rland, 16)
                sp.dma_start(b_r[:, :], A["b_router"].unsqueeze(0).to_broadcast([P, EXPERTS])).then_inc(rland, 16)

            @block.tensor
            def _(t):
                for i in range(9):
                    n = P if i < NT else DEC
                    if i >= 2:
                        act.wait(t, f"y1T{i - 2}")
                    for k in range(4):
                        mm = t.transpose(ps[i % 2][:, k * P:k * P + n], Yt[0:n, i, k * P:(k + 1) * P], ident[0:n, 0:n])
                    pe.did(mm, f"y1T{i}")
                t.wait_ge(g_land, 32)
                for i in range(9):
                    n = P if i < NT else DEC
                    act.wait(t, f"y1T{i}")
                    if i >= 2:
                        dve.wait(t, f"G{i - 2}")
                    for k in range(4):
                        mm = t.matmul(ps[2 + i % 2][0:n, :], y1T[:, k, i * P:i * P + n], glu_w[:, k, :], start=(k == 0), stop=(k == 3))
                    pe.did(mm, f"glu{i}")
                for i in range(9):
                    n = P if i < NT else DEC
                    dve.wait(t, f"n{i}")
                    if i >= 2:
                        dve.wait(t, f"oT{i - 2}")
                    for k in range(4):
                        mm = t.transpose(ps[4 + i % 2][:, k * P:k * P + n], Yt[0:n, i, k * P:(k + 1) * P], ident[0:n, 0:n])
                    pe.did(mm, f"oT{i}")

            @block.scalar
            def _(a):
                for i in range(9):
                    n = P if i < NT else DEC
                    pe.wait(a, f"y1T{i}")
                    act.did(a.activation(y1T[:, :, i * P:i * P + n], ps[i % 2][:, :].rearrange("p (k n) -> p k n", k=4)[:, :, 0:n], ACT.Copy), f"y1T{i}")
                for i in range(10):
                    if i < 9:
                        n = P if i < NT else DEC
                        dve.wait(a, f"G{i}")
                        act.did(a.activation(G[0:n, i, :], G[0:n, i, :], ACT.Sigmoid), f"sig{i}")
                    if i >= 1:
                        j = i - 1
                        n = P if j < NT else DEC
                        dve.wait(a, f"y{j}")
                        act.drain(a)
                        act.did(a.activation(gsq[0:n, :], Yt[0:n, j, :], ACT.Square, accum_out=small[0:n, j:j + 1]), "ss")
                dve.wait(a, "ms")
                act.did(a.activation(small[:, 10:19], small[:, 10:19], ACT.Sqrt), "rms")

            @block.vector
            def _(v):
                v.wait_ge(g_land, 32)
                for i in range(10):
                    if i < 9:
                        n = P if i < NT else DEC
                        pe.wait(v, f"glu{i}")
                        dve.did(v.tensor_tensor(G[0:n, i, :], ps[2 + i % 2][0:n, :], glu_b[0:n, :], ALU.add), f"G{i}")
                    if i >= 1:
                        j = i - 1
                        n = P if j < NT else DEC
                        act.wait(v, f"sig{j}")
                        dve.did(v.tensor_tensor(Yt[0:n, j, :], Yt[0:n, j, :], G[0:n, j, :], ALU.mult), f"y{j}")
                act.wait(v, "ss")
                dve.did(v.tensor_scalar(small[:, 10:19], small[:, 0:9], 1.0 / GW, EPS, ALU.mult, ALU.add), "ms")
                act.wait(v, "rms")
                dve.did(v.reciprocal(small[:, 20:29], small[:, 10:19]))
                dve.drain(v)
                for i in range(9):
                    n = P if i < NT else DEC
                    dve.did(v.tensor_scalar(Yt[0:n, i, :], Yt[0:n, i, :], small[0:n, 20 + i:21 + i], None, ALU.mult), f"n{i}")
                for i in range(9):
                    n = P if i < NT else DEC
                    pe.wait(v, f"oT{i}")
                    dst = hT[:, 4:8, i:SEQ:LAGS] if i < NT else hT[:, 4:8, SEQ:T]
                    dve.did(v.tensor_tensor(dst, ps[4 + i % 2][:, :].rearrange("p (k n) -> p k n", k=4)[:, :, 0:n],
                                            bc(vecT[:, SNG:SNG + 4], [P, 4, n]), ALU.mult), f"oT{i}")
        s5s.close()

        s6 = ctx.enter_context(ExitStack())
        t6 = lambda name, shape, dt=F32: s6.enter_context(nc.sbuf_tensor(name, shape, dt))
        H2 = t6("H2", [P, 9, D])
        rowsP = V[:, :, :, :].rearrange("p g k c -> p (g k c)")[:, 0:3 * D].rearrange("p (n d) -> p n d", n=3)
        rowsD = Yt[0:DEC, :, :].rearrange("p i n -> p (i n)")[:, 0:3 * D].rearrange("p (n d) -> p n d", n=3)
        r6 = room(small_room[:, :])
        A2 = r6(P, KD, 9)
        h2T = V[:, :, :, :].rearrange("p g k c -> p (g k c)")[:, 3 * D:4 * D].rearrange("p (k n) -> p k n", k=KD)
        EE = [P, 9, EXPERTS]
        wgu = w_out[:, :, :].rearrange("p k n -> p (k n)").rearrange("p (b k n) -> p b k n", b=2, k=KD)
        wdn = y1T[:, :, :].rearrange("p k n -> p (k n)")[:, 0:4 * D].rearrange("p (b k n) -> p b k n", b=2, k=2)
        wg_v = A["w_gate"][0].rearrange("e (k p) f -> e p k f", p=P)
        wu_v = A["w_up"][0].rearrange("e (k p) f -> e p k f", p=P)
        wd_v = A["w_down"][0].rearrange("e (k p) d -> e p k d", p=P)
        gu_in, dn_in = ([sem(f"{n}_even"), sem(f"{n}_odd")] for n in ("gate_up_land", "down_land"))

        def load_gate_up(sp, e, b):
            for dst, src in ((wgu[:, b, :, 0:FE], wg_v), (wgu[:, b, :, FE:2 * FE], wu_v)):
                sp.dma_start(dst, src[bass.ds(e, 1)].rearrange("o p k f -> (o p) k f")).then_inc(gu_in[b], 16)

        def load_down(sp, e, b):
            sp.dma_start(wdn[:, b], wd_v[bass.ds(e, 1)].rearrange("o p k d -> (o p) k d")).then_inc(dn_in[b], 16)
        lg = r6(*EE)
        sel, m1, oh1, oh2, tmp = (r6(*EE) for _ in range(5))
        g4 = r6(P, 6, 36)
        col = r6(P, 8, 9)
        rank_e = r6(P, 16)
        sidx = r6(P, SLOTS, EXPERTS)
        cmp_ = r6(P, SLOTS, EXPERTS)
        cnt = r6(*EE)
        ex = r6(P, 4, EXPERTS)
        valid = r6(P, 1)
        upx = r6(P, P)
        ones_m = r6(P, P)
        scat = sem("scat")
        pe, act, dve, pool = steps("s6_pe"), steps("s6_act"), steps("s6_dve"), steps("s6_pool")
        GT1, SH2, SC2, GT2 = 16, 24, 32, 40

        with nc.Block() as block:
            @block.sync
            def _(sp):
                pe.wait(sp, "mix8_1")
                for e in range(2):
                    load_gate_up(sp, e, e)
                    load_down(sp, e, e)

            @block.gpsimd
            def _(g):
                pool.did(g.memset(upx[:, :], 1.0))
                pool.did(g.memset(ones_m[:, :], 1.0))
                pool.did(g.memset(lg[:, :, :], 0.0))
                pool.did(g.memset(valid[:, :], 0.0))
                pool.drain(g)
                pool.did(g.memset(valid[0:DEC, :], 1.0))
                for e in range(16):
                    pool.did(g.memset(rank_e[:, e:e + 1], float(16 - e)))
                pool.did(g.iota(sidx[:, :, :], pattern=[[1, SLOTS], [0, EXPERTS]], base=0, channel_multiplier=0,
                                allow_small_or_imprecise_dtypes=True))
                pool.drain(g)
                pool.did(g.affine_select(out=upx[:, :], in_=upx[:, :], compare_op=ALU.is_gt, fill=0.0, base=0,
                                         pattern=[[1, P]], channel_multiplier=-1), "consts")
                dve.wait(g, "pos")
                g.wait_ge(zland, 16 * (SLOTS // 2 + 2))
                for i in range(9):
                    n = P if i < NT else DEC
                    for j in range(2):
                        g.indirect_dma_start(xs_d, bass.IndirectOffsetOnAxis(ap=pos[0:n, i, j:j + 1], axis=0), H2[0:n, i, :], None).then_inc(scat, 16)
                g.wait_ge(scat, 16 * 18)

            def route_T(t, i):
                n = P if i < NT else DEC
                dve.wait(t, f"H2_{i}")
                if i >= 1:
                    act.wait(t, f"h2T{i - 1}")
                for k in range(KD):
                    mm = t.transpose(ps[4 + k // 4][:, (k % 4) * P:(k % 4) * P + n], H2[0:n, i, k * P:(k + 1) * P], ident[0:n, 0:n])
                pe.did(mm, f"h2T{i}")

            def route(t, i):
                n = P if i < NT else DEC
                act.wait(t, f"h2T{i}")
                if i >= 1:
                    dve.wait(t, f"lg{i - 1}")
                for k in range(KD):
                    mm = t.matmul(ps[6][0:n, 0:EXPERTS], h2T[:, k, 0:n], w_r[:, k, :], start=(k == 0), stop=(k == KD - 1))
                pe.did(mm, f"lg{i}")

            @block.tensor
            def _(t):
                dve.wait(t, "A2")
                for n, base in enumerate((GT1, None, SH2)):
                    for half_ in range(2):
                        b = 2 * n + half_
                        for k in range(4 * half_, 4 * half_ + 4):
                            src = A2[:, k, :] if base is None else modT[:, base + k, :]
                            mm = t.matmul(ps[b % 4][:, (k % 4) * P:(k % 4 + 1) * P], src[:, 0:1].to_broadcast([P, P]), ident[:, :], start=True, stop=True)
                        for k in range(4 * half_, 4 * half_ + 4):
                            src = A2[:, k, :] if base is None else modT[:, base + k, :]
                            mm = t.matmul(ps[4 + b % 4][0:DEC, (k % 4) * P:(k % 4 + 1) * P], src[:, 1:9], ident[:, :], start=True, stop=True)
                        pe.did(mm, f"row{b}")
                        if b >= 3:
                            act.wait(t, f"row{b - 3}")
                act.wait(t, "row5")
                t.wait_ge(land6, 48)
                t.wait_ge(rland, 32)
                for i in range(9):
                    n = P if i < NT else DEC
                    for half_ in range(2):
                        b = 2 * (i % 2) + half_
                        if i >= 2:
                            dve.wait(t, f"mix{i - 2}_{half_}")
                        for k in range(KD):
                            mm = t.matmul(ps[b][0:n, :], hT[:, k, i * P:i * P + n], w_out[:, k, half_ * 512:(half_ + 1) * 512], start=(k == 0), stop=(k == KD - 1))
                        pe.did(mm, f"mix{i}_{half_}")
                        if half_ == 0 and i >= 2:
                            route(t, i - 2)
                    if i >= 1:
                        route_T(t, i - 1)
                route(t, 7)
                route_T(t, 8)
                route(t, 8)
                dve.wait(t, "oh")
                t.matmul(ps[4][:, 0:144], upx[:, :], cnt[:, :, :].rearrange("p i e -> p (i e)"), start=True, stop=True)
                pe.did(t.matmul(ps[5][:, 0:144], ones_m[:, :], cnt[:, :, :].rearrange("p i e -> p (i e)"), start=True, stop=True), "cnt")

            @block.scalar
            def _(a):
                for b in range(6):
                    n, half_ = b // 2, b % 2
                    pe.wait(a, f"row{b}")
                    act.did(a.activation(rowsP[:, n, half_ * 512:(half_ + 1) * 512], ps[b % 4][:, :], ACT.Copy))
                    act.did(a.activation(rowsD[:, n, half_ * 512:(half_ + 1) * 512], ps[4 + b % 4][0:DEC, :], ACT.Copy), f"row{b}")
                def route_copy(i):
                    n = P if i < NT else DEC
                    pe.wait(a, f"h2T{i}")
                    if i >= 1:
                        pe.wait(a, f"lg{i - 1}")
                    for half_ in range(2):
                        act.did(a.activation(h2T[:, 4 * half_:4 * half_ + 4, 0:n],
                                             ps[4 + half_][:, :].rearrange("p (k n) -> p k n", k=4)[:, :, 0:n], ACT.Copy), f"h2T{i}")

                for i in range(9):
                    n = P if i < NT else DEC
                    if i >= 2:
                        route_copy(i - 2)
                    dve.wait(a, f"x1_{i}")
                    act.did(a.activation(H2[0:n, i, :], X2[0:n, i, :], ACT.Square, accum_out=small[0:n, i:i + 1]), f"ss{i}")
                    dve.wait(a, f"ms{i}")
                    act.did(a.activation(small[0:n, 10 + i:11 + i], small[0:n, 10 + i:11 + i], ACT.Sqrt), f"rms{i}")
                route_copy(7)
                route_copy(8)
                dve.wait(a, "lg8")
                act.did(a.activation(lg[:, :, :], lg[:, :, :], ACT.Sigmoid), "scores")

            @block.vector
            def _(v):
                def tt(out, x, y, op, name=None):
                    dve.drain(v)
                    dve.did(v.tensor_tensor(out, x, y, op), name)

                dve.did(v.tensor_scalar(A2[:, :, :], modT[:, SC2:SC2 + 8, :], 1.0, None, ALU.add))
                tt(A2[:, :, :], A2[:, :, :], bc(vecT[:, N2G:N2G + 8], [P, 8, 9]), ALU.mult, "A2")
                act.wait(v, "row5")
                v.wait_ge(land6, 48)
                pool.wait(v, "consts")
                def copy_lg(i):
                    n = P if i < NT else DEC
                    pe.wait(v, f"lg{i}")
                    dve.did(v.tensor_copy(lg[0:n, i, :], ps[6][0:n, 0:EXPERTS]), f"lg{i}")

                for i in range(9):
                    n = P if i < NT else DEC
                    row = rowsP if i < NT else rowsD
                    for half_ in range(2):
                        b, c0 = 2 * (i % 2) + half_, half_ * 512
                        if half_ == 1 and i >= 2:
                            copy_lg(i - 2)
                        pe.wait(v, f"mix{i}_{half_}")
                        dve.did(v.tensor_tensor(H2[0:n, i, c0:c0 + 512], ps[b][0:n, :], row[0:n, 0, c0:c0 + 512], ALU.mult), f"mix{i}_{half_}")
                    tt(X2[0:n, i, :], X2[0:n, i, :], H2[0:n, i, :], ALU.add, f"x1_{i}")
                    act.wait(v, f"ss{i}")
                    dve.did(v.tensor_scalar(small[0:n, 10 + i:11 + i], small[0:n, i:i + 1], 1.0 / D, EPS, ALU.mult, ALU.add), f"ms{i}")
                    act.wait(v, f"rms{i}")
                    dve.did(v.reciprocal(small[0:n, 20 + i:21 + i], small[0:n, 10 + i:11 + i]))
                    dve.drain(v)
                    dve.did(v.scalar_tensor_tensor(out=H2[0:n, i, :], in0=X2[0:n, i, :], scalar=small[0:n, 20 + i:21 + i], in1=row[0:n, 1, :],
                                                   op0=ALU.mult, op1=ALU.mult))
                    tt(H2[0:n, i, :], H2[0:n, i, :], row[0:n, 2, :], ALU.add, f"H2_{i}")
                for i in (7, 8):
                    copy_lg(i)
                act.wait(v, "scores")
                b4 = lambda c: c.unsqueeze(2).to_broadcast(EE)
                tt(sel[:, :, :], lg[:, :, :], bc(b_r[:, :], EE, 1), ALU.add)
                q4 = sel[:, :, :].rearrange("p i (g r) -> p (i g) r", r=4)
                for n, (x, y) in enumerate(((0, 1), (0, 2), (0, 3), (1, 2), (1, 3), (2, 3))):
                    tt(g4[:, n, :], q4[:, :, x], q4[:, :, y], ALU.add)
                for n in range(1, 6):
                    tt(g4[:, 0, :], g4[:, 0, :], g4[:, n, :], ALU.max)
                gs_ = g4[:, 0, :].rearrange("p (i g) -> p i g", g=4)
                g4s = [P, 9, 4]
                dve.drain(v)
                dve.did(v.tensor_reduce(col[:, 0, :], gs_, AX.X, ALU.max))
                v1, v2 = (g4[:, n, :].rearrange("p (i g) -> p i g", g=4) for n in (1, 2))
                tt(v1, gs_, bc(col[:, 0, :], g4s), ALU.is_equal)
                tt(v1, v1, bc(rank_e[:, 12:16], g4s, 1), ALU.mult)
                dve.drain(v)
                dve.did(v.tensor_reduce(col[:, 0, :], v1, AX.X, ALU.max))
                tt(v2, v1, bc(col[:, 0, :], g4s), ALU.is_equal)
                ing = v2.rearrange("p i g -> p (i g)").unsqueeze(2).to_broadcast([P, 36, 4])
                t4_ = tmp[:, :, :].rearrange("p i (g r) -> p (i g) r", r=4)
                s4_ = sel[:, :, :].rearrange("p i (g r) -> p (i g) r", r=4)
                tt(s4_, q4, ing, ALU.mult)
                dve.drain(v)
                dve.did(v.tensor_scalar(v1, v2, 1e30, -1e30, ALU.mult, ALU.add))
                tt(s4_, s4_, v1.rearrange("p i g -> p (i g)").unsqueeze(2).to_broadcast([P, 36, 4]), ALU.add)

                def first_max(oh):
                    dve.drain(v)
                    dve.did(v.tensor_reduce(col[:, 1, :], sel[:, :, :], AX.X, ALU.max))
                    tt(m1[:, :, :], sel[:, :, :], b4(col[:, 1, :]), ALU.is_equal)
                    tt(m1[:, :, :], m1[:, :, :], bc(rank_e[:, :], EE, 1), ALU.mult)
                    dve.drain(v)
                    dve.did(v.tensor_reduce(col[:, 1, :], m1[:, :, :], AX.X, ALU.max))
                    tt(oh[:, :, :], m1[:, :, :], b4(col[:, 1, :]), ALU.is_equal)

                first_max(oh1)
                dve.drain(v)
                dve.did(v.scalar_tensor_tensor(out=sel[:, :, :].rearrange("p i e -> p (i e)"), in0=oh1[:, :, :].rearrange("p i e -> p (i e)"), scalar=-2e30,
                                               in1=sel[:, :, :].rearrange("p i e -> p (i e)"), op0=ALU.mult, op1=ALU.add))
                first_max(oh2)
                tt(cnt[:, :, :], oh1[:, :, :], oh2[:, :, :], ALU.add)
                dve.drain(v)
                dve.did(v.tensor_scalar(cnt[:, NT, :], cnt[:, NT, :], valid[:, :], None, ALU.mult), "oh")
                pe.wait(v, "cnt")
                tot = m1
                dve.did(v.tensor_copy(tot[:, :, :].rearrange("p i e -> p (i e)"), ps[5][:, 0:144]))
                dve.did(v.tensor_copy(sel[:, :, :].rearrange("p i e -> p (i e)"), ps[4][:, 0:144]))
                dve.drain(v)
                dve.did(v.tensor_copy(ex[:, 0, :], tot[:, 0, :]))
                for i in range(1, 9):
                    tt(sel[:, i, :], sel[:, i, :], ex[:, 0, :], ALU.add)
                    tt(ex[:, 0, :], ex[:, 0, :], tot[:, i, :], ALU.add)
                dve.drain(v)
                dve.did(v.tensor_scalar(ex[:, 0, :], ex[:, 0, :], 1.0 / P, 127.0 / P - 127.0 / 256, ALU.mult, ALU.add))
                dve.drain(v)
                dve.did(v.tensor_scalar(ex[:, 0, :], ex[:, 0, :], ROUND, -ROUND, ALU.add, ALU.add))
                dve.drain(v)
                dve.did(v.tensor_scalar(ex[:, 0, :], ex[:, 0, :], 1.0, None, ALU.max))
                dve.did(v.memset(ex[:, 3, :], 1.0))
                dve.drain(v)
                dve.did(v.tensor_tensor_scan(ex[:, 1, :], ex[:, 3, :], ex[:, 0, :], 0.0, ALU.mult, ALU.add))
                tt(ex[:, 2, :], ex[:, 1, :], ex[:, 0, :], ALU.subtract)
                dve.drain(v)
                dve.did(v.tensor_copy(exp_t[:, 0:EXPERTS], ex[0:1, 2, :]))
                dve.drain(v)
                dve.did(v.tensor_scalar(ex[:, 2, :], ex[:, 2, :], float(P), None, ALU.mult))
                tt(sel[:, :, :], sel[:, :, :], bc(ex[:, 2, :], EE, 1), ALU.add)
                for n, oh in enumerate((oh1, oh2)):
                    tt(tmp[:, :, :], oh[:, :, :], sel[:, :, :], ALU.mult)
                    dve.drain(v)
                    dve.did(v.tensor_reduce(col[:, 5 + n, :], tmp[:, :, :], AX.X, ALU.add))
                dve.drain(v)
                dve.did(v.tensor_copy(pos[:, :, :], col[:, 5:7, :].rearrange("p n i -> p i n")), "pos")
                for n, oh in enumerate((oh1, oh2)):
                    tt(tmp[:, :, :], oh[:, :, :], lg[:, :, :], ALU.mult)
                    dve.drain(v)
                    dve.did(v.tensor_reduce(col[:, 2 + n, :], tmp[:, :, :], AX.X, ALU.add))
                tt(col[:, 4, :], col[:, 2, :], col[:, 3, :], ALU.add)
                dve.drain(v)
                dve.did(v.reciprocal(col[:, 4, :], col[:, 4, :]))
                for n in range(2):
                    tt(combine[:, :, n], col[:, 2 + n, :], col[:, 4, :], ALU.mult)
                tt(cmp_[:, :, :], bc(ex[:, 1, :], [P, SLOTS, EXPERTS], 1), sidx[:, :, :], ALU.is_le)
                dve.drain(v)
                dve.did(v.tensor_reduce(sidx[:, :, 0], cmp_[:, :, :], AX.X, ALU.add))
                dve.drain(v)
                dve.did(v.tensor_scalar(sidx[:, :, 0], sidx[:, :, 0], float(EXPERTS - 1), None, ALU.min))
                dve.drain(v)
                e_, half_e, par = (x[0:1, :, 0:1] for x in (sidx, cmp_, sidx[:, :, 1:2]))

                def ts(out, x, c1, c2):
                    dve.drain(v)
                    dve.did(v.tensor_scalar(out, x, c1, c2, ALU.mult, ALU.add))
                ts(half_e, e_, 0.5, -0.25)
                dve.drain(v)
                dve.did(v.tensor_scalar(half_e, half_e, ROUND, -ROUND, ALU.add, ALU.add))
                dve.drain(v)
                dve.did(v.scalar_tensor_tensor(out=par, in0=half_e, scalar=-2.0, in1=e_, op0=ALU.mult, op1=ALU.add))
                tt(e_, half_e, par, ALU.add)
                dve.drain(v)
                dve.did(v.tensor_copy(slot_t[:, :, 0:1], par))
                ts(slot_t[:, :, 1:2], half_e, 16.0, 16.0)
                dve.drain(v)
                dve.did(v.tensor_scalar(e_, e_, 1.0, 16.0, ALU.max, ALU.mult))
                dve.drain(v)
                dve.did(v.tensor_copy(slot_t[:, :, 2:3], e_))
                ts(ex[0:1, 3, 0:1], ex[0:1, 1, EXPERTS - 1:EXPERTS], 0.5, 0.25)
                dve.drain(v)
                dve.did(v.tensor_scalar(ex[0:1, 3, 0:1], ex[0:1, 3, 0:1], ROUND, -ROUND, ALU.add, ALU.add))
                dve.drain(v)
                dve.did(v.tensor_copy(exp_t[:, EXPERTS:EXPERTS + 1], ex[0:1, 3, 0:1]))
                ts(exp_t[:, EXPERTS + 1:EXPERTS + 2], ex[0:1, 3, 0:1], 1.0, -1.0)
                ts(exp_t[:, EXPERTS + 2:EXPERTS + 3], ex[0:1, 3, 0:1], 2.0, -1.0)
                dve.at["slots"] = dve.n
        s6.close()

        s7 = ctx.enter_context(ExitStack())
        t7 = lambda name, shape: s7.enter_context(nc.sbuf_tensor(name, shape, F32))
        xin = [t7(f"xin{p}", [P, D]) for p in range(2)]
        xT = [t7(f"xT{p}", [P, KD, P]) for p in range(2)]
        sg = [t7(f"sg{p}", [P, FE]) for p in range(2)]
        hh_ = [t7(f"hh{p}", [P, FE]) for p in range(2)]
        aT = [t7(f"aT{p}", [P, 2, P]) for p in range(2)]
        yo = [t7(f"yo{p}", [P, D]) for p in range(2)]
        x_in, y_out = ([sem(f"{n}{p}") for p in range(2)] for n in ("x_in", "y_out"))
        y_half, xT_half = sem("y_half"), sem("xT_half")
        xT_ps, xT_sb, gu_ps, silu_sb, h_sb, aT_ps, aT_sb, dn_ps, y_sb = (sem(n) for n in (
            "xT_ps", "xT_sb", "gu_ps", "silu_sb", "h_sb", "aT_ps", "aT_sb", "dn_ps", "y_sb"))
        xs_v = ys_v = xs_d.rearrange("(s p) d -> s p d", p=P)
        PAIRS = SLOTS // 2

        def pairs(eng, body, tail=None):
            used = eng.value_load(exp_t[0:1, EXPERTS:EXPERTS + 1], min_val=EXPERTS // 2, max_val=PAIRS)
            body(0)
            with eng.Fori(1, PAIRS) as it:
                with eng.If(it < used):
                    body(it)
            if tail is not None:
                tail(*(eng.value_load(exp_t[0:1, EXPERTS + n:EXPERTS + n + 1], min_val=n * EXPERTS // 2 - 1, max_val=n * PAIRS - 1) for n in (1, 2)))

        with nc.Block() as block:
            @block.sync
            def _(sp):
                with sp.Fori(1, EXPERTS // 2) as it:
                    for b in range(2):
                        done = sp.value_load(exp_t[0:1, bass.ds(it * 2 + (b - 1), 1)], min_val=1, max_val=SLOTS)
                        sp.wait_ge(gu_ps, done)
                        load_gate_up(sp, it * 2 + b, b)
                        sp.wait_ge(dn_ps, done)
                        load_down(sp, it * 2 + b, b)

            @block.gpsimd
            def _(g):
                def load(s, p):
                    g.dma_start(xin[p][:, :], xs_v[bass.ds(s, 1)].rearrange("o p d -> p (o d)")).then_inc(x_in[p], 16)

                def body(it):
                    if isinstance(it, int):
                        load(1, 1)
                    else:
                        g.wait_ge(xT_ps, it * 2)
                        load(it * 2 + 1, 1)
                    g.wait_ge(xT_ps, it * 2 + 1)
                    load(it * 2 + 2, 0)
                load(0, 0)
                pairs(g, body)

            @block.tensor
            def _(t):
                def buffer(s):
                    return (t.value_load(slot_t[0:1, bass.ds(s, 1), 0], min_val=0, max_val=1),
                            *(t.value_load(slot_t[0:1, bass.ds(s, 1), n], min_val=0, max_val=16 * EXPERTS // 2) for n in (1, 2)))

                def transposes(it, p, s):
                    t.wait_ge(x_in[p], (it + 1) * 16)
                    if not (isinstance(s, int) and s == 0):
                        t.wait_ge(xT_sb, s)
                    for k in range(KD):
                        mm = t.transpose(ps[k // 4][:, (k % 4) * P:(k % 4 + 1) * P], xin[p][:, k * P:(k + 1) * P], ident[:, :])
                    mm.then_inc(xT_ps, 1)

                def act_transposes(p, s):
                    t.wait_ge(h_sb, s + 1)
                    for k in range(2):
                        mm = t.transpose(ps[4][:, k * P:(k + 1) * P], hh_[p][:, k * P:(k + 1) * P], ident[:, :])
                    mm.then_inc(aT_ps, 1)

                def down(p, s):
                    buf, even, odd = buffer(s)
                    t.wait_ge(aT_sb, s + 1)
                    t.wait_ge(dn_in[0], even)
                    t.wait_ge(dn_in[1], odd)
                    if not (isinstance(s, int) and s == 0):
                        t.wait_ge(y_sb, s)
                    for half_ in range(2):
                        for k in range(2):
                            mm = t.matmul(ps[5 + half_][:, :], aT[p][:, k, :],
                                          wdn[:, bass.ds(buf, 1), k, half_ * 512:(half_ + 1) * 512].rearrange("p o n -> p (o n)"),
                                          start=(k == 0), stop=(k == 1))
                    mm.then_inc(dn_ps, 1)

                def body(it):
                    for p in range(2):
                        s = it * 2 + p
                        static = isinstance(it, int)
                        buf, even, odd = buffer(s)
                        t.wait_ge(xT_sb, s + 1)
                        t.wait_ge(gu_in[0], even * 2)
                        t.wait_ge(gu_in[1], odd * 2)
                        if not (static and s < 2):
                            t.wait_ge(h_sb, s - 1)
                        for k in range(KD):
                            mm = t.matmul(ps[2 + p][:, :], xT[p][:, k, :], wgu[:, bass.ds(buf, 1), k, :].rearrange("p o n -> p (o n)"),
                                          start=(k == 0), stop=(k == KD - 1))
                        mm.then_inc(gu_ps, 1)
                        if not (static and s == 0):
                            act_transposes(1 - p, s - 1)
                        transposes(it + p, 1 - p, s + 1)
                        if not (static and s == 0):
                            down(1 - p, s - 1)

                def tail(it, s):
                    act_transposes(1, s)
                    down(1, s)
                transposes(0, 0, 0)
                pairs(t, body, tail)

            @block.scalar
            def _(a):
                def out(it, p, s):
                    a.wait_ge(dn_ps, s + 1)
                    if not (isinstance(it, int) and it == 0):
                        a.wait_ge(y_out[p], it * 16)
                    a.activation(yo[p][:, 0:512], ps[5][:, :], ACT.Copy).then_inc(y_half, 1)
                    a.activation(yo[p][:, 512:D], ps[6][:, :], ACT.Copy).then_inc(y_sb, 1)
                    a.wait_ge(y_half, s + 1)
                    a.wait_ge(y_sb, s + 1)
                    a.dma_start(ys_v[bass.ds(s, 1)].rearrange("o p d -> (o p) d"), yo[p][:, :]).then_inc(y_out[p], 16)

                def body(it):
                    for p in range(2):
                        s = it * 2 + p
                        static = isinstance(it, int)
                        a.wait_ge(gu_ps, s + 1)
                        if not (static and s < 2):
                            a.wait_ge(h_sb, s - 1)
                        a.activation(sg[p][:, :], ps[2 + p][:, 0:FE], ACT.Silu).then_inc(silu_sb, 1)
                        if not (static and s == 0):
                            out(it - 1 + p, 1 - p, s - 1)

                def tail(it, s):
                    out(it, 1, s)
                    for p in range(2):
                        a.wait_ge(y_out[p], it * 16 + 16)
                        a.activation(sg[p][:, 0:1], sg[p][:, 0:1], ACT.Copy).then_inc(silu_sb, 1)
                pairs(a, body, tail)

            @block.vector
            def _(v):
                def x_copy(p, s):
                    v.wait_ge(xT_ps, s + 1)
                    if not (isinstance(s, int) and s < 2):
                        v.wait_ge(gu_ps, s - 1)
                    v.tensor_copy(xT[p][:, 0:4, :].rearrange("p k n -> p (k n)"), ps[0][:, :]).then_inc(xT_half, 1)
                    v.wait_ge(xT_half, s + 1)
                    v.tensor_copy(xT[p][:, 4:8, :].rearrange("p k n -> p (k n)"), ps[1][:, :]).then_inc(xT_sb, 1)

                def body(it):
                    for p in range(2):
                        s = it * 2 + p
                        static = isinstance(it, int)
                        v.wait_ge(silu_sb, s + 1)
                        if not (static and s < 2):
                            v.wait_ge(aT_ps, s - 1)
                        v.tensor_tensor(hh_[p][:, :], sg[p][:, :], ps[2 + p][:, FE:2 * FE], ALU.mult).then_inc(h_sb, 1)
                        if not (static and s == 0):
                            a_copy(1 - p, s - 1, None if static and s < 3 else s - 2)
                        x_copy(1 - p, s + 1)

                def a_copy(p, s, down_done):
                    v.wait_ge(aT_ps, s + 1)
                    if down_done is not None:
                        v.wait_ge(dn_ps, down_done)
                    v.tensor_copy(aT[p][:, :, :].rearrange("p k n -> p (k n)"), ps[4][:, 0:FE]).then_inc(aT_sb, 1)

                x_copy(0, 0)
                pairs(v, body, lambda it, s: a_copy(1, s, it * 2))
        s7.close()

        s8 = ctx.enter_context(ExitStack())
        t8 = lambda name, shape: s8.enter_context(nc.sbuf_tensor(name, shape, F32))
        gt2P, gt2D, fg = t8("gt2P", [P, D]), Yt[0:DEC, 0:2, :].rearrange("p i n -> p (i n)"), t8("fg", [P, D])
        ya = t8("ya", [P, 3, 2, D])
        sq8 = hT[:, :, :].rearrange("p k t -> p (k t)")[:, 0:2 * D].rearrange("p (b d) -> p b d", b=2)
        sqj = hT[:, :, :].rearrange("p k t -> p (k t)")[:, 2 * D:3 * D]
        yn = V[:, :, :, :].rearrange("p g k c -> p (g k c)")[:, 0:2 * D].rearrange("p (b d) -> p b d", b=2)
        fland, ygot, y_fin = sem("fland"), [sem(f"ygot{n}") for n in range(3)], [sem(f"y_fin{n}") for n in range(2)]
        pe, act, dve = steps("s8_pe"), steps("s8_act"), steps("s8_dve")
        with nc.Block() as block:
            @block.sync
            def _(sp):
                sp.dma_start(fg[:, :], A["final_g"].unsqueeze(0).to_broadcast([P, D])).then_inc(fland, 16)
                for i in range(9):
                    dve.wait(sp, f"yn{i}")
                    if i < NT:
                        sp.dma_start(O["y_p"][0, i * P:(i + 1) * P, :], yn[:, i % 2, :]).then_inc(y_fin[i % 2], 16)
                    else:
                        sp.dma_start(O["y_s"][:, 0, :], yn[0:DEC, i % 2, :]).then_inc(y_fin[i % 2], 16)
                sp.wait_ge(y_fin[0], 16 * 5)
                sp.wait_ge(y_fin[1], 16 * 4)

            @block.gpsimd
            def _(g):
                for i in range(9):
                    n = P if i < NT else DEC
                    if i >= 3:
                        dve.wait(g, f"c{i - 3}")
                        act.wait(g, f"c0_{i - 3}")
                    for j in range(2):
                        g.indirect_dma_start(ya[0:n, i % 3, j, :], None, ys_d, bass.IndirectOffsetOnAxis(ap=pos[0:n, i, j:j + 1], axis=0)).then_inc(ygot[i % 3], 16)

            @block.tensor
            def _(t):
                for half_ in range(2):
                    for k in range(4):
                        mm = t.matmul(ps[half_][:, k * P:(k + 1) * P], modT[:, GT2 + 4 * half_ + k, 0:1].to_broadcast([P, P]), ident[:, :], start=True, stop=True)
                        mm = t.matmul(ps[2 + half_][0:DEC, k * P:(k + 1) * P], modT[:, GT2 + 4 * half_ + k, 1:9], ident[:, :], start=True, stop=True)
                pe.did(mm, "gt2")

            @block.scalar
            def _(a):
                pe.wait(a, "gt2")
                for half_ in range(2):
                    c = slice(half_ * 512, (half_ + 1) * 512)
                    act.did(a.activation(gt2P[:, c], ps[half_][:, :], ACT.Copy))
                    act.did(a.activation(gt2D[:, c], ps[2 + half_][0:DEC, :], ACT.Copy), "gt2")
                def scaled(i):
                    n = P if i < NT else DEC
                    a.wait_ge(ygot[i % 3], 32 * (i // 3 + 1))
                    if i >= 2:
                        dve.wait(a, f"x{i - 2}")
                    act.did(a.activation(sq8[0:n, i % 2, :], ya[0:n, i % 3, 0, :], ACT.Copy, scale=combine[0:n, i, 0:1]), f"c0_{i}")
                scaled(0)
                scaled(1)
                for i in range(11):
                    if i < 9:
                        n = P if i < NT else DEC
                        dve.wait(a, f"x{i}")
                        act.drain(a)
                        act.did(a.activation(sqj[0:n, :], X2[0:n, i, :], ACT.Square, accum_out=small[0:n, i:i + 1]), f"ss{i}")
                        if i + 2 < 9:
                            scaled(i + 2)
                    if 1 <= i < 10:
                        n = P if i - 1 < NT else DEC
                        dve.wait(a, f"ms{i - 1}")
                        act.did(a.activation(small[0:n, 9 + i:10 + i], small[0:n, 9 + i:10 + i], ACT.Sqrt), f"rms{i - 1}")
                    if i >= 2:
                        j = i - 2
                        n = P if j < NT else DEC
                        dve.wait(a, f"inv{j}")
                        if j >= 2:
                            a.wait_ge(y_fin[j % 2], 16 * (j // 2))
                        act.did(a.activation(yn[0:n, j % 2, :], X2[0:n, j, :], ACT.Copy, scale=small[0:n, 20 + j:21 + j]), f"xn{j}")

            @block.vector
            def _(v):
                act.wait(v, "gt2")
                v.wait_ge(fland, 16)
                for i in range(12):
                    if i < 9:
                        n = P if i < NT else DEC
                        gt = gt2P if i < NT else gt2D
                        v.wait_ge(ygot[i % 3], 32 * (i // 3 + 1))
                        mix = sq8[0:n, i % 2, :]
                        act.wait(v, f"c0_{i}")
                        dve.did(v.scalar_tensor_tensor(out=mix, in0=ya[0:n, i % 3, 1, :], scalar=combine[0:n, i, 1:2], in1=mix, op0=ALU.mult, op1=ALU.add), f"c{i}")
                        dve.drain(v)
                        dve.did(v.tensor_tensor(mix, mix, gt[0:n, :], ALU.mult))
                        dve.drain(v)
                        dve.did(v.tensor_tensor(X2[0:n, i, :], X2[0:n, i, :], mix, ALU.add), f"x{i}")
                    if 1 <= i < 10:
                        m = P if i - 1 < NT else DEC
                        act.wait(v, f"ss{i - 1}")
                        dve.did(v.tensor_scalar(small[0:m, 9 + i:10 + i], small[0:m, i - 1:i], 1.0 / D, EPS, ALU.mult, ALU.add), f"ms{i - 1}")
                    if 2 <= i < 11:
                        m = P if i - 2 < NT else DEC
                        act.wait(v, f"rms{i - 2}")
                        dve.did(v.reciprocal(small[0:m, 18 + i:19 + i], small[0:m, 8 + i:9 + i]), f"inv{i - 2}")
                    if i >= 3:
                        j = i - 3
                        m = P if j < NT else DEC
                        act.wait(v, f"xn{j}")
                        dve.did(v.tensor_tensor(yn[0:m, j % 2, :], yn[0:m, j % 2, :], fg[0:m, :], ALU.mult), f"yn{j}")


_INS = ["x_prompt", "x_sample", "c_prompt", "c_sample", "state_conv", "state_gdn", "state_s5_re", "state_s5_im",
        "norm1_g", "norm2_g", "w_ada", "b_ada", "w_in", "conv_w", "a_log", "dt_bias", "gdn_norm_g",
        "s5_lambda_re", "s5_lambda_im", "s5_log_dt", "s5_b_re", "s5_b_im", "s5_c_re", "s5_c_im", "s5_d",
        "s5_glu_w", "s5_glu_b", "s5_norm_g", "w_out", "w_router", "b_router", "w_gate", "w_up", "w_down", "final_g"]
_OUTS = [("y_p", (1, SEQ, D)), ("y_s", (DEC, 1, D)), ("conv_p", (1, 1, CW - 1, QKV)), ("gdn_p", (1, 1, HEADS, P, P)),
         ("re_p", (1, 1, GROUPS, ST)), ("im_p", (1, 1, GROUPS, ST)), ("conv_s", (1, DEC, CW - 1, QKV)),
         ("gdn_s", (1, DEC, HEADS, P, P)), ("re_s", (1, DEC, GROUPS, ST)), ("im_s", (1, DEC, GROUPS, ST))]


def program(new_core, shapes):
    marks = {}
    for _ in range(2):
        nc = new_core()
        A = {n: nc.dram_tensor("in_" + n, shape, F32, kind="ExternalInput").ap() for n, shape in shapes}
        O = {n: nc.dram_tensor("out_" + n, shape, F32, kind="ExternalOutput").ap() for n, shape in _OUTS}
        emit(nc, A, O, marks)
    return nc


def kernel(**inputs):
    import numpy as np
    import concourse.bacc as bacc
    from concourse.bass_utils import run_bass_kernel_spmd

    arrays = {"in_" + n: np.ascontiguousarray(inputs[n]) for n in _INS}
    nc = program(lambda: bacc.Bacc("TRN2", target_bir_lowering=False, num_devices=1),
                 [(n, arrays["in_" + n].shape) for n in _INS])
    r = run_bass_kernel_spmd(nc, [arrays], core_ids=[0])
    return tuple(r.results[0]["out_" + n] for n, _ in _OUTS)
```
